# Optimizing a Trainium2 kernel written in Bass

```python
import jax, jax.numpy as jnp
from jax import lax
import numpy as np

D_MODEL = 2048
BATCH = 1
SEQ = 256
DEPTH = 2

D_MIX = D_MODEL
EPS = 1e-6
SWA_HEAD_DIM = 64
SWA_HEADS = D_MIX // 2 // SWA_HEAD_DIM
SWA_KV_HEADS = 4
SWA_GROUP = SWA_HEADS // SWA_KV_HEADS
SWA_WIDTH = SWA_HEADS * SWA_HEAD_DIM
SWA_KV_WIDTH = SWA_KV_HEADS * SWA_HEAD_DIM
WINDOW = 128
ROT_DIM = SWA_HEAD_DIM // 4
ROPE_THETA = 500000.0
SG_WIDTH = D_MIX // 4
SG_GROUPS = 8
SG_GROUP_DIM = SG_WIDTH // SG_GROUPS
SG_CHUNK = 128
GLA_HEADS = 4
GLA_WIDTH = D_MIX // 4
GLA_DV = GLA_WIDTH // GLA_HEADS
GLA_DK = GLA_DV // 2
GLA_KEY_WIDTH = GLA_HEADS * GLA_DK
GLA_GATE_RANK = 16
GLA_GATE_TAU = 16.0
GLA_CHUNK = 64
IN_SIZES = (SWA_WIDTH, SWA_KV_WIDTH, SWA_KV_WIDTH,
            SG_WIDTH, SG_WIDTH,
            GLA_KEY_WIDTH, GLA_KEY_WIDTH, GLA_WIDTH,
            GLA_GATE_RANK,
            D_MIX)
IN_PROJ_WIDTH = SWA_WIDTH + 2 * SWA_KV_WIDTH + 2 * SG_WIDTH + 2 * GLA_KEY_WIDTH + GLA_WIDTH + GLA_GATE_RANK + D_MIX


def rms_norm(x, g):
    x32 = x.astype(jnp.float32)
    y = x32 * lax.rsqrt(jnp.mean(x32 * x32, axis=-1, keepdims=True) + EPS)
    return (y * g.astype(jnp.float32)).astype(x.dtype)

def partial_rope(t, positions):
    half = ROT_DIM // 2
    inv_freq = ROPE_THETA ** (-(jnp.arange(half, dtype=jnp.float32) * (2.0 / ROT_DIM)))
    ang = positions.astype(jnp.float32)[..., None] * inv_freq
    cos = jnp.cos(ang)[:, :, None, :]
    sin = jnp.sin(ang)[:, :, None, :]
    tr = t[..., :ROT_DIM].astype(jnp.float32)
    t1, t2 = tr[..., :half], tr[..., half:]
    rot = jnp.concatenate([t1 * cos - t2 * sin, t2 * cos + t1 * sin], axis=-1)
    return jnp.concatenate([rot.astype(t.dtype), t[..., ROT_DIM:]], axis=-1)

def sliding_window_attention(q, k, v, sinks):
    bsz, seq = q.shape[0], q.shape[1]
    nb = seq // WINDOW
    qb = q.reshape(bsz, nb, WINDOW, SWA_KV_HEADS, SWA_GROUP, SWA_HEAD_DIM).astype(jnp.float32)

    def band(t):
        tb = t.reshape(bsz, nb, WINDOW, SWA_KV_HEADS, SWA_HEAD_DIM)
        prev = jnp.pad(tb[:, :-1], ((0, 0), (1, 0), (0, 0), (0, 0), (0, 0)))
        return jnp.concatenate([prev, tb], axis=2).astype(jnp.float32)

    kb, vb = band(k), band(v)
    scores = jnp.einsum('bnqgrd,bnkgd->bngrqk', qb, kb) * (SWA_HEAD_DIM ** -0.5)
    qi = jnp.arange(WINDOW)[:, None]
    kj = jnp.arange(2 * WINDOW)[None, :]
    dist = qi + WINDOW - kj
    blk = jnp.arange(nb)[:, None, None]
    valid = (dist >= 0) & (dist < WINDOW) & (blk * WINDOW + kj[None] - WINDOW >= 0)
    scores = jnp.where(valid[None, :, None, None], scores, -jnp.inf)
    sink = sinks.astype(jnp.float32).reshape(1, 1, SWA_KV_HEADS, SWA_GROUP, 1, 1)
    m = jnp.maximum(scores.max(axis=-1, keepdims=True), sink)
    p = jnp.exp(scores - m)
    probs = p / (p.sum(axis=-1, keepdims=True) + jnp.exp(sink - m))
    out = jnp.einsum('bngrqk,bnkgd->bnqgrd', probs, vb)
    return out.reshape(bsz, seq, SWA_WIDTH).astype(q.dtype)

def chunked_spatial_gating(u, v, w_s, b_s, ln_g, ln_b):
    bsz, seq = v.shape[0], v.shape[1]
    nc = seq // SG_CHUNK
    v32 = v.astype(jnp.float32)
    mu = jnp.mean(v32, axis=-1, keepdims=True)
    var = jnp.mean(jnp.square(v32 - mu), axis=-1, keepdims=True)
    vn = (v32 - mu) * lax.rsqrt(var + EPS) * ln_g.astype(jnp.float32) + ln_b.astype(jnp.float32)
    vn = vn.reshape(bsz, nc, SG_CHUNK, SG_GROUPS, SG_GROUP_DIM)
    causal = jnp.tril(jnp.ones((SG_CHUNK, SG_CHUNK), dtype=bool))
    w = jnp.where(causal[None], w_s.astype(jnp.float32), 0.0)
    mixed = jnp.einsum('gts,bnsgc->bntgc', w, vn) + b_s.astype(jnp.float32).T[None, None, :, :, None]
    return (u.astype(jnp.float32) * mixed.reshape(bsz, seq, SG_WIDTH)).astype(u.dtype)

def gated_linear_attention(q, k, v, log_alpha):
    bsz, seq = q.shape[0], q.shape[1]
    nc = seq // GLA_CHUNK

    def to_chunks(t):
        return t.astype(jnp.float32).reshape(bsz, nc, GLA_CHUNK, GLA_HEADS, t.shape[-1]).transpose(1, 0, 3, 2, 4)

    causal = jnp.tril(jnp.ones((GLA_CHUNK, GLA_CHUNK), dtype=bool))

    def step(state, xs):
        qc, kc, vc, lac = xs
        b = jnp.cumsum(lac, axis=2)
        diff = b[:, :, :, None, :] - b[:, :, None, :, :]
        decay = jnp.exp(jnp.where(causal[:, :, None], diff, -jnp.inf))
        scores = jnp.einsum('bhtd,bhsd,bhtsd->bhts', qc, kc, decay)
        o = jnp.einsum('bhts,bhsv->bhtv', scores, vc) + jnp.einsum('bhtd,bhdv->bhtv', qc * jnp.exp(b), state)
        b_last = b[:, :, -1:, :]
        state = state * jnp.exp(b_last)[:, :, 0, :, None] + jnp.einsum('bhsd,bhsv->bhdv', kc * jnp.exp(b_last - b), vc)
        return state, o

    state0 = jnp.zeros((bsz, GLA_HEADS, GLA_DK, GLA_DV), dtype=jnp.float32)
    qs = to_chunks(q) * (GLA_DK ** -0.5)
    _, o = lax.scan(step, state0, (qs, to_chunks(k), to_chunks(v), to_chunks(log_alpha)))
    return o.transpose(1, 0, 3, 2, 4).reshape(bsz, seq, GLA_HEADS, GLA_DV)

def hybrid_layer(x, c, positions, w_mod, b_mod, g_pre, g_post, w_in, w_out, swa_sinks,
                 sg_w, sg_b, sg_ln_g, sg_ln_b, gla_w_gate_up, gla_b_gate, gla_norm_g):
    bsz, seq = x.shape[0], x.shape[1]
    mod = jax.nn.silu(c) @ w_mod + b_mod
    shift, scale, gate = jnp.split(mod, 3, axis=-1)
    h = rms_norm(x, g_pre) * (1.0 + scale[:, None, :]) + shift[:, None, :]
    proj = h @ w_in
    offsets = np.cumsum(IN_SIZES)[:-1].tolist()
    a_q, a_k, a_v, s_u, s_v, c_q, c_k, c_v, c_g, z = jnp.split(proj, offsets, axis=-1)
    a_q = partial_rope(a_q.reshape(bsz, seq, SWA_HEADS, SWA_HEAD_DIM), positions)
    a_k = partial_rope(a_k.reshape(bsz, seq, SWA_KV_HEADS, SWA_HEAD_DIM), positions)
    a_v = a_v.reshape(bsz, seq, SWA_KV_HEADS, SWA_HEAD_DIM)
    y_a = sliding_window_attention(a_q, a_k, a_v, swa_sinks)
    y_b = chunked_spatial_gating(jax.nn.gelu(s_u), jax.nn.gelu(s_v), sg_w, sg_b, sg_ln_g, sg_ln_b)
    gate_logits = (c_g @ gla_w_gate_up + gla_b_gate).astype(jnp.float32)
    log_alpha = jax.nn.log_sigmoid(gate_logits) / GLA_GATE_TAU
    o_c = gated_linear_attention(c_q.reshape(bsz, seq, GLA_HEADS, GLA_DK),
                                 c_k.reshape(bsz, seq, GLA_HEADS, GLA_DK),
                                 c_v.reshape(bsz, seq, GLA_HEADS, GLA_DV),
                                 log_alpha.reshape(bsz, seq, GLA_HEADS, GLA_DK))
    y_c = rms_norm(o_c, gla_norm_g).reshape(bsz, seq, GLA_WIDTH).astype(x.dtype)
    y = jnp.concatenate([y_a, y_b, y_c], axis=-1) * jax.nn.silu(z)
    out = y @ w_out
    return x + gate[:, None, :] * rms_norm(out, g_post)

def first_inputs(seed: int = 0) -> dict:
    key = jax.random.key(seed)
    ks = jax.random.split(key, 17)
    nrm = jax.random.normal
    f32 = jnp.float32
    x = nrm(ks[0], (BATCH, SEQ, D_MODEL), f32)
    c = nrm(ks[1], (BATCH, D_MODEL), f32)
    positions = jax.random.randint(ks[2], (BATCH, 1), 0, 4096, dtype=jnp.int32) + jnp.arange(SEQ, dtype=jnp.int32)[None, :]
    w_mod = nrm(ks[3], (DEPTH, D_MODEL, 3 * D_MODEL), f32) * (0.5 * D_MODEL ** -0.5)
    b_mod = 0.01 * nrm(ks[4], (DEPTH, 3 * D_MODEL), f32)
    g_pre = 1.0 + 0.05 * nrm(ks[5], (DEPTH, D_MODEL), f32)
    g_post = 1.0 + 0.05 * nrm(ks[6], (DEPTH, D_MODEL), f32)
    w_in = nrm(ks[7], (DEPTH, D_MODEL, IN_PROJ_WIDTH), f32) * (D_MODEL ** -0.5)
    w_out = nrm(ks[8], (DEPTH, D_MIX, D_MODEL), f32) * (D_MIX ** -0.5)
    swa_sinks = 0.5 * nrm(ks[9], (DEPTH, SWA_HEADS), f32)
    sg_w = nrm(ks[10], (DEPTH, SG_GROUPS, SG_CHUNK, SG_CHUNK), f32) * (SG_CHUNK ** -0.5)
    sg_b = 1.0 + 0.1 * nrm(ks[11], (DEPTH, SG_GROUPS, SG_CHUNK), f32)
    sg_ln_g = 1.0 + 0.05 * nrm(ks[12], (DEPTH, SG_WIDTH), f32)
    sg_ln_b = 0.02 * nrm(ks[13], (DEPTH, SG_WIDTH), f32)
    gla_w_gate_up = nrm(ks[14], (DEPTH, GLA_GATE_RANK, GLA_KEY_WIDTH), f32) * (GLA_GATE_RANK ** -0.5)
    gla_b_gate = 0.1 * nrm(ks[15], (DEPTH, GLA_KEY_WIDTH), f32)
    gla_norm_g = 1.0 + 0.05 * nrm(ks[16], (DEPTH, GLA_DV), f32)
    return {'x': x, 'c': c, 'positions': positions, 'w_mod': w_mod, 'b_mod': b_mod,
            'g_pre': g_pre, 'g_post': g_post, 'w_in': w_in, 'w_out': w_out, 'swa_sinks': swa_sinks,
            'sg_w': sg_w, 'sg_b': sg_b, 'sg_ln_g': sg_ln_g, 'sg_ln_b': sg_ln_b,
            'gla_w_gate_up': gla_w_gate_up, 'gla_b_gate': gla_b_gate, 'gla_norm_g': gla_norm_g}

def first_block(x, c, positions, w_mod, b_mod, g_pre, g_post, w_in, w_out, swa_sinks,
              sg_w, sg_b, sg_ln_g, sg_ln_b, gla_w_gate_up, gla_b_gate, gla_norm_g):
    for l in range(DEPTH):
        x = hybrid_layer(x, c, positions, w_mod[l], b_mod[l], g_pre[l], g_post[l], w_in[l], w_out[l],
                         swa_sinks[l], sg_w[l], sg_b[l], sg_ln_g[l], sg_ln_b[l],
                         gla_w_gate_up[l], gla_b_gate[l], gla_norm_g[l])
    return x


HEAD_DIM = 128
N_HEADS_A = 12
N_HEADS_B = 12
WIDTH_A = N_HEADS_A * HEAD_DIM
WIDTH_B = N_HEADS_B * HEAD_DIM
DILATED_PATTERNS = ((128, 1), (512, 4), (2048, 16))
Q_BLOCK = 128
ROPE_THETA_2 = 10000.0
LN_EPS = 1e-5
DEEPNORM_ALPHA = float((2 * DEPTH) ** 0.25)
DEEPNORM_BETA = float((8 * DEPTH) ** -0.25)
FORGET_BIAS_INIT = 2.0

SPLIT_SIZES = (WIDTH_A, WIDTH_A, WIDTH_A, WIDTH_A,
               WIDTH_B, WIDTH_B, WIDTH_B, WIDTH_B,
               N_HEADS_B,
               2 * D_MODEL)
SPLIT_POINTS = tuple(int(v) for v in np.cumsum(SPLIT_SIZES)[:-1])
N_IN_COLS = int(sum(SPLIT_SIZES))


def rope(t, pos):
    half = HEAD_DIM // 2
    inv_freq = ROPE_THETA_2 ** (-jnp.arange(half, dtype=jnp.float32) / half)
    ang = pos.astype(jnp.float32)[:, None] * inv_freq[None, :]
    cos = jnp.cos(ang)[None, :, None, :]
    sin = jnp.sin(ang)[None, :, None, :]
    t32 = t.astype(jnp.float32)
    t1, t2 = t32[..., :half], t32[..., half:]
    return jnp.concatenate([t1 * cos - t2 * sin, t1 * sin + t2 * cos], axis=-1).astype(t.dtype)

def dilated_pattern(q, k, v, window, dilation):
    B, S, H, hd = q.shape
    span = window // dilation
    L = S // dilation
    nblk = -(-L // Q_BLOCK)
    Lp = nblk * Q_BLOCK

    def to_residue(t):
        t = t.reshape(B, L, dilation, H, hd).transpose(0, 2, 1, 3, 4)
        return jnp.pad(t, ((0, 0), (0, 0), (0, Lp - L), (0, 0), (0, 0)))

    def band_keys(t):
        tp = jnp.pad(t, ((0, 0), (0, 0), (Q_BLOCK, 0), (0, 0), (0, 0)))
        tp = tp.reshape(B, dilation, nblk + 1, Q_BLOCK, H, hd)
        return jnp.concatenate([tp[:, :, :-1], tp[:, :, 1:]], axis=3)

    qb = to_residue(q).reshape(B, dilation, nblk, Q_BLOCK, H, hd)
    kb = band_keys(to_residue(k))
    vb = band_keys(to_residue(v))

    n_idx = jnp.arange(nblk)[:, None, None]
    i_idx = jnp.arange(Q_BLOCK)[None, :, None]
    j_idx = jnp.arange(2 * Q_BLOCK)[None, None, :]
    dist = Q_BLOCK + i_idx - j_idx
    valid = (dist >= 0) & (dist <= span) & (n_idx * Q_BLOCK + j_idx - Q_BLOCK >= 0)
    valid = valid[None, None, :, None]

    scale = HEAD_DIM ** -0.5
    s = jnp.einsum('bdnihe,bdnjhe->bdnhij', qb, kb, preferred_element_type=jnp.float32) * scale
    s = jnp.where(valid, s, -jnp.inf)
    m = jnp.max(s, axis=-1, keepdims=True)
    p = jnp.exp(s - m)
    den = jnp.sum(p, axis=-1, keepdims=True)
    out = jnp.einsum('bdnhij,bdnjhe->bdnihe', p, vb.astype(jnp.float32))
    out = out / jnp.moveaxis(den, 3, 4)
    lse = jnp.moveaxis((m + jnp.log(den))[..., 0], 3, 4)

    out = out.reshape(B, dilation, Lp, H, hd)[:, :, :L].transpose(0, 2, 1, 3, 4).reshape(B, S, H, hd)
    lse = lse.reshape(B, dilation, Lp, H)[:, :, :L].transpose(0, 2, 1, 3).reshape(B, S, H)
    return out, lse

def dilated_mixture(q, k, v):
    outs, lses = [], []
    for window, dilation in DILATED_PATTERNS:
        o, l = dilated_pattern(q, k, v, window, dilation)
        outs.append(o)
        lses.append(l)
    w = jax.nn.softmax(jnp.stack(lses, axis=0), axis=0)
    return jnp.sum(w[..., None] * jnp.stack(outs, axis=0), axis=0).astype(q.dtype)

def forgetting_attention(q, k, v, log_f):
    B, S, H, hd = q.shape
    nblk = S // Q_BLOCK
    cum = jnp.cumsum(log_f, axis=1).transpose(0, 2, 1)
    q_blocks = q.reshape(B, nblk, Q_BLOCK, H, hd).transpose(1, 0, 2, 3, 4)
    c_blocks = cum.reshape(B, H, nblk, Q_BLOCK).transpose(2, 0, 1, 3)
    kpos = jnp.arange(S)
    scale = HEAD_DIM ** -0.5

    def block(args):
        n, qn, cn = args
        s = jnp.einsum('bihe,bjhe->bhij', qn, k, preferred_element_type=jnp.float32) * scale
        s = s + cn[..., :, None] - cum[..., None, :]
        qpos = n * Q_BLOCK + jnp.arange(Q_BLOCK)
        causal = kpos[None, :] <= qpos[:, None]
        s = jnp.where(causal[None, None], s, -jnp.inf)
        p = jax.nn.softmax(s, axis=-1)
        return jnp.einsum('bhij,bjhe->bihe', p, v.astype(jnp.float32)).astype(q.dtype)

    out = lax.map(block, (jnp.arange(nblk), q_blocks, c_blocks))
    return out.transpose(1, 0, 2, 3, 4).reshape(B, S, H, hd)

def layer_norm(x, g, b):
    x32 = x.astype(jnp.float32)
    mu = jnp.mean(x32, axis=-1, keepdims=True)
    var = jnp.mean(jnp.square(x32 - mu), axis=-1, keepdims=True)
    y = (x32 - mu) * lax.rsqrt(var + LN_EPS)
    return (y * g.astype(jnp.float32) + b.astype(jnp.float32)).astype(x.dtype)

def hybrid_layer_2(x, pos, w_in, b_forget, b_gate, w_up_a, w_up_b, w_out, ln_g, ln_b):
    B, S, _ = x.shape
    h = jnp.einsum('bsd,dc->bsc', x, w_in)
    qa, ka, va, za, qb, kb, vb, zb, f_logit, g_logit = jnp.split(h, SPLIT_POINTS, axis=-1)
    heads = lambda t, n: t.reshape(B, S, n, HEAD_DIM)

    qa = rope(heads(qa, N_HEADS_A), pos)
    ka = rope(heads(ka, N_HEADS_A), pos)
    out_a = dilated_mixture(qa, ka, heads(va, N_HEADS_A)).reshape(B, S, WIDTH_A)
    up_a = jnp.einsum('bsw,wd->bsd', out_a * jax.nn.silu(za), w_up_a)

    log_f = jax.nn.log_sigmoid((f_logit + b_forget).astype(jnp.float32))
    out_b = forgetting_attention(heads(qb, N_HEADS_B), heads(kb, N_HEADS_B),
                                 heads(vb, N_HEADS_B), log_f).reshape(B, S, WIDTH_B)
    up_b = jnp.einsum('bsw,wd->bsd', out_b * jax.nn.silu(zb), w_up_b)

    gates = jax.nn.sigmoid(g_logit + b_gate)
    g_a, g_b = gates[..., :D_MODEL], gates[..., D_MODEL:]
    y = jnp.einsum('bsd,de->bse', g_a * up_a + g_b * up_b, w_out)

    return layer_norm(DEEPNORM_ALPHA * x + y, ln_g, ln_b)

def second_inputs(seed: int = 0) -> dict:
    key = jax.random.key(seed)
    ks = jax.random.split(key, 10)
    x = jax.random.normal(ks[0], (BATCH, SEQ, D_MODEL), jnp.float32)

    offs = (0,) + SPLIT_POINTS
    col_scale = jnp.ones((N_IN_COLS,), jnp.float32)
    col_scale = col_scale.at[offs[2]:offs[3]].set(DEEPNORM_BETA)
    col_scale = col_scale.at[offs[6]:offs[7]].set(DEEPNORM_BETA)
    w_in = jax.random.normal(ks[1], (DEPTH, D_MODEL, N_IN_COLS), jnp.float32) * (D_MODEL ** -0.5) * col_scale
    b_forget = FORGET_BIAS_INIT + 0.1 * jax.random.normal(ks[2], (DEPTH, N_HEADS_B), jnp.float32)
    b_gate = 0.02 * jax.random.normal(ks[3], (DEPTH, 2 * D_MODEL), jnp.float32)
    w_up_a = jax.random.normal(ks[4], (DEPTH, WIDTH_A, D_MODEL), jnp.float32) * (WIDTH_A ** -0.5) * DEEPNORM_BETA
    w_up_b = jax.random.normal(ks[5], (DEPTH, WIDTH_B, D_MODEL), jnp.float32) * (WIDTH_B ** -0.5) * DEEPNORM_BETA
    w_out = jax.random.normal(ks[6], (DEPTH, D_MODEL, D_MODEL), jnp.float32) * (D_MODEL ** -0.5) * DEEPNORM_BETA
    ln_g = 1.0 + 0.02 * jax.random.normal(ks[7], (DEPTH, D_MODEL), jnp.float32)
    ln_b = 0.02 * jax.random.normal(ks[8], (DEPTH, D_MODEL), jnp.float32)
    return {"x": x, "w_in": w_in, "b_forget": b_forget, "b_gate": b_gate,
            "w_up_a": w_up_a, "w_up_b": w_up_b, "w_out": w_out,
            "ln_g": ln_g, "ln_b": ln_b}

def second_block(x, w_in, b_forget, b_gate, w_up_a, w_up_b, w_out, ln_g, ln_b):
    pos = jnp.arange(x.shape[1], dtype=jnp.int32)
    for l in range(DEPTH):
        x = hybrid_layer_2(x, pos, w_in[l], b_forget[l], b_gate[l],
                         w_up_a[l], w_up_b[l], w_out[l], ln_g[l], ln_b[l])
    return x


def setup_inputs(seed=0):
    out = dict(first_inputs(seed))
    for name, value in second_inputs(seed + 1).items():
        if name != "x":
            out[name + "_2"] = value
    return out


def reference(
    x, c, positions, w_mod, b_mod, g_pre, g_post, w_in, w_out, swa_sinks, sg_w, sg_b, sg_ln_g,
    sg_ln_b, gla_w_gate_up, gla_b_gate, gla_norm_g, w_in_2, b_forget_2, b_gate_2, w_up_a_2,
    w_up_b_2, w_out_2, ln_g_2, ln_b_2,
):
    x = first_block(
        x, c, positions, w_mod, b_mod, g_pre, g_post, w_in, w_out, swa_sinks, sg_w, sg_b,
        sg_ln_g, sg_ln_b, gla_w_gate_up, gla_b_gate, gla_norm_g,
    )
    return second_block(
        x, w_in_2, b_forget_2, b_gate_2, w_up_a_2, w_up_b_2, w_out_2, ln_g_2, ln_b_2,
    )


_drawn_inputs = setup_inputs


def setup_inputs(seed=0):
    import zlib

    import numpy as np

    out = dict(_drawn_inputs(seed))
    spreads = {}
    factors = {'b_mod': 3.039,
     'g_post': 2.669,
     'swa_sinks': 8.0,
     'sg_b': 2.745,
     'sg_ln_g': 7.812,
     'sg_ln_b': 32.957,
     'gla_b_gate': 3.918,
     'gla_norm_g': 3.744,
     'b_forget_2': 64.0,
     'b_gate_2': 59.376,
     'w_up_a_2': 5.097,
     'w_up_b_2': 2.948}
    for name, (base, spread) in spreads.items():
        noise = np.random.default_rng([zlib.crc32(name.encode()), seed]).standard_normal(out[name].shape)
        drawn = base * np.exp(spread * noise) if base else spread * noise
        out[name] = __import__('jax').numpy.asarray(drawn.astype(out[name].dtype))
    for name, factor in factors.items():
        out[name] = (out[name] * factor).astype(out[name].dtype)
    return out
```

```python
from contextlib import ExitStack

import numpy as np

import concourse.bass as bass
from concourse import mybir

F32 = mybir.dt.float32
F32R = mybir.dt.float32r
U32 = mybir.dt.uint32
I32 = mybir.dt.int32
ACT = mybir.ActivationFunctionType
ALU = mybir.AluOpType
AX = mybir.AxisListType

P = 128
SEQ = 256
TB = SEQ // P
D = 2048
KT = D // P
CW = 512
NCW = D // CW
GK = 2
SLOTS = 4
NEG = -1.0e30
DEPTH = 2

HD = 128
NH2 = 12
W2 = NH2 * HD
HPG = CW // HD
NGRP = 2 * NH2 // HPG
KT_UP = W2 // P
ALPHA = float((2 * DEPTH) ** 0.25)
SCALE2 = float(HD) ** -0.5
LN_EPS = 1e-5


def at(layer, per_layer, count):
    return layer * per_layer + count


def second_plan():
    chunks = []
    for half in range(2):
        for grp in range(3):
            chunks += [(kind, 3 * half + grp) for kind in "qkvz"]
        chunks += [("g", NCW * half + j) for j in range(NCW)]
        chunks += [("u", NCW * half + j) for j in range(NCW)]
    chunks += [("o", j) for j in range(NCW)]
    first, n = [], 0
    for kind, _ in chunks:
        first.append(n)
        n += (KT_UP if kind == "u" else KT) // GK
    return chunks, first, n


CHUNKS2, FIRST2, GRAN2 = second_plan()


def granules2(c):
    return (FIRST2 + [GRAN2])[c + 1] - FIRST2[c]


def group_step(c, g):
    found = []
    for q in range(len(CHUNKS2)):
        if CHUNKS2[q][0] == "q" and q <= c:
            r = FIRST2[c] + g - FIRST2[q]
            if r < 48:
                found.append((CHUNKS2[q][1], r))
    return found


F_CHUNK = [i for i, k in enumerate(CHUNKS2) if k == ("g", 1)][0]


def fills2(c, g):
    out = []
    if c == 0:
        out += [("x", 0), ("x", 1)] if g == 0 else [("x", g + 1)] if g < KT // 2 - 1 else []
    for grp, r in group_step(c, g):
        out += {12: [("q", grp, 0), ("q", grp, 1)], 20: [("k", grp, 0), ("k", grp, 1)], 28: [("p", grp, 0)],
                29: [("p", grp, 1)], 30: [("p", grp, 2)], 38: [("a", grp, 0)], 39: [("a", grp, 1)]}.get(r, [])
    if (c, g) == (F_CHUNK, 4):
        out += [("f", 0), ("f", 1)]
    if c and CHUNKS2[c - 1][0] == "u" and CHUNKS2[c - 1][1] >= NCW and g == 3:
        j = CHUNKS2[c - 1][1] - NCW
        out += [("y", 2 * j), ("y", 2 * j + 1)]
    return out


def units2(c, g):
    out = []
    for grp, r in group_step(c, g):
        out += {23: [("s", grp, 0)], 24: [("s", grp, 1)], 25: [("s", grp, 2)],
                33: [("o", grp, 0)], 34: [("o", grp, 1)]}.get(r, [])
    if (c, g) == (F_CHUNK, 0):
        out += [("f", 0), ("f", 1)]
    return out


def numbered(what):
    names = [n for c in range(len(CHUNKS2)) for g in range(granules2(c)) for n in what(c, g)]
    return {name: i for i, name in enumerate(names)}


FILL2 = numbered(fills2)
UNIT2 = numbered(units2)
NF2, NU2 = len(FILL2), len(UNIT2)
assert NF2 % 2 == 0 and NU2 % 2 == 0
SPLIT2 = {name: i for i, name in enumerate([n for n in FILL2 if n[0] in "xay"])}
VLINKS2 = 52


def second_block(nc, ctx, x, rings, ps, dram):
    raw, whi, wlo = rings
    acc, psT, psS = ps

    def sb(name, shape, dt=F32):
        return ctx.enter_context(nc.sbuf_tensor(name, shape, dt))

    def sem(name):
        return ctx.enter_context(nc.semaphore(name))

    xhi = sb("xhi", [P, KT, SEQ], F32R)
    xlo = sb("xlo", [P, KT, SEQ], F32R)
    ahi = sb("ahi", [P, KT_UP, SEQ], F32R)
    alo = sb("alo", [P, KT_UP, SEQ], F32R)
    y = sb("y", [P, TB, D])
    gb = sb("gb", [P, TB, D])
    stage = sb("stage", [P, TB, CW])
    qT = sb("qT", [P, HPG, SEQ])
    kT = sb("kT", [P, HPG, SEQ])
    v = sb("v", [P, TB, CW])
    z = sb("z", [P, TB, CW])
    prob = sb("prob", [P, 3, CW])
    probT = sb("probT", [P, 3, CW])
    rtmp = sb("rtmp", [P, CW])
    ident = sb("ident", [P, P])
    mask_a = sb("mask_a", [P, P + SEQ])
    mask_b = sb("mask_b", [P, P + SEQ])
    tables = sb("tables", [P, 2, 3, TB, HD // 2])
    gate_row = sb("gate_row", [P, 2, CW])
    wf = sb("wf", [P, KT, NH2])
    wfhi = sb("wfhi", [P, KT, NH2], F32R)
    wflo = sb("wflo", [P, KT, NH2], F32R)
    bf = sb("bf", [P, NH2])
    fb = sb("fb", [P, TB, NH2])
    fl = sb("fl", [NH2, SEQ])
    fe = sb("fe", [NH2, SEQ])
    ncum = sb("ncum", [NH2, SEQ])
    ones = sb("ones", [P, SEQ])
    mx = sb("mx", [P, 3, HPG])
    den = sb("den", [P, TB, HPG])
    rden = sb("rden", [P, TB, HPG])
    stats = sb("stats", [P, TB, NCW, 6])
    mv = sb("mv", [P, TB, 2])
    std = sb("std", [P, TB])
    rstd = sb("rstd", [P, TB])
    eps = sb("eps", [P, 1])

    s_w = [sem(f"c_w{i}") for i in range(SLOTS)]
    s_hi = sem("c_hi")
    s_lo = sem("c_lo")
    s_used = sem("c_used")
    s_acc = [sem(f"c_acc{i}") for i in range(2)]
    s_tfull = sem("c_tfull")
    s_thi = sem("c_thi")
    s_tfree = [sem(f"c_tfree{i}") for i in range(2)]
    s_sfull = sem("c_sfull")
    s_sfree = [sem(f"c_sfree{i}") for i in range(2)]
    s_const = sem("c_const")
    s_mem = sem("c_mem")
    s_rope = sem("c_rope")
    s_max = sem("c_max")
    s_exp = sem("c_exp")
    s_att = sem("c_att")
    s_gate = sem("c_gate")
    s_grow = [sem(f"c_grow{i}") for i in range(2)]
    s_fw = sem("c_fw")
    s_fwh = sem("c_fwh")
    s_fln = sem("c_fln")
    s_cum = sem("c_cum")
    s_y = sem("c_y")
    s_lnp = sem("c_lnp")
    s_var = sem("c_var")
    s_std = sem("c_std")
    s_xn = sem("c_xn")
    s_self = sem("c_self")
    s_out = sem("c_out")

    block = ctx.enter_context(nc.Block())
    nch = len(CHUNKS2)

    def group_chunk(grp):
        return CHUNKS2.index(("q", grp))

    def dst_of(name):
        if name[0] == "a":
            return ahi, alo, HPG * (name[1] % 3) + 2 * name[2]
        return xhi, xlo, 2 * name[1]

    def multiplied(l, c):
        return s_used, at(l, GRAN2, SLOTS + FIRST2[c] + granules2(c))

    def acc_read(l, c):
        return s_acc[c % 2], at(l, nch // 2, c // 2 + 2)

    def unit_read(l, name):
        return s_sfree[UNIT2[name] % 2], at(l, NU2 // 2, UNIT2[name] // 2 + 2)

    def unit_full(l, name):
        return s_sfull, at(l, NU2, UNIT2[name] + 1)

    def copied(l, name):
        return s_tfree[FILL2[name] % 2], at(l, NF2 // 2, FILL2[name] // 2 + 2)

    def filled(l, name):
        return s_tfull, at(l, NF2, FILL2[name] + 1)

    def bank_t(name):
        return psT[FILL2[name] % 2]

    @block.sync
    def _(sp):
        for n in range(SLOTS):
            sp.dma_start(raw[:, n, :], dram["w"][n]).then_inc(s_w[n], 16)
        with sp.Fori(1, DEPTH * GRAN2 // SLOTS) as i:
            for b in range(SLOTS):
                src = dram["w"][sp.snap(i * SLOTS + b)]
                sp.wait_ge(s_lo, i * SLOTS + b - SLOTS + 1)
                sp.dma_start(raw[:, b, :], src).then_inc(s_w[b], 16)
        for j in range(NCW):
            sp.wait_ge(s_xn, DEPTH * NCW + j + 1)
            sp.dma_start(dram["out"][:, j * CW:(j + 1) * CW].rearrange("(b p) n -> p b n", p=P),
                         x[:, :, j * CW:(j + 1) * CW]).then_inc(s_out, 16)
        sp.wait_ge(s_out, 16 * NCW)

    @block.gpsimd
    def _(pool):
        for tile, name in ((ident, "ident"), (mask_a, "mask_a"), (mask_b, "mask_b"), (tables, "tables")):
            pool.dma_start(tile[:], dram[name]).then_inc(s_const, 16)
        with pool.Fori(0, DEPTH) as l:
            pool.dma_start(wf[:], dram["wf"][pool.snap(l)]).then_inc(s_fw, 16)
            pool.dma_start(bf[:], dram["bf"][pool.snap(l)].partition_broadcast(P)).then_inc(s_fw, 16)
            for j in range(2 * NCW):
                bias = dram["bg"][pool.snap(l * 2 * NCW + j)].partition_broadcast(P)
                if j >= 2:
                    pool.wait_ge(*acc_read(l, CHUNKS2.index(("g", j - 2))))
                pool.dma_start(gate_row[:, j % 2, :], bias).then_inc(s_grow[j % 2], 16)
            pool.wait_ge(s_y, at(l, NCW, NCW))
            pool.dma_start(gb[:, 0, :], dram["ln_g"][pool.snap(l)].partition_broadcast(P)).then_inc(s_lnp, 16)
            pool.dma_start(gb[:, 1, :], dram["ln_b"][pool.snap(l)].partition_broadcast(P)).then_inc(s_lnp, 16)

    @block.scalar
    def _(act):
        act.wait_ge(s_mem, 2)

        with act.Fori(0, DEPTH) as l:

            def hi(n):
                act.wait_ge(s_w[n % SLOTS], at(l, 16 * GRAN2 // SLOTS, 16 * (n // SLOTS + 1)))
                act.wait_ge(s_used, at(l, GRAN2, n + 1))
                act.activation(whi[:, n % SLOTS, :], raw[:, n % SLOTS, :], ACT.Copy).then_inc(s_hi, 1)

            def fill_hi(name):
                h, _, k = dst_of(name)
                act.wait_ge(*filled(l, name))
                act.activation(h[:, k:k + 2, :], bank_t(name)[:].rearrange("p (k t) -> p k t", k=2),
                               ACT.Copy).then_inc(s_thi, 1)

            def fill_copy(name, dst):
                act.wait_ge(*filled(l, name))
                act.activation(dst, bank_t(name)[:], ACT.Copy).then_inc(s_tfree[FILL2[name] % 2], 1)

            def evacuate(c, dst, func, scale=1.0):
                act.wait_ge(*multiplied(l, c))
                act.activation(dst[:], acc[c % 2][:], func, scale=scale).then_inc(s_acc[c % 2], 1)

            def attention(grp, r):
                c0 = group_chunk(grp)
                if grp >= 3 and r == 12:
                    evacuate(c0, stage, ACT.Copy, SCALE2)
                if grp >= 3 and r == 20:
                    act.wait_ge(*filled(l, ("q", grp, 1)))
                    evacuate(c0 + 1, stage, ACT.Copy)
                if r in (15, 16):
                    i = r - 15
                    fill_copy(("q", grp, i), qT[:, 2 * i:2 * i + 2, :].rearrange("p h t -> p (h t)"))
                if r in (23, 24):
                    i = r - 23
                    fill_copy(("k", grp, i), kT[:, 2 * i:2 * i + 2, :].rearrange("p h t -> p (h t)"))
                if r in (28, 29, 30):
                    u = r - 28
                    act.wait_ge(s_max, at(l, 3 * NGRP, 3 * grp + u + 1))
                    w = P if u == 0 else SEQ
                    for i in range(CW // w):
                        h = i + max(0, 2 * (u - 1))
                        p = act.activation(prob[:, u, i * w:(i + 1) * w], prob[:, u, i * w:(i + 1) * w], ACT.Exp,
                                           bias=mx[:, u, i:i + 1], accum_out=den[:, min(u, 1), h:h + 1])
                    p.then_inc(s_exp, 1)
                if r == 31:
                    evacuate(c0 + 2, v, ACT.Copy)
                if r in (32, 33, 34):
                    fill_copy(("p", grp, r - 32), probT[:, r - 32, :])
                if r == 36:
                    evacuate(c0 + 3, z, ACT.Silu)
                if r in (42, 43):
                    fill_hi(("a", grp, r - 42))

            act.wait_ge(s_fw, at(l, 32, 32))
            act.activation(wfhi[:], wf[:], ACT.Copy).then_inc(s_fwh, 1)
            for c in range(nch):
                prev, j = CHUNKS2[c - 1] if c else (None, None)
                for g in range(granules2(c)):
                    if c == 0:
                        fill_hi(("x", g))
                    hi(FIRST2[c] + g)
                    for grp, r in group_step(c, g):
                        attention(grp, r)
                    if prev == "g" and g == 4:
                        act.wait_ge(*acc_read(l, c - 1))
                        t = (y if j < NCW else gb)[:, :, (j % NCW) * CW:(j % NCW + 1) * CW]
                        act.activation(t, t, ACT.Sigmoid).then_inc(s_gate, 1)
                    if prev == "u" and j >= NCW and g == 5:
                        fill_hi(("y", 2 * (j - NCW)))
                        fill_hi(("y", 2 * (j - NCW) + 1))
                    if (c, g) == (F_CHUNK, 7):
                        for tb in range(TB):
                            act.wait_ge(*copied(l, ("f", tb)))
                        act.activation(fe[:], fe[:], ACT.Exp).then_inc(s_fln, 1)
                        act.wait_ge(s_fln, at(l, 2, 1))
                        act.activation(fe[:], fe[:], ACT.Ln, bias=1.0).then_inc(s_fln, 1)
            act.wait_ge(s_var, l + 1)
            act.activation(std[:], mv[:, :, 1], ACT.Sqrt, bias=eps[:, 0:1]).then_inc(s_std, 1)

    @block.vector
    def _(dve):
        dve.memset(ones[:], 1.0).then_inc(s_mem, 1)
        dve.memset(eps[:], LN_EPS).then_inc(s_mem, 1)
        for i, (s, credit) in enumerate(((s_used, SLOTS), (s_acc[0], 1), (s_acc[1], 1), (s_tfree[0], 1), (s_tfree[1], 1),
                          (s_sfree[0], 1), (s_sfree[1], 1), (s_xn, NCW))):
            dve.memset(rtmp[:, i:i + 1], 0.0).then_inc(s, credit)
        dve.wait_ge(s_const, 64)
        dve.wait_ge(s_mem, 2)
        links = [0]

        with dve.Fori(0, DEPTH) as l:

            def link(ins):
                links[0] += 1
                ins.then_inc(s_self, 1)
                dve.wait_ge(s_self, at(l, VLINKS2, links[0]))

            def lo(n):
                dve.wait_ge(s_hi, at(l, GRAN2, n + 1))
                dve.tensor_tensor(wlo[:, n % SLOTS, :], raw[:, n % SLOTS, :], whi[:, n % SLOTS, :].bitcast(F32),
                                  ALU.subtract).then_inc(s_lo, 1)

            def fill_lo(name):
                h, w, k = dst_of(name)
                dve.wait_ge(s_thi, at(l, len(SPLIT2), SPLIT2[name] + 1))
                dve.tensor_tensor(w[:, k:k + 2, :], bank_t(name)[:].rearrange("p (k t) -> p k t", k=2),
                                  h[:, k:k + 2, :].bitcast(F32), ALU.subtract)\
                    .then_inc(s_tfree[FILL2[name] % 2], 1)

            def rope(c, which, tb):
                if tb == 0:
                    dve.wait_ge(*multiplied(l, c))
                    if which:
                        dve.wait_ge(*filled(l, ("q", CHUNKS2[c][1], 1)))
                half = HD // 2
                src = acc[c % 2][:, tb, :].rearrange("p (h s e) -> p h s e", s=2, e=half)
                tmp = rtmp[:].rearrange("p (h s e) -> p h s e", s=2, e=half)
                cos, sin, nsin = (tables[:, which, i, tb, :].unsqueeze(1) for i in range(3))
                dve.tensor_tensor(stage[:, tb, :].rearrange("p (h e) -> p h e", e=half),
                                  acc[c % 2][:, tb, :].rearrange("p (h e) -> p h e", e=half),
                                  cos.broadcast_to([P, 2 * HPG, half]), ALU.mult)
                dve.tensor_tensor(tmp[:, :, 0, :], src[:, :, 1, :], nsin.broadcast_to([P, HPG, half]), ALU.mult)
                last = dve.tensor_tensor(tmp[:, :, 1, :], src[:, :, 0, :], sin.broadcast_to([P, HPG, half]),
                                         ALU.mult)
                if tb == 0:
                    link(last)
                else:
                    last.then_inc(s_acc[c % 2], 1)
                    dve.wait_ge(*acc_read(l, c))
                last = dve.tensor_tensor(stage[:, tb, :], stage[:, tb, :], rtmp[:], ALU.add)
                if tb == 0:
                    link(last)
                else:
                    last.then_inc(s_rope, 1)

            def attention(grp, r):
                c0 = group_chunk(grp)
                if grp < 3 and r in (12, 13):
                    rope(c0, 0, r - 12)
                if grp < 3 and r in (20, 21):
                    rope(c0 + 1, 1, r - 20)
                if r in (27, 28, 29):
                    u = r - 27
                    name = ("s", grp, u)
                    bank = UNIT2[name] % 2
                    m = mask_a if grp < 3 else mask_b
                    n, w, m = (HPG, P, m[:, 0:P]) if u == 0 else (2, SEQ, m[:, P:P + SEQ])
                    dve.wait_ge(*unit_full(l, name))
                    p = prob[:, u, :].rearrange("p (h s) -> p h s", s=w)
                    dve.tensor_tensor(p, psS[bank][:].rearrange("p (h s) -> p h s", s=w),
                                      m.unsqueeze(1).broadcast_to([P, n, w]), ALU.add).then_inc(s_sfree[bank], 1)
                    dve.wait_ge(*unit_read(l, name))
                    link(dve.tensor_reduce(mx[:, u, 0:n], p, AX.X, ALU.max))
                    dve.tensor_scalar(mx[:, u, 0:n], mx[:, u, 0:n], -1.0, None, ALU.mult).then_inc(s_max, 1)
                if r == 36:
                    dve.wait_ge(s_exp, at(l, 3 * NGRP, 3 * grp + 3))
                    link(dve.reciprocal(rden[:], den[:]))
                if r in (37, 38):
                    tb = r - 37
                    name = ("o", grp, tb)
                    bank = UNIT2[name] % 2
                    dve.wait_ge(*unit_full(l, name))
                    if tb == 0:
                        dve.wait_ge(*acc_read(l, c0 + 3))
                    else:
                        dve.wait_ge(s_att, at(l, TB * NGRP, TB * grp + 1))
                    t = rtmp[:].rearrange("p (h e) -> p h e", e=HD)
                    dve.tensor_tensor(t, psS[bank][:].rearrange("p (h e) -> p h e", e=HD),
                                      rden[:, tb, :].unsqueeze(2).broadcast_to([P, HPG, HD]), ALU.mult)\
                        .then_inc(s_sfree[bank], 1)
                    dve.wait_ge(*unit_read(l, name))
                    dve.tensor_tensor(z[:, tb, :], z[:, tb, :], rtmp[:], ALU.mult).then_inc(s_att, 1)

            def gate_logits(c):
                j = CHUNKS2[c][1]
                dve.wait_ge(*multiplied(l, c))
                dve.wait_ge(s_grow[j % 2], at(l, 16 * NCW, 16 * (j // 2 + 1)))
                t = (y if j < NCW else gb)[:, :, (j % NCW) * CW:(j % NCW + 1) * CW]
                dve.tensor_tensor(t, acc[c % 2][:], gate_row[:, j % 2, :].unsqueeze(1).broadcast_to([P, TB, CW]),
                                  ALU.add).then_inc(s_acc[c % 2], 1)

            def gated(c):
                j = CHUNKS2[c][1]
                cols = slice((j % NCW) * CW, (j % NCW + 1) * CW)
                dve.wait_ge(*multiplied(l, c))
                dve.wait_ge(s_gate, at(l, 2 * NCW, j + 1))
                t = (y if j < NCW else gb)[:, :, cols]
                dve.tensor_tensor(t, t, acc[c % 2][:], ALU.mult).then_inc(s_acc[c % 2], 1)
                if j >= NCW:
                    dve.wait_ge(*acc_read(l, c))
                    dve.tensor_tensor(y[:, :, cols], y[:, :, cols], t, ALU.add).then_inc(s_y, 1)

            def residual(c):
                j = CHUNKS2[c][1]
                cols = slice(j * CW, (j + 1) * CW)
                dve.wait_ge(*multiplied(l, c))
                dve.scalar_tensor_tensor(out=x[:, :, cols], in0=x[:, :, cols], scalar=ALPHA, in1=acc[c % 2][:],
                                         op0=ALU.mult, op1=ALU.add).then_inc(s_acc[c % 2], 1)
                dve.wait_ge(*acc_read(l, c))
                for tb in range(TB):
                    last = dve.bn_stats(stats[:, tb, j, :], x[:, tb, cols])
                link(last)

            dve.wait_ge(s_fwh, at(l, 2, 1))
            dve.tensor_tensor(wflo[:], wf[:], wfhi[:].bitcast(F32), ALU.subtract).then_inc(s_fwh, 1)
            for c in range(nch):
                prev, j = CHUNKS2[c - 1] if c else (None, None)
                for g in range(granules2(c)):
                    if c == 0:
                        fill_lo(("x", g))
                    lo(FIRST2[c] + g)
                    for grp, r in group_step(c, g):
                        attention(grp, r)
                        if r in (42, 43):
                            fill_lo(("a", grp, r - 42))
                    if prev == "g" and g == 3:
                        gate_logits(c - 1)
                    if prev == "u" and g == 3:
                        gated(c - 1)
                    if prev == "o" and g == 3:
                        residual(c - 1)
                    if prev == "u" and j >= NCW and g == 5:
                        fill_lo(("y", 2 * (j - NCW)))
                        fill_lo(("y", 2 * (j - NCW) + 1))
                    if (c, g) == (F_CHUNK, 4):
                        for tb in range(TB):
                            bank = UNIT2["f", tb] % 2
                            dve.wait_ge(*unit_full(l, ("f", tb)))
                            dve.tensor_tensor(fb[:, tb, :], psS[bank][:, 0:NH2], bf[:], ALU.add)\
                                .then_inc(s_sfree[bank], 1)
                    if (c, g) == (F_CHUNK, 6):
                        for tb in range(TB):
                            tok = slice(tb * P, (tb + 1) * P)
                            bank = FILL2["f", tb] % 2
                            dve.wait_ge(*filled(l, ("f", tb)))
                            link(dve.tensor_scalar(fe[:, tok], psT[bank][0:NH2, 0:P], -1.0, None, ALU.mult))
                            dve.tensor_tensor(fe[:, tok], psT[bank][0:NH2, 0:P], fe[:, tok], ALU.min)
                            dve.tensor_scalar(fl[:, tok], psT[bank][0:NH2, 0:P], 0.0, None, ALU.min)\
                                .then_inc(s_tfree[bank], 1)
                    if (c, g) == (F_CHUNK + 1, 1):
                        dve.wait_ge(s_fln, at(l, 2, 2))
                        link(dve.tensor_tensor(fl[:], fe[:], fl[:], ALU.subtract))
                        dve.tensor_tensor_scan(ncum[:], ones[0:NH2, :], fl[:], 0.0, ALU.mult, ALU.add)\
                            .then_inc(s_cum, 1)
            residual(nch - 1)

            dve.memset(rtmp[:, 0:1], 0.0)
            for tb in range(TB):
                last = dve.bn_aggr(mv[:, tb, :], stats[:, tb, :, :])
            last.then_inc(s_var, 1)
            dve.wait_ge(s_std, l + 1)
            link(dve.reciprocal(rstd[:], std[:]))
            dve.wait_ge(s_lnp, at(l, 32, 32))
            for j in range(NCW):
                cols = slice(j * CW, (j + 1) * CW)
                for tb in range(TB):
                    last = dve.tensor_scalar(x[:, tb, cols], x[:, tb, cols], mv[:, tb, 0:1], rstd[:, tb:tb + 1],
                                             ALU.subtract, ALU.mult)
                link(last)
                link(dve.tensor_tensor(x[:, :, cols], x[:, :, cols],
                                       gb[:, 0, cols].unsqueeze(1).broadcast_to([P, TB, CW]), ALU.mult))
                dve.tensor_tensor(x[:, :, cols], x[:, :, cols],
                                  gb[:, 1, cols].unsqueeze(1).broadcast_to([P, TB, CW]), ALU.add).then_inc(s_xn, 1)
        assert links[0] == VLINKS2, links

    @block.tensor
    def _(pe):
        pe.wait_ge(s_const, 64)
        pe.wait_ge(s_mem, 2)

        with pe.Fori(0, DEPTH) as l:

            def fill(name):
                i = FILL2[name]
                pe.wait_ge(s_tfree[i % 2], at(l, NF2 // 2, i // 2 + 1))
                kind, bank = name[0], bank_t(name)
                if kind in "xyaqk":
                    if kind == "x":
                        if name[1] % 2 == 0:
                            pe.wait_ge(s_xn, at(l, NCW, name[1] // 2 + 1))
                        src, col = x, 2 * P * name[1]
                    elif kind == "y":
                        pe.wait_ge(s_y, at(l, NCW, name[1] // 2 + 1))
                        src, col = y, 2 * P * name[1]
                    elif kind == "a":
                        pe.wait_ge(s_att, at(l, TB * NGRP, TB * (name[1] + 1)))
                        src, col = z, 2 * P * name[2]
                    else:
                        if name[1] < 3:
                            pe.wait_ge(s_rope, at(l, NGRP, 2 * name[1] + 1 + (kind == "k")))
                        else:
                            pe.wait_ge(*acc_read(l, group_chunk(name[1]) + (kind == "k")))
                        src, col = stage, 2 * P * name[2]
                    for k in range(2):
                        for tb in range(TB):
                            t = pe.transpose(bank[:, k * SEQ + tb * P:k * SEQ + (tb + 1) * P],
                                             src[:, tb, col + k * P:col + (k + 1) * P], ident[:])
                elif kind == "p":
                    pe.wait_ge(s_exp, at(l, 3 * NGRP, 3 * name[1] + name[2] + 1))
                    for k in range(4):
                        t = pe.transpose(bank[:, k * P:(k + 1) * P], prob[:, name[2], k * P:(k + 1) * P], ident[:])
                else:
                    pe.wait_ge(*unit_read(l, name))
                    t = pe.transpose(bank[0:NH2, 0:P], fb[:, name[1], :], ident[:])
                t.then_inc(s_tfull, 1)

            def unit(name):
                i = UNIT2[name]
                bank = psS[i % 2]
                pe.wait_ge(s_sfree[i % 2], at(l, NU2 // 2, i // 2 + 1))
                if name[0] == "s":
                    _, grp, u = name
                    if u == 0:
                        for p in range(2):
                            pe.wait_ge(*copied(l, ("k", grp, p)))
                        if grp == 3:
                            pe.wait_ge(s_cum, l + 1)
                    w, tb = (P, 0) if u == 0 else (SEQ, 1)
                    for b in range(CW // w):
                        h = b + max(0, 2 * (u - 1))
                        out = bank[:, b * w:(b + 1) * w]
                        m = pe.matmul(out, qT[:, h, tb * P:(tb + 1) * P], kT[:, h, 0:w], start=True, stop=(grp < 3))
                        if grp >= 3:
                            head = HPG * (grp - 3) + h
                            m = pe.matmul(out, ident[0:NH2, head:head + 1].broadcast_to([NH2, P]), ncum[:, 0:w],
                                          start=False, stop=True)
                elif name[0] == "o":
                    _, grp, tb = name
                    if tb == 0:
                        pe.wait_ge(*acc_read(l, group_chunk(grp) + 2))
                    for p in ((0,), (1, 2))[tb]:
                        pe.wait_ge(*copied(l, ("p", grp, p)))
                    for h in range(HPG):
                        for s in range(tb + 1):
                            u, col = (0, h) if tb == 0 else (1 + h // 2, 2 * (h % 2) + s)
                            m = pe.matmul(bank[:, h * HD:(h + 1) * HD], probT[:, u, col * P:(col + 1) * P],
                                          v[:, s, h * HD:(h + 1) * HD], start=(s == 0), stop=(s == tb))
                else:
                    pe.wait_ge(s_fwh, at(l, 2, 2))
                    tok = slice(name[1] * P, (name[1] + 1) * P)
                    for k in range(KT):
                        for q, (a, w) in enumerate(((xhi, wfhi), (xhi, wflo), (xlo, wfhi))):
                            m = pe.matmul(bank[:, 0:NH2], a[:, k, tok], w[:, k, :],
                                          start=(k == 0 and q == 0), stop=(k == KT - 1 and q == 2))
                m.then_inc(s_sfull, 1)

            for c, (kind, j) in enumerate(CHUNKS2):
                ahead, alow = (ahi, alo) if kind == "u" else (xhi, xlo)
                for g in range(granules2(c)):
                    for name in fills2(c, g):
                        fill(name)
                    for name in units2(c, g):
                        unit(name)
                    if c == 0:
                        pe.wait_ge(*copied(l, ("x", g)))
                    if (kind, j) == ("o", 0):
                        pe.wait_ge(*copied(l, ("y", g)))
                    if kind == "u" and j % NCW == 0 and g == 0:
                        for p in range(2):
                            pe.wait_ge(*copied(l, ("a", 2 + 3 * (j // NCW), p)))
                    if g == 0:
                        pe.wait_ge(s_acc[c % 2], at(l, nch // 2, c // 2 + 1))
                    n = FIRST2[c] + g
                    pe.wait_ge(s_lo, at(l, GRAN2, n + 1))
                    for k in range(GK):
                        for tb in range(TB):
                            tile = slice(tb * P, (tb + 1) * P)
                            kk = GK * g + k
                            for q, (a, b) in enumerate(((ahead, whi), (ahead, wlo), (alow, whi))):
                                m = pe.matmul(acc[c % 2][:, tb, :], a[:, kk, tile],
                                              b[:, n % SLOTS, k * CW:(k + 1) * CW],
                                              start=(kk == 0 and q == 0),
                                              stop=(kk == GK * granules2(c) - 1 and q == 2))
                    m.then_inc(s_used, 1)


def rope_tables():
    half = HD // 2
    inv = (np.float32(10000.0) ** (-np.arange(half, dtype=np.float32) / half)).astype(np.float32)
    ang = (np.arange(SEQ, dtype=np.float32)[:, None] * inv[None, :]).astype(np.float32).astype(np.float64)
    t = np.stack([np.cos(ang), np.sin(ang), -np.sin(ang)])
    t = np.stack([t * SCALE2, t]).reshape(2, 3, TB, P, half).transpose(3, 0, 1, 2, 4)
    return np.ascontiguousarray(t.astype(np.float32))


def band(weight):
    t, s = np.arange(P)[:, None], np.arange(SEQ)[None, :]
    return np.concatenate([weight(t - s[:, :P]), weight(t + P - s)], axis=1).astype(np.float32)


def constants():
    count = lambda d: sum(((d >= 0) & (d <= w) & (d % r == 0)).astype(int) for w, r in
                          ((128, 1), (512, 4), (2048, 16)))
    return {
        "ident": np.eye(P, dtype=np.float32),
        "mask_a": band(lambda d: np.where(count(d) > 0, np.log(np.maximum(count(d), 1)), NEG)),
        "mask_b": band(lambda d: np.where(d >= 0, 0.0, NEG)),
        "tables": rope_tables(),
    }


def columns(w, start):
    k = w.shape[0] // P
    return w[:, start:start + CW].reshape(k // GK, GK, P, CW).transpose(0, 2, 1, 3).reshape(k // GK, P, GK * CW)


def second_stream(w_in, w_up_a, w_up_b, w_out):
    starts = {"q": 0, "k": W2, "v": 2 * W2, "z": 3 * W2}
    out = []
    for l in range(DEPTH):
        for kind, j in CHUNKS2:
            if kind in starts:
                out.append(columns(w_in[l], starts[kind] + (4 * W2) * (j // 3) + CW * (j % 3)))
            elif kind == "g":
                out.append(columns(w_in[l], 8 * W2 + NH2 + CW * j))
            elif kind == "u":
                out.append(columns((w_up_a if j < NCW else w_up_b)[l], CW * (j % NCW)))
            else:
                out.append(columns(w_out[l], CW * j))
    return np.concatenate(out)


A_HEADS = 16
A_HD = 64
A_W = A_HEADS * A_HD
A_KV = 4
A_KVW = A_KV * A_HD
A_PER = A_HEADS // A_KV
WINDOW = 128
ROT = A_HD // 4
S_W = D // 4
S_G = 8
S_GD = S_W // S_G
G_HEADS = 4
G_DV = 128
G_DK = 64
G_KW = G_HEADS * G_DK
RANK = 16
TAU = 16.0
EPS = 1e-6
LEVELS = (128, 64, 32, 16, 8, 4, 2, 1)
MOD_W = 1024
MOD_N = KT * D // MOD_W
OFF_GATE = A_W + 2 * A_KVW + 2 * S_W + 2 * G_KW + G_HEADS * G_DV
OFF_Z = OFF_GATE + RANK
CHUNKS1 = [("gqk", A_W + 2 * A_KVW + 2 * S_W), ("gv", A_W + 2 * A_KVW + 2 * S_W + 2 * G_KW), ("kv", A_W),
           ("q0", 0), ("q1", CW), ("su", A_W + 2 * A_KVW), ("sv", A_W + 2 * A_KVW + S_W),
           ("z3", OFF_Z + 3 * CW), ("z2", OFF_Z + 2 * CW), ("z0", OFF_Z), ("z1", OFF_Z + CW)]
C1 = {name: i for i, (name, _) in enumerate(CHUNKS1)}
Z_ORDER = (3, 2, 0, 1)
GPC = KT // GK
NCH1 = len(CHUNKS1) + NCW
GRAN1 = NCH1 * GPC
R_OUT = len(CHUNKS1) * GPC
R_SWA = (52, 59, 66, 73)
R_MOD = {2: 8, 0: 49, 1: 83}
R_MODG, R_MODS, R_MODA = (40, 44), 78, 112


def fills1(l, r):
    if r < 0:
        return []
    out = []
    if r < GPC - 1:
        out += [("h", l, 0), ("h", l, 1)] if r == 0 else [("h", l, r + 1)]
    if r == 12:
        out += [("cg", l), ("gq", l), ("gk", l)]
    if r == 31:
        out += [("ak", l)]
    if r in (41, 49):
        out += [("aq", l, (r - 41) // 8, 0), ("aq", l, (r - 41) // 8, 1)]
    for grp, b in enumerate(R_SWA):
        if 5 <= r - b <= 7:
            out += [("p", l, grp, r - b - 5)]
    if R_OUT <= r < R_OUT + GPC - 1:
        out += [("y", l, 0), ("y", l, 1)] if r == R_OUT else [("y", l, r - R_OUT + 1)]
    return out


def units1(l, r):
    if r < 0:
        return [("ms", 0), ("ma", 0)]
    out = []
    if r == 8:
        out += [("cg", l, 0), ("cg", l, 1)]
    if r == 15:
        out += [("gl", l)]
    if r == 22:
        out += [("sc", l, -1, 0), ("sc", l, -1, 1)]
    if r == 24:
        out += [("dz", l, 0)]
    for i in range(len(LEVELS)):
        if i and r == 22 + 4 * i:
            out += [("dz", l, i)]
        if r == 27 + 4 * i:
            out += [("sc", l, i, 0), ("sc", l, i, 1)]
    if r in R_MODG:
        out += [("mg", l, 2 * R_MODG.index(r) + j) for j in range(2)]
    for grp, b in enumerate(R_SWA):
        if 0 <= r - b <= 2:
            out += [("s", l, grp, r - b)]
        if r - b == 12:
            out += [("o", l, grp)]
    if r in (62, 63):
        out += [("go", l, r - 62)]
    if r in (69, 70):
        out += [("sg", l, r - 69)]
    if l + 1 < DEPTH and r == R_MODS:
        out += [("ms", l + 1)]
    if l + 1 < DEPTH and r == R_MODA:
        out += [("ma", l + 1)]
    return out


STEPS1 = [(0, -1)] + [(l, r) for l in range(DEPTH) for r in range(GRAN1)]
FILL1 = {name: i for i, name in enumerate(n for s in STEPS1 for n in fills1(*s))}
UNIT1 = {name: i for i, name in enumerate(n for s in STEPS1 for n in units1(*s))}
THIRDS = [(0, 0), (0, 1)] + [(0, 2), (1, 0), (1, 1), (1, 2)]


def mod_step(l, r):
    if r >= R_MOD[2] and r < R_MOD[2] + MOD_N:
        return THIRDS.index((l, 2)), r - R_MOD[2]
    for third in (0, 1):
        if l + 1 < DEPTH and R_MOD[third] <= r < R_MOD[third] + MOD_N:
            return THIRDS.index((l + 1, third)), r - R_MOD[third]
    return None


def first_block(nc, ctx, x, rings, ps, dram):
    raw, whi, wlo = rings
    acc, psT, psS = ps

    def sb(name, shape, dt=F32):
        return ctx.enter_context(nc.sbuf_tensor(name, shape, dt))

    def sem(name):
        return ctx.enter_context(nc.semaphore(name))

    hhi = sb("hhi", [P, KT, SEQ], F32R)
    hlo = sb("hlo", [P, KT, SEQ], F32R)
    y = sb("b_y", [P, TB, D])
    macc = sb("macc", [P, D])
    mraw = sb("mraw", [P, 2, MOD_W])
    gain = sb("gain", [P, D])
    stage = sb("b_stage", [P, TB, CW])
    zt = sb("zt", [P, TB, CW])
    scr = sb("scr", [P, 6, CW])
    rt = sb("rt", [P, CW])
    av = sb("av", [P, TB, A_KVW])
    kT = sb("b_kT", [P, A_KV // 2, SEQ])
    qT = sb("b_qT", [P, A_HEADS // 2, SEQ])
    la = sb("la", [P, TB, G_KW])
    st = sb("st", [P, 2, 4, P])
    stx = sb("stx", [P, G_HEADS, P])
    sums = sb("sums", [P, len(LEVELS) + 1, P])
    lmask = sb("lmask", [P, len(LEVELS), P], mybir.dt.uint8)
    wmask = sb("wmask", [P, P + SEQ])
    ident = sb("b_ident", [P, P])
    ones = sb("b_ones", [P, P])
    sgw = sb("sgw", [P, S_G, P])
    lnr = sb("lnr", [P, 2, S_W])
    sgb = sb("sgb", [P, S_G])
    gnorm = sb("gnorm", [P, G_DV])
    wg = sb("wg", [P, KT, RANK])
    wghi = sb("wghi", [P, KT, RANK], F32R)
    wglo = sb("wglo", [P, KT, RANK], F32R)
    gup = sb("gup", [RANK, G_KW])
    gbias = sb("gbias", [P, G_KW])
    cgs = sb("cgs", [P, TB, RANK])
    cgT = sb("cgT", [RANK, SEQ])
    sinks = sb("sinks", [P, A_HEADS])
    cvec = sb("cvec", [P, KT])
    csil = sb("csil", [P, KT])
    gpre = sb("gpre", [P, KT])
    shift = sb("shift", [P, DEPTH, KT])
    scale = sb("scale", [P, DEPTH, KT])
    posi = sb("posi", [P, TB], I32)
    posf = sb("posf", [P, TB])
    invf = sb("invf", [P, ROT // 2])
    ang = sb("ang", [P, 4, TB, ROT // 2])
    cs = sb("cs", [P, 2, TB, ROT // 2])
    mx = sb("b_mx", [P, 3, A_PER])
    snk = sb("snk", [P, TB, A_PER])
    den = sb("b_den", [P, TB, A_PER])
    rden = sb("b_rden", [P, 2, TB, A_PER])
    sq = sb("sq", [P, TB, NCW])
    rms = sb("rms", [P, 2, TB])
    gsq = sb("gsq", [P, 2, TB, G_HEADS])
    stats = sb("b_stats", [P, TB, 6])
    mv = sb("b_mv", [P, TB, 2])
    lstd = sb("lstd", [P, 2, TB])
    eps = sb("b_eps", [P, 1])

    s_w = [sem(f"b_w{i}") for i in range(SLOTS)]
    s_hi = sem("b_hi")
    s_lo = sem("b_lo")
    s_used = sem("b_used")
    s_acc = [sem(f"b_acc{i}") for i in range(2)]
    s_tfull = sem("b_tfull")
    s_thi = sem("b_thi")
    s_tfree = [sem(f"b_tfree{i}") for i in range(2)]
    s_sfull = sem("b_sfull")
    s_sfree = [sem(f"b_sfree{i}") for i in range(2)]
    s_x = sem("b_x")
    s_const = sem("b_const")
    s_mem = sem("b_mem")
    s_par = sem("b_par")
    s_sgw = sem("b_sgw")
    s_m = [sem(f"b_m{i}") for i in range(2)]
    s_macc = sem("b_macc")
    s_mzero = sem("b_mzero")
    s_mbias = sem("b_mbias")
    s_gain = sem("b_gain")
    s_mod = sem("b_mod")
    s_silu = sem("b_silu")
    s_ang = sem("b_ang")
    s_trig = sem("b_trig")
    s_sq = sem("b_sq")
    s_ssum = sem("b_ssum")
    s_rms = sem("b_rms")
    s_xn = sem("b_xn")
    s_h = sem("b_h")
    s_wg = sem("b_wg")
    s_neg = sem("b_neg")
    s_ln = sem("b_ln")
    s_la = sem("b_la")
    s_gx = sem("b_gx")
    s_rope = sem("b_rope")
    s_max = sem("b_max")
    s_exp = sem("b_exp")
    s_y = sem("b_ypart")
    s_gsq = sem("b_gsq")
    s_grms = sem("b_grms")
    s_var = sem("b_var")
    s_std = sem("b_std")
    s_vn = sem("b_vn")
    s_ym = sem("b_ym")
    s_xd = sem("b_xd")
    s_self = sem("b_self")

    block = ctx.enter_context(nc.Block())
    gv = y[:, :, 0:CW]
    gqT, gkT = y[:, 0, CW:2 * CW], y[:, 1, CW:2 * CW]
    ks = scr[:, 5, :].rearrange("p (b n) -> p b n", b=TB)
    junk = scr[:].rearrange("p a n -> p (a n)").bitcast(mybir.dt.bfloat16)

    def need(eng, sv):
        if sv[1] > 0:
            eng.wait_ge(*sv)

    def chunk(l, name):
        return l * NCH1 + (len(CHUNKS1) + name if isinstance(name, int) else C1[name])

    def multiplied(c):
        return s_used, GPC * (c + 1)

    def acc_read(c):
        return s_acc[c % 2], c // 2 + 1

    def unit_full(name):
        return s_sfull, UNIT1[name] + 1

    def unit_read(name):
        return s_sfree[UNIT1[name] % 2], UNIT1[name] // 2 + 1

    def bank_s(name):
        return psS[UNIT1[name] % 2]

    def filled(name):
        return s_tfull, FILL1[name] + 1

    def copied(name):
        return s_tfree[FILL1[name] % 2], FILL1[name] // 2 + 1

    def bank_t(name):
        return psT[FILL1[name] % 2]

    def split_index(name):
        return GPC * (2 * name[1] + (name[0] == "y")) + name[2]

    def exp_index(l, grp, u):
        return 3 * (A_KV * l + grp) + u + 1

    n_par = 10

    @block.sync
    def _(sp):
        sp.dma_start(x[:], dram["x"].rearrange("(b p) n -> p b n", p=P)).then_inc(s_x, 16)

        def mod(q, i):
            n = MOD_N * q + i
            if n >= 2:
                sp.wait_ge(s_macc, n - 1)
            l, third = THIRDS[q]
            sp.dma_start(mraw[:, n % 2, :], dram["w_mod"][l, third, i]).then_inc(s_m[n % 2], 16)

        for q in range(2):
            for i in range(MOD_N):
                mod(q, i)
        for n in range(DEPTH * GRAN1):
            step = mod_step(*divmod(n, GRAN1))
            if n >= SLOTS:
                sp.wait_ge(s_lo, n - SLOTS + 1)
            sp.dma_start(raw[:, n % SLOTS, :], dram["w1"][n]).then_inc(s_w[n % SLOTS], 16)
            if step:
                mod(*step)

    @block.gpsimd
    def _(pool):
        pool.dma_start(cvec[:], dram["c"]).then_inc(s_const, 16)
        for tile, name in ((posi, "positions"), (ident, "ident"), (sums, "sums"), (y[:, 0, 0:len(LEVELS) * P].rearrange("p (i n) -> p i n", n=P), "lmask"),
                           (wmask, "mask_w")):
            pool.dma_start(tile[:], dram[name]).then_inc(s_const, 16)
        pool.dma_start(invf[:], dram["inv_freq"].partition_broadcast(P)).then_inc(s_const, 16)

        def mod_bias(q):
            l, third = THIRDS[q]
            pool.wait_ge(s_mzero, q + 1)
            pool.dma_start(macc[0:1, :], dram["b_mod"][l, third:third + 1, :]).then_inc(s_mbias, 16)

        def parameters(l):
            if l:
                pool.wait_ge(s_ym, NCW * l)
            pool.dma_start(gpre[:], dram["g_pre"][l]).then_inc(s_par, 16)
            pool.dma_start(wg[:], dram["wg"][l]).then_inc(s_par, 16)
            pool.dma_start(gup[:], dram["gate_up"][l]).then_inc(s_par, 16)
            pool.dma_start(gbias[:], dram["b_gate"][l].partition_broadcast(P)).then_inc(s_par, 16)
            pool.dma_start(gnorm[:], dram["gnorm"][l].partition_broadcast(P)).then_inc(s_par, 16)
            pool.dma_start(sinks[:], dram["sinks"][l].partition_broadcast(P)).then_inc(s_par, 16)
            pool.dma_start(sgb[:], dram["sg_b"][l]).then_inc(s_par, 16)
            pool.dma_start(lnr[:, 0, :], dram["sg_ln_g"][l].partition_broadcast(P)).then_inc(s_par, 16)
            pool.dma_start(lnr[:, 1, :], dram["sg_ln_b"][l].partition_broadcast(P)).then_inc(s_par, 16)
            pool.dma_start(sgw[:], dram["sg_w"][l]).then_inc(s_par, 16)
            pool.wait_ge(s_par, 16 * n_par * (l + 1))
            pool.affine_select(out=sgw[:], in_=sgw[:], compare_op=ALU.is_ge, fill=0.0, base=0,
                               pattern=[[0, S_G], [1, P]], channel_multiplier=-1).then_inc(s_sgw, 1)

        mod_bias(0)
        parameters(0)
        mod_bias(1)
        for l in range(DEPTH):
            if l:
                pool.wait_ge(s_xd, NCW * l)
            pool.dma_start(gain[:], dram["g_post"][l].partition_broadcast(P)).then_inc(s_gain, 16)
            mod_bias(THIRDS.index((l, 2)))
            if l + 1 < DEPTH:
                mod_bias(THIRDS.index((l + 1, 0)))
                mod_bias(THIRDS.index((l + 1, 1)))
                parameters(l + 1)

    @block.scalar
    def _(act):
        act.wait_ge(s_const, 112)
        act.wait_ge(s_mem, 2)
        act.activation(csil[:], cvec[:], ACT.Silu).then_inc(s_silu, 1)

        def hi(n):
            act.wait_ge(s_w[n % SLOTS], 16 * (n // SLOTS + 1))
            if n >= SLOTS:
                act.wait_ge(s_used, n - SLOTS + 1)
            act.activation(whi[:, n % SLOTS, :], raw[:, n % SLOTS, :], ACT.Copy).then_inc(s_hi, 1)

        def fill_copy(name, dst, rows=P, n=CW):
            act.wait_ge(*filled(name))
            act.activation(dst, bank_t(name)[0:rows, 0:n], ACT.Copy).then_inc(s_tfree[FILL1[name] % 2], 1)

        def fill_hi(name):
            if name[0] == "h":
                act.wait_ge(*copied(name))
                src = zt[:, name[2] % 2, :]
            else:
                act.wait_ge(*filled(name))
                src = bank_t(name)[:]
            k = 2 * name[2] if name[0] == "h" else y_tile(name[2])
            act.activation(hhi[:, k:k + 2, :], src.rearrange("p (k t) -> p k t", k=2), ACT.Copy).then_inc(s_thi, 1)

        def squares(src, j, last_inc=None):
            for tb in range(TB):
                k = TB * j + tb
                last = act.activation(junk[:, k * CW:(k + 1) * CW], src[:, tb, :], ACT.Square,
                                      accum_out=sq[:, tb, j:j + 1])
            last.then_inc(last_inc, 1)

        def root(n):
            act.wait_ge(s_ssum, n + 1)
            act.activation(rms[:, 0, :], rms[:, 1, :], ACT.Sqrt, scale=1.0 / D, bias=eps[:, 0:1]).then_inc(s_rms, 1)

        def x_squares(l):
            for j in range(NCW):
                if l:
                    act.wait_ge(s_xd, NCW * (l - 1) + j + 1)
                squares(x[:, :, j * CW:(j + 1) * CW], j, s_sq)

        def out_chunk(l, j):
            c = chunk(l, j)
            act.wait_ge(*multiplied(c))
            act.activation(y[:, :, j * CW:(j + 1) * CW], acc[c % 2][:], ACT.Copy)
            squares(acc[c % 2], j, s_acc[c % 2])

        act.wait_ge(s_ang, 1)
        act.activation(cs[:].rearrange("p a b n -> p (a b n)"), ang[:, 0:2].rearrange("p a b n -> p (a b n)"),
                       ACT.Sin).then_inc(s_trig, 1)
        act.wait_ge(s_x, 16)
        for l in range(DEPTH):
            x_squares(l)
            root(2 * l)
            for r in range(GRAN1):
                if r < GPC:
                    fill_hi(("h", l, r))
                if R_OUT <= r < R_OUT + GPC:
                    fill_hi(("y", l, r - R_OUT))
                hi(GRAN1 * l + r)
                if r == 7:
                    act.wait_ge(s_par, 16 * n_par * (l + 1))
                    act.activation(wghi[:], wg[:], ACT.Copy).then_inc(s_wg, 1)
                if r == 12:
                    c = chunk(l, "gqk")
                    act.wait_ge(*multiplied(c))
                    act.activation(stage[:, :, 0:G_KW], acc[c % 2][:, :, 0:G_KW], ACT.Copy, scale=G_DK ** -0.5)
                    act.activation(stage[:, :, G_KW:], acc[c % 2][:, :, G_KW:], ACT.Copy).then_inc(s_acc[c % 2], 1)
                if r == 14:
                    fill_copy(("cg", l), cgT[:], RANK, SEQ)
                if r == 15:
                    fill_copy(("gq", l), gqT)
                if r == 16:
                    fill_copy(("gk", l), gkT)
                if r == 19:
                    act.wait_ge(s_neg, l + 1)
                    act.activation(zt[:, 0, :], zt[:, 0, :], ACT.Exp).then_inc(s_ln, 1)
                    act.wait_ge(s_ln, 2 * l + 1)
                    act.activation(zt[:, 0, :], zt[:, 0, :], ACT.Ln, bias=1.0).then_inc(s_ln, 1)
                if r == 20:
                    c = chunk(l, "gv")
                    act.wait_ge(*multiplied(c))
                    act.activation(gv, acc[c % 2][:], ACT.Copy).then_inc(s_acc[c % 2], 1)
                for i in range(len(LEVELS)):
                    if r == (26 + 4 * i if i else 27):
                        if i >= 2:
                            act.wait_ge(*unit_full(("sc", l, i - 2, 1)))
                        act.wait_ge(*unit_full(("dz", l, i)))
                        act.activation(zt[:, i % 2, :], bank_s(("dz", l, i))[:], ACT.Exp)\
                            .then_inc(s_sfree[UNIT1["dz", l, i] % 2], 1)
                if r == 28:
                    c = chunk(l, "kv")
                    act.wait_ge(*multiplied(c))
                    act.activation(ks, acc[c % 2][:, :, 0:A_KVW], ACT.Copy)
                    act.activation(av[:], acc[c % 2][:, :, A_KVW:], ACT.Copy).then_inc(s_acc[c % 2], 1)
                if r == 34:
                    fill_copy(("ak", l), kT[:].rearrange("p k t -> p (k t)"))
                if r in (36, 44):
                    c = chunk(l, "q0" if r == 36 else "q1")
                    if r == 44:
                        act.wait_ge(*filled(("aq", l, 0, 1)))
                    act.wait_ge(*multiplied(c))
                    dst = stage[:].rearrange("p b (i s e) -> p b i s e", s=2, e=A_HD)
                    for s in range(2):
                        last = act.activation(dst[:, :, :, s, :], acc[c % 2][:, :, s * A_KVW:(s + 1) * A_KVW]
                                              .rearrange("p b (i e) -> p b i e", e=A_HD), ACT.Copy,
                                              scale=A_HD ** -0.5)
                    last.then_inc(s_acc[c % 2], 1)
                if r in (45, 53):
                    i = (r - 45) // 8
                    for k in range(2):
                        a = 4 * i + 2 * k
                        fill_copy(("aq", l, i, k), qT[:, a:a + 2, :].rearrange("p h t -> p (h t)"))
                for grp, b in enumerate(R_SWA):
                    if 5 <= r - b <= 7:
                        u = r - b - 5
                        act.wait_ge(s_max, exp_index(l, grp, u))
                        w = P if u == 0 else SEQ
                        h0, n = max(0, 2 * (u - 1)), CW // w
                        act.activation(snk[:, min(u, 1), h0:h0 + n], snk[:, min(u, 1), h0:h0 + n], ACT.Exp)
                        for i in range(n):
                            p = act.activation(scr[:, u, i * w:(i + 1) * w], scr[:, u, i * w:(i + 1) * w], ACT.Exp,
                                               bias=mx[:, u, i:i + 1], accum_out=den[:, min(u, 1), h0 + i:h0 + i + 1])
                        p.then_inc(s_exp, 1)
                    if 9 <= r - b <= 11:
                        fill_copy(("p", l, grp, r - b - 9), scr[:, 3 + r - b - 9, :])
                if r == 52:
                    c = chunk(l, "su")
                    act.wait_ge(*multiplied(c))
                    act.activation(y[:, :, 2 * CW:3 * CW], acc[c % 2][:], ACT.Gelu_apprx_tanh)\
                        .then_inc(s_acc[c % 2], 1)
                if r == 60:
                    c = chunk(l, "sv")
                    act.wait_ge(*multiplied(c))
                    act.wait_ge(*unit_full(("sc", l, len(LEVELS) - 1, 1)))
                    act.activation(zt[:], acc[c % 2][:], ACT.Gelu_apprx_tanh).then_inc(s_acc[c % 2], 1)
                if r == 62:
                    act.wait_ge(s_var, l + 1)
                    act.activation(lstd[:, 0, :], mv[:, :, 1], ACT.Sqrt, bias=eps[:, 0:1]).then_inc(s_std, 1)
                if r == 66:
                    for tb in range(TB):
                        act.wait_ge(*unit_full(("go", l, tb)))
                        act.activation(y[:, tb, 3 * CW:], bank_s(("go", l, tb))[:], ACT.Copy)\
                            .then_inc(s_sfree[UNIT1["go", l, tb] % 2], 1)
                if r == 69:
                    act.wait_ge(s_gsq, l + 1)
                    act.activation(gsq[:, 1], gsq[:, 0], ACT.Sqrt, scale=1.0 / G_DV, bias=eps[:, 0:1])\
                        .then_inc(s_grms, 1)
                if r in (72, 76, 84, 92):
                    i = (72, 76, 84, 92).index(r)
                    c = chunk(l, f"z{Z_ORDER[i]}")
                    act.wait_ge(*multiplied(c))
                    if i == 0:
                        act.wait_ge(*unit_full(("sg", l, 1)))
                    else:
                        act.wait_ge(s_ym, NCW * l + i)
                    act.activation(zt[:], acc[c % 2][:], ACT.Silu).then_inc(s_acc[c % 2], 1)
                if r >= R_OUT + GPC and (r - R_OUT) % GPC == 4:
                    out_chunk(l, (r - R_OUT) // GPC - 1)
            out_chunk(l, NCW - 1)
            root(2 * l + 1)

    @block.vector
    def _(dve):
        links = [0]

        def link(ins):
            links[0] += 1
            ins.then_inc(s_self, 1)
            dve.wait_ge(s_self, links[0])

        def lo(n):
            dve.wait_ge(s_hi, n + 1)
            dve.tensor_tensor(wlo[:, n % SLOTS, :], raw[:, n % SLOTS, :], whi[:, n % SLOTS, :].bitcast(F32),
                              ALU.subtract).then_inc(s_lo, 1)

        def fill_lo(name):
            dve.wait_ge(s_thi, split_index(name) + 1)
            if name[0] == "h":
                k, src = 2 * name[2], zt[:, name[2] % 2, :]
                signal = s_h
            else:
                k, src = y_tile(name[2]), bank_t(name)[:]
                signal = s_tfree[FILL1[name] % 2]
            dve.tensor_tensor(hlo[:, k:k + 2, :], src.rearrange("p (k t) -> p k t", k=2),
                              hhi[:, k:k + 2, :].bitcast(F32), ALU.subtract).then_inc(signal, 1)

        def fill_mod(l, i):
            name = ("h", l, i)
            dve.wait_ge(*filled(name))
            if i >= 2:
                dve.wait_ge(s_h, GPC * l + i - 1)
            for k in range(2):
                kt = 2 * i + k
                last = dve.tensor_scalar(zt[:, i % 2, k * SEQ:(k + 1) * SEQ], bank_t(name)[:, k * SEQ:(k + 1) * SEQ],
                                         scale[:, l, kt:kt + 1], shift[:, l, kt:kt + 1], ALU.mult, ALU.add)
            last.then_inc(s_tfree[FILL1[name] % 2], 1)

        def mod_zero(q):
            if q:
                l, third = THIRDS[q - 1]
                dve.wait_ge(*unit_full(("ms", l) if third == 0 else ("ma", l) if third == 1 else ("mg", l, NCW - 1)))
            dve.memset(macc[:], 0.0).then_inc(s_mzero, 1)

        def mod(q, i):
            n = MOD_N * q + i
            kt, half = divmod(i, D // MOD_W)
            cols = slice(half * MOD_W, (half + 1) * MOD_W)
            if i == 0:
                dve.wait_ge(s_mbias, 16 * (q + 1))
            if i >= 2:
                dve.wait_ge(s_macc, n - 1)
            dve.wait_ge(s_m[n % 2], 16 * (n // 2 + 1))
            dve.scalar_tensor_tensor(out=macc[:, cols], in0=mraw[:, n % 2, :], scalar=csil[:, kt:kt + 1],
                                     in1=macc[:, cols], op0=ALU.mult, op1=ALU.add).then_inc(s_macc, 1)

        def mod_shift(l):
            dve.wait_ge(*unit_full(("ms", l)))
            dve.tensor_copy(shift[:, l, :], bank_s(("ms", l))[:, 0:KT]).then_inc(s_sfree[UNIT1["ms", l] % 2], 1)

        def mod_scale(l):
            dve.wait_ge(*unit_full(("ma", l)))
            dve.wait_ge(s_par, 16 * n_par * (l + 1))
            dve.scalar_tensor_tensor(out=scale[:, l, :], in0=bank_s(("ma", l))[:, 0:KT], scalar=1.0, in1=gpre[:],
                                     op0=ALU.add, op1=ALU.mult).then_inc(s_sfree[UNIT1["ma", l] % 2], 1)
            dve.wait_ge(*unit_read(("ma", l)))

        def mean_square(n):
            dve.tensor_reduce(rms[:, 1, :], sq[:], AX.X, ALU.add).then_inc(s_ssum, 1)
            dve.wait_ge(s_rms, n + 1)
            link(dve.reciprocal(rms[:, 1, :], rms[:, 0, :]))

        def rope(src, heads):
            half = ROT // 2
            v4 = src.rearrange("p b (h e) -> p b h e", e=A_HD)
            t1, t2 = v4[:, :, :, 0:half], v4[:, :, :, half:ROT]
            n = TB * heads * half
            tmp = [rt[:, i * n:(i + 1) * n].rearrange("p (b h e) -> p b h e", b=TB, e=half) for i in range(4)]
            cos, sin = (cs[:, i].unsqueeze(2).broadcast_to([P, TB, heads, half]) for i in range(2))
            dve.tensor_tensor(tmp[0], t1, cos, ALU.mult)
            dve.tensor_tensor(tmp[1], t2, sin, ALU.mult)
            dve.tensor_tensor(tmp[2], t2, cos, ALU.mult)
            link(dve.tensor_tensor(tmp[3], t1, sin, ALU.mult))
            dve.tensor_tensor(t1, tmp[0], tmp[1], ALU.subtract)
            link(dve.tensor_tensor(t2, tmp[2], tmp[3], ALU.add))
            dve.memset(rt[:, 0:1], 0.0).then_inc(s_rope, 1)

        def scores(l, grp, u):
            name = ("s", l, grp, u)
            n, w, m = (A_PER, P, wmask[:, 0:P]) if u == 0 else (2, SEQ, wmask[:, P:P + SEQ])
            h0 = max(0, 2 * (u - 1))
            sink = sinks[:, A_PER * grp + h0:A_PER * grp + h0 + n]
            dve.wait_ge(*unit_full(name))
            p = scr[:, u, :].rearrange("p (h s) -> p h s", s=w)
            dve.tensor_tensor(p, bank_s(name)[:].rearrange("p (h s) -> p h s", s=w),
                              m.unsqueeze(1).broadcast_to([P, n, w]), ALU.add).then_inc(s_sfree[UNIT1[name] % 2], 1)
            dve.wait_ge(*unit_read(name))
            link(dve.tensor_reduce(mx[:, u, 0:n], p, AX.X, ALU.max))
            link(dve.tensor_tensor(mx[:, u, 0:n], mx[:, u, 0:n], sink, ALU.max))
            link(dve.tensor_scalar(mx[:, u, 0:n], mx[:, u, 0:n], -1.0, None, ALU.mult))
            dve.tensor_tensor(snk[:, min(u, 1), h0:h0 + n], sink, mx[:, u, 0:n], ALU.add).then_inc(s_max, 1)

        def denominators(l, grp):
            dve.wait_ge(s_exp, exp_index(l, grp, 2))
            link(dve.tensor_tensor(den[:], den[:], snk[:], ALU.add))
            link(dve.reciprocal(rden[:, grp % 2], den[:]))

        def attended(l, grp):
            name = ("o", l, grp)
            dve.wait_ge(*unit_full(name))
            if grp == 0:
                dve.wait_ge(*unit_full(("go", l, 1)))
            for tb in range(TB):
                last = dve.tensor_tensor(y[:, tb, grp * A_KVW:(grp + 1) * A_KVW].rearrange("p (h e) -> p h e", e=A_HD),
                                         bank_s(name)[:, tb * A_KVW:(tb + 1) * A_KVW]
                                         .rearrange("p (h e) -> p h e", e=A_HD),
                                         rden[:, grp % 2, tb, :].unsqueeze(2).broadcast_to([P, A_PER, A_HD]), ALU.mult)
            last.then_inc(s_sfree[UNIT1[name] % 2], 1)
            dve.wait_ge(*unit_read(name))

        def angles():
            tau = 2.0 * np.pi
            parts = [6.28125]
            parts.append(float(np.float32(np.round((tau - parts[0]) * 2 ** 21) / 2 ** 21)))
            parts.append(float(np.float32(tau - parts[0] - parts[1])))
            magic = 1.5 * 2.0 ** 23
            link(dve.tensor_copy(posf[:], posi[:]))
            for tb in range(TB):
                last = dve.tensor_scalar(ang[:, 0, tb, :], invf[:], posf[:, tb:tb + 1], None, ALU.mult)
            link(last)
            a, n, r, t = (ang[:, i].rearrange("p b e -> p (b e)") for i in (0, 1, 2, 3))
            link(dve.tensor_scalar(n, a, 1.0 / tau, None, ALU.mult))
            link(dve.tensor_scalar(t, n, magic, None, ALU.add))
            link(dve.tensor_scalar(n, t, magic, None, ALU.subtract))
            link(dve.scalar_tensor_tensor(out=r, in0=n, scalar=-parts[0], in1=a, op0=ALU.mult, op1=ALU.add))
            link(dve.scalar_tensor_tensor(out=t, in0=n, scalar=-parts[1], in1=r, op0=ALU.mult, op1=ALU.add))
            link(dve.scalar_tensor_tensor(out=r, in0=n, scalar=-parts[2], in1=t, op0=ALU.mult, op1=ALU.add))
            link(dve.tensor_scalar(n, r, 3.1415925, -3.1415925, ALU.min, ALU.max))
            link(dve.tensor_scalar(t, n, -1.0, None, ALU.mult))
            link(dve.tensor_tensor(t, t, n, ALU.max))
            dve.tensor_scalar(a, t, -1.0, float(np.pi / 2), ALU.mult, ALU.add).then_inc(s_ang, 1)

        dve.memset(ones[:], 1.0).then_inc(s_mem, 1)
        dve.memset(eps[:], EPS).then_inc(s_mem, 1)
        mod_zero(0)
        dve.wait_ge(s_mem, 2)
        dve.wait_ge(s_const, 112)
        link(dve.tensor_copy(lmask[:].rearrange("p i n -> p (i n)"), y[:, 0, 0:len(LEVELS) * P]))
        angles()
        dve.wait_ge(s_silu, 1)
        for q in range(2):
            if q:
                mod_zero(q)
                mod_shift(0)
            for i in range(MOD_N):
                mod(q, i)
        mod_scale(0)
        mod_zero(2)

        for l in range(DEPTH):
            dve.wait_ge(s_sq, NCW * (l + 1))
            mean_square(2 * l)
            for j in range(NCW):
                cols = slice(j * CW, (j + 1) * CW)
                for tb in range(TB):
                    last = dve.tensor_scalar(y[:, tb, cols], x[:, tb, cols], rms[:, 1, tb:tb + 1], None, ALU.mult)
                last.then_inc(s_xn, 1)
            for r in range(GRAN1):
                if r < GPC:
                    if r == 0:
                        fill_mod(l, 0)
                    if r + 1 < GPC:
                        fill_mod(l, r + 1)
                    fill_lo(("h", l, r))
                if R_OUT <= r < R_OUT + GPC:
                    fill_lo(("y", l, r - R_OUT))
                lo(GRAN1 * l + r)
                if r == 8:
                    dve.wait_ge(s_wg, 2 * l + 1)
                    dve.tensor_tensor(wglo[:], wg[:], wghi[:].bitcast(F32), ALU.subtract).then_inc(s_wg, 1)
                if r == 11:
                    for tb in range(TB):
                        name = ("cg", l, tb)
                        dve.wait_ge(*unit_full(name))
                        dve.tensor_copy(cgs[:, tb, :], bank_s(name)[:, 0:RANK]).then_inc(s_sfree[UNIT1[name] % 2], 1)
                if r == 18:
                    name = ("gl", l)
                    flat = la[:].rearrange("p b n -> p (b n)")
                    dve.wait_ge(*unit_full(name))
                    dve.tensor_tensor(la[:], bank_s(name)[:].rearrange("p (b n) -> p b n", b=TB),
                                      gbias[:].unsqueeze(1).broadcast_to([P, TB, G_KW]), ALU.add)\
                        .then_inc(s_sfree[UNIT1[name] % 2], 1)
                    dve.wait_ge(*unit_read(name))
                    link(dve.tensor_scalar(zt[:, 0, :], flat, -1.0, None, ALU.mult))
                    dve.tensor_tensor(zt[:, 0, :], zt[:, 0, :], flat, ALU.min).then_inc(s_neg, 1)
                    dve.wait_ge(s_neg, l + 1)
                    link(dve.tensor_scalar(flat, flat, 0.0, 1.0 / TAU, ALU.min, ALU.mult))
                if r == 21:
                    flat = la[:].rearrange("p b n -> p (b n)")
                    dve.wait_ge(s_ln, 2 * l + 2)
                    dve.scalar_tensor_tensor(out=flat, in0=zt[:, 0, :], scalar=-1.0 / TAU, in1=flat,
                                             op0=ALU.mult, op1=ALU.add).then_inc(s_la, 1)
                    link(dve.memset(st[:], 0.0))
                for i in range(-1, len(LEVELS)):
                    if i >= 0 and r == 28 + 4 * i:
                        m = LEVELS[i]
                        dve.wait_ge(*unit_read(("dz", l, i)))
                        for src, half in ((gqT, 1), (gkT, 0)):
                            a = zt[:, i % 2, :].rearrange("p (n s m) -> p n s m", s=2, m=m)[:, :, half, :]
                            b = src.rearrange("p (n s m) -> p n s m", s=2, m=m)[:, :, half, :]
                            last = dve.tensor_tensor(a, a, b, ALU.mult)
                        last.then_inc(s_gx, 1)
                    if r == (31 + 4 * i if i >= 0 else 26):
                        for odd in range(2):
                            name = ("sc", l, i, odd)
                            bank = bank_s(name)
                            dve.wait_ge(*unit_full(name))
                            if i == 0:
                                dst = stx[:].rearrange("p (k o) t -> p k o t", o=2)[:, :, odd, :]
                                ins = dve.tensor_copy(dst, bank[:, 0:2 * P].rearrange("p (k t) -> p k t", t=P))
                            else:
                                mask = lmask[:, i if i > 0 else 0, :].unsqueeze(1).broadcast_to([P, 4, P])
                                ins = dve.copy_predicated(st[:, odd], mask, bank[:].rearrange("p (k t) -> p k t", t=P))
                            ins.then_inc(s_sfree[UNIT1[name] % 2], 1)
                            dve.wait_ge(*unit_read(name))
                if r == 30:
                    dve.wait_ge(*acc_read(chunk(l, "kv")))
                    rope(ks, A_KV)
                if r in (37, 45):
                    dve.wait_ge(*acc_read(chunk(l, "q0" if r == 37 else "q1")))
                    rope(stage[:], A_HEADS // 2)
                if r - 4 in R_MODG:
                    for j in range(2 * R_MODG.index(r - 4), 2 * R_MODG.index(r - 4) + 2):
                        name = ("mg", l, j)
                        dve.wait_ge(s_gain, 16 * (l + 1))
                        dve.wait_ge(*unit_full(name))
                        dve.tensor_tensor(gain[:, j * CW:(j + 1) * CW], gain[:, j * CW:(j + 1) * CW], bank_s(name)[:],
                                          ALU.mult).then_inc(s_sfree[UNIT1[name] % 2], 1)
                    if r - 4 == R_MODG[1] and l + 1 < DEPTH:
                        mod_zero(THIRDS.index((l + 1, 0)))
                if l + 1 < DEPTH and r == R_MODS + 4:
                    mod_shift(l + 1)
                    mod_zero(THIRDS.index((l + 1, 1)))
                if l + 1 < DEPTH and r == R_MODA + 4:
                    mod_scale(l + 1)
                    mod_zero(THIRDS.index((l + 1, 2)))
                for grp, b in enumerate(R_SWA):
                    if 4 <= r - b <= 6:
                        scores(l, grp, r - b - 4)
                    if r - b == 9:
                        denominators(l, grp)
                    if r - b == 16:
                        attended(l, grp)
                if r == 61:
                    dve.wait_ge(*acc_read(chunk(l, "sv")))
                    for tb in range(TB):
                        last = dve.bn_stats(stats[:, tb, :], zt[:, tb, :])
                    link(last)
                    for tb in range(TB):
                        last = dve.bn_aggr(mv[:, tb, :], stats[:, tb, :])
                    last.then_inc(s_var, 1)
                if r == 63:
                    dve.wait_ge(s_std, l + 1)
                    link(dve.reciprocal(lstd[:, 1, :], lstd[:, 0, :]))
                    for tb in range(TB):
                        last = dve.tensor_scalar(zt[:, tb, :], zt[:, tb, :], mv[:, tb, 0:1], lstd[:, 1, tb:tb + 1],
                                                 ALU.subtract, ALU.mult)
                    link(last)
                    link(dve.tensor_tensor(zt[:], zt[:], lnr[:, 0, :].unsqueeze(1).broadcast_to([P, TB, S_W]), ALU.mult))
                if r == 64:
                    dve.tensor_tensor(zt[:], zt[:], lnr[:, 1, :].unsqueeze(1).broadcast_to([P, TB, S_W]), ALU.add)\
                        .then_inc(s_vn, 1)
                if r in (67, 68):
                    tb = r - 67
                    dve.wait_ge(*unit_read(("go", l, tb)))
                    link(dve.tensor_tensor(rt[:], y[:, tb, 3 * CW:], y[:, tb, 3 * CW:], ALU.mult))
                    last = dve.tensor_reduce(gsq[:, 0, tb, :], rt[:].rearrange("p (h e) -> p h e", e=G_DV), AX.X, ALU.add)
                    if tb == 0:
                        link(last)
                    else:
                        last.then_inc(s_gsq, 1)
                        dve.wait_ge(s_gsq, l + 1)
                if r == 70:
                    dve.wait_ge(s_grms, l + 1)
                    link(dve.reciprocal(gsq[:, 0], gsq[:, 1]))
                    gy = y[:, :, 3 * CW:].rearrange("p b (h e) -> p b h e", e=G_DV)
                    link(dve.tensor_tensor(gy, gy, gsq[:, 0].unsqueeze(3).broadcast_to([P, TB, G_HEADS, G_DV]), ALU.mult))
                    for tb in range(TB):
                        last = dve.tensor_tensor(gy[:, tb], gy[:, tb],
                                                 gnorm[:].unsqueeze(1).broadcast_to([P, G_HEADS, G_DV]), ALU.mult)
                    link(last)
                if r == 73:
                    for tb in range(TB):
                        name = ("sg", l, tb)
                        dve.wait_ge(*unit_full(name))
                        dve.tensor_tensor(rt[:].rearrange("p (g e) -> p g e", e=S_GD),
                                          bank_s(name)[:].rearrange("p (g e) -> p g e", e=S_GD),
                                          sgb[:].unsqueeze(2).broadcast_to([P, S_G, S_GD]), ALU.add)\
                            .then_inc(s_sfree[UNIT1[name] % 2], 1)
                        dve.wait_ge(*unit_read(name))
                        link(dve.tensor_tensor(y[:, tb, 2 * CW:3 * CW], y[:, tb, 2 * CW:3 * CW], rt[:], ALU.mult))
                if r in (73, 77, 85, 93):
                    i = (73, 77, 85, 93).index(r)
                    j = Z_ORDER[i]
                    dve.wait_ge(*acc_read(chunk(l, f"z{j}")))
                    dve.tensor_tensor(y[:, :, j * CW:(j + 1) * CW], y[:, :, j * CW:(j + 1) * CW], zt[:], ALU.mult)\
                        .then_inc(s_ym, 1)
                step = mod_step(l, r)
                if step:
                    mod(*step)
            for j in (NCW - 2, NCW - 1):
                dve.wait_ge(*acc_read(chunk(l, j)))
            mean_square(2 * l + 1)
            for j in range(NCW):
                cols = slice(j * CW, (j + 1) * CW)
                for tb in range(TB):
                    last = dve.scalar_tensor_tensor(out=y[:, tb, cols], in0=y[:, tb, cols], scalar=rms[:, 1, tb:tb + 1],
                                                    in1=gain[:, cols], op0=ALU.mult, op1=ALU.mult)
                link(last)
                dve.tensor_tensor(x[:, :, cols], x[:, :, cols], y[:, :, cols], ALU.add).then_inc(s_xd, 1)

    @block.tensor
    def _(pe):
        pe.wait_ge(s_const, 112)
        pe.wait_ge(s_mem, 2)

        def fill(name):
            i, bank, kind, l = FILL1[name], bank_t(name), name[0], name[1]
            need(pe, (s_tfree[i % 2], i // 2))
            if kind == "h":
                pe.wait_ge(s_xn, NCW * l + name[2] // 2 + 1)
                src, cols = y, [P * (2 * name[2] + k) for k in range(2)]
            elif kind == "y":
                pe.wait_ge(s_ym, NCW * l + name[2] // 2 + 1)
                src, cols = y, [P * (y_tile(name[2]) + k) for k in range(2)]
            elif kind in ("gq", "gk"):
                pe.wait_ge(*acc_read(chunk(l, "gqk")))
                src, cols = stage, [(kind == "gk") * G_KW + k * P for k in range(2)]
            elif kind == "ak":
                pe.wait_ge(s_rope, 3 * l + 1)
                src, cols = ks, [k * P for k in range(2)]
            elif kind == "aq":
                pe.wait_ge(s_rope, 3 * l + 2 + name[2])
                src, cols = stage, [P * (2 * name[3] + k) for k in range(2)]
            if kind == "p":
                pe.wait_ge(s_exp, exp_index(l, name[2], name[3]))
                for k in range(4):
                    t = pe.transpose(bank[:, k * P:(k + 1) * P], scr[:, name[3], k * P:(k + 1) * P], ident[:])
            elif kind == "cg":
                for tb in range(TB):
                    pe.wait_ge(*unit_read(("cg", l, tb)))
                    t = pe.transpose(bank[0:RANK, tb * P:(tb + 1) * P], cgs[:, tb, :], ident[:])
            else:
                for k in range(2):
                    for tb in range(TB):
                        t = pe.transpose(bank[:, k * SEQ + tb * P:k * SEQ + (tb + 1) * P],
                                         src[:, tb, cols[k]:cols[k] + P], ident[:])
            t.then_inc(s_tfull, 1)

        def unit(name):
            i, bank, kind, l = UNIT1[name], bank_s(name), name[0], name[1]
            need(pe, (s_sfree[i % 2], i // 2))
            if kind in ("ms", "ma", "mg"):
                q = THIRDS.index((l, ("ms", "ma", "mg").index(kind)))
                pe.wait_ge(s_macc, MOD_N * (q + 1))
                if kind == "mg":
                    m = pe.matmul(bank[:], ones[:], macc[:, name[2] * CW:(name[2] + 1) * CW], start=True, stop=True)
                else:
                    for k in range(KT):
                        m = pe.matmul(bank[:, k:k + 1], macc[:, k * P:(k + 1) * P], ones[:, 0:1],
                                      start=True, stop=True)
            elif kind == "cg":
                pe.wait_ge(s_wg, 2 * l + 2)
                tok = slice(name[2] * P, (name[2] + 1) * P)
                for k in range(KT):
                    for q, (a, w) in enumerate(((hhi, wghi), (hhi, wglo), (hlo, wghi))):
                        m = pe.matmul(bank[:, 0:RANK], a[:, k, tok], w[:, k, :],
                                      start=(k == 0 and q == 0), stop=(k == KT - 1 and q == 2))
            elif kind == "gl":
                pe.wait_ge(*copied(("cg", l)))
                for tb in range(TB):
                    m = pe.matmul(bank[:, tb * G_KW:(tb + 1) * G_KW], cgT[:, tb * P:(tb + 1) * P], gup[:],
                                  start=True, stop=True)
            elif kind == "dz":
                if name[2] == 0:
                    pe.wait_ge(s_la, l + 1)
                for pair in range(2):
                    for tb in range(TB):
                        col = pair * SEQ + tb * P
                        t = name[2] + 1 if name[2] else tb
                        m = pe.matmul(bank[:, col:col + P], la[:, tb, pair * P:(pair + 1) * P], sums[:, t, :],
                                      start=True, stop=True)
            elif kind == "sc":
                _, _, i, odd = name
                rows = slice(odd * G_DK, (odd + 1) * G_DK)
                if i < 0:
                    pe.wait_ge(*copied(("gq", l)))
                    pe.wait_ge(*copied(("gk", l)))
                    key, query = gkT, gqT
                else:
                    pe.wait_ge(s_gx, len(LEVELS) * l + i + 1)
                    key = query = zt[:, i % 2, :]
                for pair in range(2):
                    if i == 0:
                        m = pe.matmul(bank[:, pair * P:(pair + 1) * P], key[rows, pair * SEQ:pair * SEQ + P],
                                      query[rows, pair * SEQ + P:(pair + 1) * SEQ], start=True, stop=True)
                    else:
                        for tb in range(TB):
                            tok = slice(pair * SEQ + tb * P, pair * SEQ + (tb + 1) * P)
                            k = TB * pair + tb
                            m = pe.matmul(bank[:, k * P:(k + 1) * P], key[rows, tok], query[rows, tok],
                                          start=True, stop=True)
            elif kind == "go":
                tb = name[2]
                if tb == 0:
                    pe.wait_ge(*unit_read(("sc", l, len(LEVELS) - 1, 0)))
                    pe.wait_ge(*unit_read(("sc", l, len(LEVELS) - 1, 1)))
                for h in range(G_HEADS):
                    out = bank[:, h * G_DV:(h + 1) * G_DV]
                    if tb:
                        pe.matmul(out, stx[:, h, :], gv[:, 0, h * G_DV:(h + 1) * G_DV], start=True, stop=False)
                    m = pe.matmul(out, st[:, h % 2, TB * (h // 2) + tb, :], gv[:, tb, h * G_DV:(h + 1) * G_DV],
                                  start=(tb == 0), stop=True)
            elif kind == "s":
                _, _, grp, u = name
                if u == 0:
                    if grp == 0:
                        pe.wait_ge(*copied(("ak", l)))
                    for k in range(2):
                        pe.wait_ge(*copied(("aq", l, grp // 2, k)))
                rows = slice((grp % 2) * A_HD, (grp % 2 + 1) * A_HD)
                w, tb = (P, 0) if u == 0 else (SEQ, 1)
                for b in range(CW // w):
                    h = 4 * (grp // 2) + b + max(0, 2 * (u - 1))
                    m = pe.matmul(bank[:, b * w:(b + 1) * w], qT[rows, h, tb * P:(tb + 1) * P],
                                  kT[rows, grp // 2, 0:w], start=True, stop=True)
            elif kind == "o":
                grp = name[2]
                for u in (1, 2):
                    pe.wait_ge(*copied(("p", l, grp, u)))
                for tb in range(TB):
                    for h in range(A_PER):
                        for s in range(tb + 1):
                            u, col = (0, h) if tb == 0 else (1 + h // 2, 2 * (h % 2) + s)
                            at_h = tb * A_KVW + h * A_HD
                            m = pe.matmul(bank[:, at_h:at_h + A_HD], scr[:, 3 + u, col * P:(col + 1) * P],
                                          av[:, s, grp * A_HD:(grp + 1) * A_HD], start=(s == 0), stop=(s == tb))
            else:
                tb = name[2]
                pe.wait_ge(s_vn, l + 1)
                pe.wait_ge(s_sgw, l + 1)
                for g in range(S_G):
                    m = pe.matmul(bank[:, g * S_GD:(g + 1) * S_GD], sgw[:, g, :], zt[:, tb, g * S_GD:(g + 1) * S_GD],
                                  start=True, stop=True)
            m.then_inc(s_sfull, 1)

        for l, r in STEPS1:
            for name in fills1(l, r):
                fill(name)
            for name in units1(l, r):
                unit(name)
            if r < 0:
                continue
            c, g = divmod(r, GPC)
            gc = NCH1 * l + c
            if c == 0:
                pe.wait_ge(s_h, GPC * l + g + 1)
            if r >= R_OUT and c == len(CHUNKS1):
                pe.wait_ge(*copied(("y", l, g)))
            if g == 0:
                need(pe, (s_acc[gc % 2], gc // 2))
            n = GRAN1 * l + r
            pe.wait_ge(s_lo, n + 1)
            for k in range(GK):
                kt = (y_tile(g) if c >= len(CHUNKS1) else GK * g) + k
                for tb in range(TB):
                    tile = slice(tb * P, (tb + 1) * P)
                    for q, (a, b) in enumerate(((hhi, whi), (hhi, wlo), (hlo, whi))):
                        m = pe.matmul(acc[gc % 2][:, tb, :], a[:, kt, tile], b[:, n % SLOTS, k * CW:(k + 1) * CW],
                                      start=(g == 0 and k == 0 and q == 0),
                                      stop=(g == GPC - 1 and k == GK - 1 and q == 2))
            m.then_inc(s_used, 1)


def y_tile(i):
    return (CW // P) * Z_ORDER[i // 2] + GK * (i % 2)


def first_constants():
    half = ROT // 2
    inv = np.float32(500000.0) ** (-(np.arange(half, dtype=np.float32) * np.float32(2.0 / ROT)))
    s, t = np.arange(P)[:, None], np.arange(P)[None, :]
    sums = [s > t, s <= t]
    masks = [s == t]
    for m in LEVELS[1:]:
        upper = (t // m) % 2 == 1
        mid = t // m * m
        after = (t // (2 * m)) * 2 * m + m
        sums.append(np.where(upper, (s >= mid) & (s <= t), (s > t) & (s < after)))
        masks.append((s // (2 * m) == t // (2 * m)) & upper & ((s // m) % 2 == 0))
    return {
        "inv_freq": inv.astype(np.float32),
        "sums": np.stack(sums, axis=1).astype(np.float32),
        "lmask": np.stack(masks, axis=1).astype(np.float32),
        "mask_w": band(lambda d: np.where((d >= 0) & (d < WINDOW), 0.0, NEG)),
    }


def first_stream(w_in, w_out):
    out = []
    for l in range(DEPTH):
        for _, start in CHUNKS1:
            out.append(columns(w_in[l], start))
        for j in range(NCW):
            tiles = columns(w_out[l], CW * j)
            out.append(tiles[[y_tile(i) // GK for i in range(GPC)]])
    return np.concatenate(out)


def by_partition(a):
    return np.ascontiguousarray(np.swapaxes(a.reshape(*a.shape[:-1], KT, P), -1, -2))


def first_arrays(x, c, positions, w_mod, b_mod, g_pre, g_post, w_in, w_out, swa_sinks, sg_w, sg_b, sg_ln_g,
                 sg_ln_b, gla_w_gate_up, gla_b_gate, gla_norm_g):
    halves = D // MOD_W
    return {
        "x": np.ascontiguousarray(x[0]),
        "c": by_partition(c[0]),
        "positions": np.ascontiguousarray(positions.reshape(TB, P).T),
        "w_mod": np.ascontiguousarray(w_mod.reshape(DEPTH, KT, P, 3, halves, MOD_W).transpose(0, 3, 1, 4, 2, 5))
        .reshape(DEPTH, 3, MOD_N, P, MOD_W),
        "b_mod": b_mod.reshape(DEPTH, 3, D),
        "g_pre": by_partition(g_pre),
        "g_post": g_post,
        "w1": first_stream(w_in, w_out),
        "wg": np.ascontiguousarray(w_in[:, :, OFF_GATE:OFF_GATE + RANK].reshape(DEPTH, KT, P, RANK)
                                   .transpose(0, 2, 1, 3)),
        "gate_up": gla_w_gate_up,
        "b_gate": gla_b_gate,
        "gnorm": gla_norm_g,
        "sinks": swa_sinks,
        "sg_w": np.ascontiguousarray(sg_w.transpose(0, 3, 1, 2)),
        "sg_b": np.ascontiguousarray(sg_b.transpose(0, 2, 1)),
        "sg_ln_g": sg_ln_g,
        "sg_ln_b": sg_ln_b,
        **first_constants(),
    }


def second_arrays(w_in, b_forget, b_gate, w_up_a, w_up_b, w_out, ln_g, ln_b):
    f = 8 * W2
    return {
        "w": second_stream(w_in, w_up_a, w_up_b, w_out),
        "wf": np.ascontiguousarray(w_in[:, :, f:f + NH2].reshape(DEPTH, KT, P, NH2).transpose(0, 2, 1, 3)),
        "bf": b_forget, "bg": b_gate.reshape(DEPTH * 2 * NCW, CW), "ln_g": ln_g, "ln_b": ln_b,
        **constants(),
    }


def program(nc, dram):
    with ExitStack() as ctx:
        def sb(name, shape, dt=F32):
            return ctx.enter_context(nc.sbuf_tensor(name, shape, dt))

        x = sb("x", [P, TB, D])
        rings = (sb("raw", [P, SLOTS, GK * CW]), sb("whi", [P, SLOTS, GK * CW], F32R),
                 sb("wlo", [P, SLOTS, GK * CW], F32R))
        acc = [ctx.enter_context(nc.psum_tensor(f"acc{i}", [P, TB, CW], F32)) for i in range(2)]
        psT = [ctx.enter_context(nc.psum_tensor(f"psT{i}", [P, CW], F32)) for i in range(2)]
        psS = [ctx.enter_context(nc.psum_tensor(f"psS{i}", [P, CW], F32)) for i in range(2)]
        with ExitStack() as first:
            first_block(nc, first, x, rings, (acc, psT, psS), dram)
        with ExitStack() as second:
            second_block(nc, second, x, rings, (acc, psT, psS), dram)


def kernel(x, c, positions, w_mod, b_mod, g_pre, g_post, w_in, w_out, swa_sinks, sg_w, sg_b, sg_ln_g, sg_ln_b,
           gla_w_gate_up, gla_b_gate, gla_norm_g, w_in_2, b_forget_2, b_gate_2, w_up_a_2, w_up_b_2, w_out_2,
           ln_g_2, ln_b_2):
    import concourse.bacc as bacc
    from concourse.bass_utils import run_bass_kernel_spmd

    nc = bacc.Bacc("TRN2", target_bir_lowering=False, num_devices=1)
    arrays = {
        **first_arrays(x, c, positions, w_mod, b_mod, g_pre, g_post, w_in, w_out, swa_sinks, sg_w, sg_b, sg_ln_g,
                       sg_ln_b, gla_w_gate_up, gla_b_gate, gla_norm_g),
        **second_arrays(w_in_2, b_forget_2, b_gate_2, w_up_a_2, w_up_b_2, w_out_2, ln_g_2, ln_b_2),
    }
    dram = {name: nc.dram_tensor(f"in_{name}", a.shape, mybir.dt.from_np(a.dtype), kind="ExternalInput").ap()
            for name, a in arrays.items()}
    dram["out"] = nc.dram_tensor("out_x", (SEQ, D), F32, kind="ExternalOutput").ap()
    program(nc, dram)
    r = run_bass_kernel_spmd(nc, [{f"in_{name}": a for name, a in arrays.items()}], core_ids=[0])
    return r.results[0]["out_x"].reshape(1, SEQ, D)
```

```python
from contextlib import ExitStack

import numpy as np

import concourse.bass as bass
from concourse import mybir

F32 = mybir.dt.float32
F32R = mybir.dt.float32r
U32 = mybir.dt.uint32
I32 = mybir.dt.int32
ACT = mybir.ActivationFunctionType
ALU = mybir.AluOpType
AX = mybir.AxisListType

P = 128
SEQ = 256
TB = SEQ // P
D = 2048
KT = D // P
CW = 512
NCW = D // CW
GK = 2
SLOTS = 4
NEG = -1.0e30
DEPTH = 2

HD = 128
NH2 = 12
W2 = NH2 * HD
HPG = CW // HD
NGRP = 2 * NH2 // HPG
KT_UP = W2 // P
ALPHA = float((2 * DEPTH) ** 0.25)
SCALE2 = float(HD) ** -0.5
LN_EPS = 1e-5


def at(layer, per_layer, count):
    return layer * per_layer + count


def second_plan():
    chunks = []
    for half in range(2):
        for grp in range(3):
            chunks += [(kind, 3 * half + grp) for kind in "qkvz"]
        chunks += [("g", NCW * half + j) for j in range(NCW)]
        chunks += [("u", NCW * half + j) for j in range(NCW)]
    chunks += [("o", j) for j in range(NCW)]
    first, n = [], 0
    for kind, _ in chunks:
        first.append(n)
        n += (KT_UP if kind == "u" else KT) // GK
    return chunks, first, n


CHUNKS2, FIRST2, GRAN2 = second_plan()


def granules2(c):
    return (FIRST2 + [GRAN2])[c + 1] - FIRST2[c]


def group_step(c, g):
    found = []
    for q in range(len(CHUNKS2)):
        if CHUNKS2[q][0] == "q" and q <= c:
            r = FIRST2[c] + g - FIRST2[q]
            if r < 48:
                found.append((CHUNKS2[q][1], r))
    return found


F_CHUNK = [i for i, k in enumerate(CHUNKS2) if k == ("g", 1)][0]


def fills2(c, g):
    out = []
    if c == 0:
        out += [("x", 0), ("x", 1)] if g == 0 else [("x", g + 1)] if g < KT // 2 - 1 else []
    for grp, r in group_step(c, g):
        out += {12: [("q", grp, 0), ("q", grp, 1)], 20: [("k", grp, 0), ("k", grp, 1)], 28: [("p", grp, 0)],
                29: [("p", grp, 1)], 30: [("p", grp, 2)], 38: [("a", grp, 0)], 39: [("a", grp, 1)]}.get(r, [])
    if (c, g) == (F_CHUNK, 4):
        out += [("f", 0), ("f", 1)]
    if c and CHUNKS2[c - 1][0] == "u" and CHUNKS2[c - 1][1] >= NCW and g == 3:
        j = CHUNKS2[c - 1][1] - NCW
        out += [("y", 2 * j), ("y", 2 * j + 1)]
    return out


def units2(c, g):
    out = []
    for grp, r in group_step(c, g):
        out += {23: [("s", grp, 0)], 24: [("s", grp, 1)], 25: [("s", grp, 2)],
                33: [("o", grp, 0)], 34: [("o", grp, 1)]}.get(r, [])
    if (c, g) == (F_CHUNK, 0):
        out += [("f", 0), ("f", 1)]
    return out


def numbered(what):
    names = [n for c in range(len(CHUNKS2)) for g in range(granules2(c)) for n in what(c, g)]
    return {name: i for i, name in enumerate(names)}


FILL2 = numbered(fills2)
UNIT2 = numbered(units2)
NF2, NU2 = len(FILL2), len(UNIT2)
assert NF2 % 2 == 0 and NU2 % 2 == 0
SPLIT2 = {name: i for i, name in enumerate([n for n in FILL2 if n[0] in "xay"])}
VLINKS2 = 45


def second_block(nc, ctx, x, rings, ps, dram, s_w):
    raw, whi, wlo = rings
    acc, psT, psS = ps

    def sb(name, shape, dt=F32):
        return ctx.enter_context(nc.sbuf_tensor(name, shape, dt))

    def sem(name):
        return ctx.enter_context(nc.semaphore(name))

    xhi = sb("xhi", [P, KT, SEQ], F32R)
    xlo = sb("xlo", [P, KT, SEQ], F32R)
    ahi = sb("ahi", [P, KT_UP, SEQ], F32R)
    alo = sb("alo", [P, KT_UP, SEQ], F32R)
    y = sb("y", [P, TB, D])
    gb = sb("gb", [P, TB, D])
    stage = sb("stage", [P, TB, CW])
    qT = sb("qT", [P, HPG, SEQ])
    kT = sb("kT", [P, HPG, SEQ])
    v = sb("v", [P, TB, CW])
    z = sb("z", [P, TB, CW])
    prob = sb("prob", [P, 3, CW])
    probT = sb("probT", [P, 3, CW])
    rtmp = sb("rtmp", [P, CW])
    ident = sb("ident", [P, P])
    mask_a = sb("mask_a", [P, P + SEQ])
    mask_b = sb("mask_b", [P, P + SEQ])
    tables = sb("tables", [P, 2, 3, TB, HD // 2])
    gate_row = sb("gate_row", [P, 2, CW])
    wf = sb("wf", [P, KT, NH2])
    wfhi = sb("wfhi", [P, KT, NH2], F32R)
    wflo = sb("wflo", [P, KT, NH2], F32R)
    bf = sb("bf", [P, NH2])
    fb = sb("fb", [P, TB, NH2])
    fl = sb("fl", [NH2, SEQ])
    fe = sb("fe", [NH2, SEQ])
    ncum = sb("ncum", [NH2, SEQ])
    ones = sb("ones", [P, SEQ])
    mx = sb("mx", [P, 3, HPG])
    den = sb("den", [P, TB, HPG])
    rden = sb("rden", [P, TB, HPG])
    stats = sb("stats", [P, TB, NCW, 6])
    mv = sb("mv", [P, TB, 2])
    std = sb("std", [P, TB])
    rstd = sb("rstd", [P, TB])
    nmr = sb("nmr", [P, TB])
    eps = sb("eps", [P, 1])

    s_hi = sem("c_hi")
    s_lo = sem("c_lo")
    s_used = sem("c_used")
    s_acc = [sem(f"c_acc{i}") for i in range(2)]
    s_tfull = sem("c_tfull")
    s_thi = sem("c_thi")
    s_tfree = [sem(f"c_tfree{i}") for i in range(2)]
    s_sfull = sem("c_sfull")
    s_sfree = [sem(f"c_sfree{i}") for i in range(2)]
    s_const = sem("c_const")
    s_mem = sem("c_mem")
    s_rope = sem("c_rope")
    s_max = sem("c_max")
    s_exp = sem("c_exp")
    s_att = sem("c_att")
    s_gate = sem("c_gate")
    s_grow = [sem(f"c_grow{i}") for i in range(2)]
    s_fw = sem("c_fw")
    s_fwh = sem("c_fwh")
    s_fln = sem("c_fln")
    s_cum = sem("c_cum")
    s_y = sem("c_y")
    s_lnp = sem("c_lnp")
    s_var = sem("c_var")
    s_std = sem("c_std")
    s_xn = sem("c_xn")
    s_xnp = sem("c_xnp")
    s_rstd = sem("c_rstd")
    s_xs = sem("c_xs")
    s_pool = sem("c_pool")
    s_self = sem("c_self")
    s_out = sem("c_out")

    block = ctx.enter_context(nc.Block())
    nch = len(CHUNKS2)

    def group_chunk(grp):
        return CHUNKS2.index(("q", grp))

    def dst_of(name):
        if name[0] == "a":
            return ahi, alo, HPG * (name[1] % 3) + 2 * name[2]
        return xhi, xlo, 2 * name[1]

    def multiplied(l, c):
        return s_used, at(l, GRAN2, SLOTS + FIRST2[c] + granules2(c))

    def acc_read(l, c):
        return s_acc[c % 2], at(l, nch // 2, c // 2 + 2)

    def unit_read(l, name):
        return s_sfree[UNIT2[name] % 2], at(l, NU2 // 2, UNIT2[name] // 2 + 2)

    def unit_full(l, name):
        return s_sfull, at(l, NU2, UNIT2[name] + 1)

    def copied(l, name):
        return s_tfree[FILL2[name] % 2], at(l, NF2 // 2, FILL2[name] // 2 + 2)

    def filled(l, name):
        return s_tfull, at(l, NF2, FILL2[name] + 1)

    def bank_t(name):
        return psT[FILL2[name] % 2]

    @block.sync
    def _(sp):
        with sp.Fori(1, DEPTH * GRAN2 // SLOTS) as i:
            for b in range(SLOTS):
                src = dram["w"][sp.snap(i * SLOTS + b)]
                sp.wait_ge(s_lo, i * SLOTS + b - SLOTS + 1)
                sp.dma_start(raw[:, b, :], src).then_inc(s_w[b], 16)
        for j in range(NCW):
            if j == 0:
                sp.wait_ge(s_xn, DEPTH + 1)
            else:
                sp.wait_ge(s_xnp, DEPTH * (NCW - 1) + j)
            sp.dma_start(dram["out"][:, j * CW:(j + 1) * CW].rearrange("(b p) n -> p b n", p=P),
                         x[:, :, j * CW:(j + 1) * CW]).then_inc(s_out, 16)
        sp.wait_ge(s_out, 16 * NCW)

    @block.gpsimd
    def _(pool):
        for tile, name in ((ident, "ident"), (mask_a, "mask_a"), (mask_b, "mask_b"), (tables, "tables")):
            pool.dma_start(tile[:], dram[name]).then_inc(s_const, 16)
        for l in range(DEPTH):
            pool.dma_start(wf[:], dram["wf"][l]).then_inc(s_fw, 16)
            pool.dma_start(bf[:], dram["bf"][l].partition_broadcast(P)).then_inc(s_fw, 16)
            for j in range(2 * NCW):
                bias = dram["bg"][l * 2 * NCW + j].partition_broadcast(P)
                if j >= 2:
                    pool.wait_ge(*acc_read(l, CHUNKS2.index(("g", j - 2))))
                pool.dma_start(gate_row[:, j % 2, :], bias).then_inc(s_grow[j % 2], 16)
            pool.wait_ge(s_y, at(l, NCW, NCW))
            pool.dma_start(gb[:, 0, :], dram["ln_g"][l].partition_broadcast(P)).then_inc(s_lnp, 16)
            pool.dma_start(gb[:, 1, :], dram["ln_b"][l].partition_broadcast(P)).then_inc(s_lnp, 16)
            pool.wait_ge(s_lnp, at(l, 32, 32))
            for j in range(1, NCW):
                cols = slice(j * CW, (j + 1) * CW)
                pool.wait_ge(s_xs, at(l, NCW - 1, j))
                pool.tensor_tensor(x[:, :, cols], x[:, :, cols], gb[:, 0, cols].unsqueeze(1).broadcast_to([P, TB, CW]),
                                   ALU.mult).then_inc(s_pool, 1)
                pool.wait_ge(s_pool, at(l, NCW - 1, j))
                pool.tensor_tensor(x[:, :, cols], x[:, :, cols], gb[:, 1, cols].unsqueeze(1).broadcast_to([P, TB, CW]),
                                   ALU.add).then_inc(s_xnp, 1)

    @block.scalar
    def _(act):
        act.wait_ge(s_mem, 2)

        with act.Fori(0, DEPTH) as l:

            def hi(n):
                act.wait_ge(s_w[n % SLOTS], at(l, 16 * GRAN2 // SLOTS, 16 * (n // SLOTS + 1)))
                act.wait_ge(s_used, at(l, GRAN2, n + 1))
                act.activation(whi[:, n % SLOTS, :], raw[:, n % SLOTS, :], ACT.Copy).then_inc(s_hi, 1)

            def fill_hi(name):
                h, _, k = dst_of(name)
                act.wait_ge(*filled(l, name))
                act.activation(h[:, k:k + 2, :], bank_t(name)[:].rearrange("p (k t) -> p k t", k=2),
                               ACT.Copy).then_inc(s_thi, 1)

            def fill_copy(name, dst):
                act.wait_ge(*filled(l, name))
                act.activation(dst, bank_t(name)[:], ACT.Copy).then_inc(s_tfree[FILL2[name] % 2], 1)

            def evacuate(c, dst, func, scale=1.0):
                act.wait_ge(*multiplied(l, c))
                act.activation(dst[:], acc[c % 2][:], func, scale=scale).then_inc(s_acc[c % 2], 1)

            def attention(grp, r):
                c0 = group_chunk(grp)
                if grp >= 3 and r == 12:
                    evacuate(c0, stage, ACT.Copy, SCALE2)
                if grp >= 3 and r == 20:
                    act.wait_ge(*filled(l, ("q", grp, 1)))
                    evacuate(c0 + 1, stage, ACT.Copy)
                if r in (15, 16):
                    i = r - 15
                    fill_copy(("q", grp, i), qT[:, 2 * i:2 * i + 2, :].rearrange("p h t -> p (h t)"))
                if r in (23, 24):
                    i = r - 23
                    fill_copy(("k", grp, i), kT[:, 2 * i:2 * i + 2, :].rearrange("p h t -> p (h t)"))
                if r in (28, 29, 30):
                    u = r - 28
                    act.wait_ge(s_max, at(l, 3 * NGRP, 3 * grp + u + 1))
                    w = P if u == 0 else SEQ
                    for i in range(CW // w):
                        h = i + max(0, 2 * (u - 1))
                        p = act.activation(prob[:, u, i * w:(i + 1) * w], prob[:, u, i * w:(i + 1) * w], ACT.Exp,
                                           bias=mx[:, u, i:i + 1], accum_out=den[:, min(u, 1), h:h + 1])
                    p.then_inc(s_exp, 1)
                if r == 31:
                    evacuate(c0 + 2, v, ACT.Copy)
                if r in (32, 33, 34):
                    fill_copy(("p", grp, r - 32), probT[:, r - 32, :])
                if r == 36:
                    evacuate(c0 + 3, z, ACT.Silu)
                if r in (42, 43):
                    fill_hi(("a", grp, r - 42))

            for c in range(nch):
                prev, j = CHUNKS2[c - 1] if c else (None, None)
                for g in range(granules2(c)):
                    if c == 0:
                        fill_hi(("x", g))
                    hi(FIRST2[c] + g)
                    if (c, g) == (F_CHUNK - 1, 0):
                        act.wait_ge(s_fw, at(l, 32, 32))
                        act.activation(wfhi[:], wf[:], ACT.Copy).then_inc(s_fwh, 1)
                    for grp, r in group_step(c, g):
                        attention(grp, r)
                    if prev == "g" and g == 4:
                        act.wait_ge(*acc_read(l, c - 1))
                        t = (y if j < NCW else gb)[:, :, (j % NCW) * CW:(j % NCW + 1) * CW]
                        act.activation(t, t, ACT.Sigmoid).then_inc(s_gate, 1)
                    if prev == "u" and j >= NCW and g == 5:
                        fill_hi(("y", 2 * (j - NCW)))
                        fill_hi(("y", 2 * (j - NCW) + 1))
                    if (c, g) == (F_CHUNK, 7):
                        for tb in range(TB):
                            act.wait_ge(*copied(l, ("f", tb)))
                        act.activation(fe[:], fe[:], ACT.Exp).then_inc(s_fln, 1)
                        act.wait_ge(s_fln, at(l, 2, 1))
                        act.activation(fe[:], fe[:], ACT.Ln, bias=1.0).then_inc(s_fln, 1)
            act.wait_ge(s_var, l + 1)
            act.activation(std[:], mv[:, :, 1], ACT.Sqrt, bias=eps[:, 0:1]).then_inc(s_std, 1)
            act.wait_ge(s_rstd, l + 1)
            for j in range(1, NCW):
                for tb in range(TB):
                    last = act.activation(x[:, tb, j * CW:(j + 1) * CW], x[:, tb, j * CW:(j + 1) * CW], ACT.Identity,
                                          scale=rstd[:, tb:tb + 1], bias=nmr[:, tb:tb + 1])
                last.then_inc(s_xs, 1)

    @block.vector
    def _(dve):
        dve.memset(ones[:], 1.0).then_inc(s_mem, 1)
        dve.memset(eps[:], LN_EPS).then_inc(s_mem, 1)
        for i, (s, credit) in enumerate(((s_used, SLOTS), (s_acc[0], 1), (s_acc[1], 1), (s_tfree[0], 1), (s_tfree[1], 1),
                          (s_sfree[0], 1), (s_sfree[1], 1), (s_xn, 1), (s_xnp, NCW - 1))):
            dve.memset(rtmp[:, i:i + 1], 0.0).then_inc(s, credit)
        dve.wait_ge(s_const, 64)
        dve.wait_ge(s_mem, 2)
        links = [0]

        with dve.Fori(0, DEPTH) as l:

            def link(ins):
                links[0] += 1
                ins.then_inc(s_self, 1)
                dve.wait_ge(s_self, at(l, VLINKS2, links[0]))

            def lo(n):
                dve.wait_ge(s_hi, at(l, GRAN2, n + 1))
                dve.tensor_tensor(wlo[:, n % SLOTS, :], raw[:, n % SLOTS, :], whi[:, n % SLOTS, :].bitcast(F32),
                                  ALU.subtract).then_inc(s_lo, 1)

            def fill_lo(name):
                h, w, k = dst_of(name)
                dve.wait_ge(s_thi, at(l, len(SPLIT2), SPLIT2[name] + 1))
                dve.tensor_tensor(w[:, k:k + 2, :], bank_t(name)[:].rearrange("p (k t) -> p k t", k=2),
                                  h[:, k:k + 2, :].bitcast(F32), ALU.subtract)\
                    .then_inc(s_tfree[FILL2[name] % 2], 1)

            def rope(c, which, tb):
                if tb == 0:
                    dve.wait_ge(*multiplied(l, c))
                    if which:
                        dve.wait_ge(*filled(l, ("q", CHUNKS2[c][1], 1)))
                half = HD // 2
                src = acc[c % 2][:, tb, :].rearrange("p (h s e) -> p h s e", s=2, e=half)
                tmp = rtmp[:].rearrange("p (h s e) -> p h s e", s=2, e=half)
                cos, sin, nsin = (tables[:, which, i, tb, :].unsqueeze(1) for i in range(3))
                dve.tensor_tensor(stage[:, tb, :].rearrange("p (h e) -> p h e", e=half),
                                  acc[c % 2][:, tb, :].rearrange("p (h e) -> p h e", e=half),
                                  cos.broadcast_to([P, 2 * HPG, half]), ALU.mult)
                dve.tensor_tensor(tmp[:, :, 0, :], src[:, :, 1, :], nsin.broadcast_to([P, HPG, half]), ALU.mult)
                last = dve.tensor_tensor(tmp[:, :, 1, :], src[:, :, 0, :], sin.broadcast_to([P, HPG, half]),
                                         ALU.mult)
                if tb == 0:
                    link(last)
                else:
                    last.then_inc(s_acc[c % 2], 1)
                    dve.wait_ge(*acc_read(l, c))
                last = dve.tensor_tensor(stage[:, tb, :], stage[:, tb, :], rtmp[:], ALU.add)
                if tb == 0:
                    link(last)
                else:
                    last.then_inc(s_rope, 1)

            def attention(grp, r):
                c0 = group_chunk(grp)
                if grp < 3 and r in (12, 13):
                    rope(c0, 0, r - 12)
                if grp < 3 and r in (20, 21):
                    rope(c0 + 1, 1, r - 20)
                if r in (27, 28, 29):
                    u = r - 27
                    name = ("s", grp, u)
                    bank = UNIT2[name] % 2
                    m = mask_a if grp < 3 else mask_b
                    n, w, m = (HPG, P, m[:, 0:P]) if u == 0 else (2, SEQ, m[:, P:P + SEQ])
                    dve.wait_ge(*unit_full(l, name))
                    p = prob[:, u, :].rearrange("p (h s) -> p h s", s=w)
                    dve.tensor_tensor(p, psS[bank][:].rearrange("p (h s) -> p h s", s=w),
                                      m.unsqueeze(1).broadcast_to([P, n, w]), ALU.add).then_inc(s_sfree[bank], 1)
                    dve.wait_ge(*unit_read(l, name))
                    link(dve.tensor_reduce(mx[:, u, 0:n], p, AX.X, ALU.max))
                    dve.tensor_scalar(mx[:, u, 0:n], mx[:, u, 0:n], -1.0, None, ALU.mult).then_inc(s_max, 1)
                if r == 36:
                    dve.wait_ge(s_exp, at(l, 3 * NGRP, 3 * grp + 3))
                    link(dve.reciprocal(rden[:], den[:]))
                if r in (37, 38):
                    tb = r - 37
                    name = ("o", grp, tb)
                    bank = UNIT2[name] % 2
                    dve.wait_ge(*unit_full(l, name))
                    if tb == 0:
                        dve.wait_ge(*acc_read(l, c0 + 3))
                    else:
                        dve.wait_ge(s_att, at(l, TB * NGRP, TB * grp + 1))
                    t = rtmp[:].rearrange("p (h e) -> p h e", e=HD)
                    dve.tensor_tensor(t, psS[bank][:].rearrange("p (h e) -> p h e", e=HD),
                                      rden[:, tb, :].unsqueeze(2).broadcast_to([P, HPG, HD]), ALU.mult)\
                        .then_inc(s_sfree[bank], 1)
                    dve.wait_ge(*unit_read(l, name))
                    dve.tensor_tensor(z[:, tb, :], z[:, tb, :], rtmp[:], ALU.mult).then_inc(s_att, 1)

            def gate_logits(c):
                j = CHUNKS2[c][1]
                dve.wait_ge(*multiplied(l, c))
                dve.wait_ge(s_grow[j % 2], at(l, 16 * NCW, 16 * (j // 2 + 1)))
                t = (y if j < NCW else gb)[:, :, (j % NCW) * CW:(j % NCW + 1) * CW]
                dve.tensor_tensor(t, acc[c % 2][:], gate_row[:, j % 2, :].unsqueeze(1).broadcast_to([P, TB, CW]),
                                  ALU.add).then_inc(s_acc[c % 2], 1)

            def gated(c):
                j = CHUNKS2[c][1]
                cols = slice((j % NCW) * CW, (j % NCW + 1) * CW)
                dve.wait_ge(*multiplied(l, c))
                dve.wait_ge(s_gate, at(l, 2 * NCW, j + 1))
                t = (y if j < NCW else gb)[:, :, cols]
                dve.tensor_tensor(t, t, acc[c % 2][:], ALU.mult).then_inc(s_acc[c % 2], 1)
                if j >= NCW:
                    dve.wait_ge(*acc_read(l, c))
                    dve.tensor_tensor(y[:, :, cols], y[:, :, cols], t, ALU.add).then_inc(s_y, 1)

            def residual(c):
                j = CHUNKS2[c][1]
                cols = slice(j * CW, (j + 1) * CW)
                dve.wait_ge(*multiplied(l, c))
                dve.scalar_tensor_tensor(out=x[:, :, cols], in0=x[:, :, cols], scalar=ALPHA, in1=acc[c % 2][:],
                                         op0=ALU.mult, op1=ALU.add).then_inc(s_acc[c % 2], 1)
                dve.wait_ge(*acc_read(l, c))
                for tb in range(TB):
                    last = dve.bn_stats(stats[:, tb, j, :], x[:, tb, cols])
                link(last)

            for c in range(nch):
                prev, j = CHUNKS2[c - 1] if c else (None, None)
                for g in range(granules2(c)):
                    if c == 0:
                        fill_lo(("x", g))
                    lo(FIRST2[c] + g)
                    if (c, g) == (F_CHUNK - 1, 1):
                        dve.wait_ge(s_fwh, at(l, 2, 1))
                        dve.tensor_tensor(wflo[:], wf[:], wfhi[:].bitcast(F32), ALU.subtract).then_inc(s_fwh, 1)
                    for grp, r in group_step(c, g):
                        attention(grp, r)
                        if r in (42, 43):
                            fill_lo(("a", grp, r - 42))
                    if prev == "g" and g == 3:
                        gate_logits(c - 1)
                    if prev == "u" and g == 3:
                        gated(c - 1)
                    if prev == "o" and g == 3:
                        residual(c - 1)
                    if prev == "u" and j >= NCW and g == 5:
                        fill_lo(("y", 2 * (j - NCW)))
                        fill_lo(("y", 2 * (j - NCW) + 1))
                    if (c, g) == (F_CHUNK, 4):
                        for tb in range(TB):
                            bank = UNIT2["f", tb] % 2
                            dve.wait_ge(*unit_full(l, ("f", tb)))
                            dve.tensor_tensor(fb[:, tb, :], psS[bank][:, 0:NH2], bf[:], ALU.add)\
                                .then_inc(s_sfree[bank], 1)
                    if (c, g) == (F_CHUNK, 6):
                        for tb in range(TB):
                            tok = slice(tb * P, (tb + 1) * P)
                            bank = FILL2["f", tb] % 2
                            dve.wait_ge(*filled(l, ("f", tb)))
                            link(dve.tensor_scalar(fe[:, tok], psT[bank][0:NH2, 0:P], -1.0, None, ALU.mult))
                            dve.tensor_tensor(fe[:, tok], psT[bank][0:NH2, 0:P], fe[:, tok], ALU.min)
                            dve.tensor_scalar(fl[:, tok], psT[bank][0:NH2, 0:P], 0.0, None, ALU.min)\
                                .then_inc(s_tfree[bank], 1)
                    if (c, g) == (F_CHUNK + 1, 1):
                        dve.wait_ge(s_fln, at(l, 2, 2))
                        link(dve.tensor_tensor(fl[:], fe[:], fl[:], ALU.subtract))
                        dve.tensor_tensor_scan(ncum[:], ones[0:NH2, :], fl[:], 0.0, ALU.mult, ALU.add)\
                            .then_inc(s_cum, 1)
            residual(nch - 1)

            dve.wait_ge(s_lnp, at(l, 32, 32))
            dve.memset(rtmp[:, 0:1], 0.0)
            for tb in range(TB):
                last = dve.bn_aggr(mv[:, tb, :], stats[:, tb, :, :])
            last.then_inc(s_var, 1)
            dve.wait_ge(s_std, l + 1)
            link(dve.reciprocal(rstd[:], std[:]))
            dve.scalar_tensor_tensor(out=nmr[:], in0=mv[:, :, 0], scalar=-1.0, in1=rstd[:], op0=ALU.mult, op1=ALU.mult)\
                .then_inc(s_rstd, 1)
            dve.wait_ge(s_rstd, l + 1)
            cols = slice(0, CW)
            for tb in range(TB):
                last = dve.scalar_tensor_tensor(out=x[:, tb, cols], in0=x[:, tb, cols], scalar=mv[:, tb, 0:1],
                                                in1=gb[:, 0, cols], op0=ALU.subtract, op1=ALU.mult)
            link(last)
            for tb in range(TB):
                last = dve.scalar_tensor_tensor(out=x[:, tb, cols], in0=x[:, tb, cols], scalar=rstd[:, tb:tb + 1],
                                                in1=gb[:, 1, cols], op0=ALU.mult, op1=ALU.add)
            last.then_inc(s_xn, 1)
        assert links[0] == VLINKS2, links

    @block.tensor
    def _(pe):
        pe.wait_ge(s_const, 64)
        pe.wait_ge(s_mem, 2)

        with pe.Fori(0, DEPTH) as l:

            def fill(name):
                i = FILL2[name]
                pe.wait_ge(s_tfree[i % 2], at(l, NF2 // 2, i // 2 + 1))
                kind, bank = name[0], bank_t(name)
                if kind in "xyaqk":
                    if kind == "x":
                        if name[1] == 0:
                            pe.wait_ge(s_xn, l + 1)
                        elif name[1] % 2 == 0:
                            pe.wait_ge(s_xnp, at(l, NCW - 1, name[1] // 2))
                        src, col = x, 2 * P * name[1]
                    elif kind == "y":
                        pe.wait_ge(s_y, at(l, NCW, name[1] // 2 + 1))
                        src, col = y, 2 * P * name[1]
                    elif kind == "a":
                        pe.wait_ge(s_att, at(l, TB * NGRP, TB * (name[1] + 1)))
                        src, col = z, 2 * P * name[2]
                    else:
                        if name[1] < 3:
                            pe.wait_ge(s_rope, at(l, NGRP, 2 * name[1] + 1 + (kind == "k")))
                        else:
                            pe.wait_ge(*acc_read(l, group_chunk(name[1]) + (kind == "k")))
                        src, col = stage, 2 * P * name[2]
                    for k in range(2):
                        for tb in range(TB):
                            t = pe.transpose(bank[:, k * SEQ + tb * P:k * SEQ + (tb + 1) * P],
                                             src[:, tb, col + k * P:col + (k + 1) * P], ident[:])
                elif kind == "p":
                    pe.wait_ge(s_exp, at(l, 3 * NGRP, 3 * name[1] + name[2] + 1))
                    for k in range(4):
                        t = pe.transpose(bank[:, k * P:(k + 1) * P], prob[:, name[2], k * P:(k + 1) * P], ident[:])
                else:
                    pe.wait_ge(*unit_read(l, name))
                    t = pe.transpose(bank[0:NH2, 0:P], fb[:, name[1], :], ident[:])
                t.then_inc(s_tfull, 1)

            def unit(name):
                i = UNIT2[name]
                bank = psS[i % 2]
                pe.wait_ge(s_sfree[i % 2], at(l, NU2 // 2, i // 2 + 1))
                if name[0] == "s":
                    _, grp, u = name
                    if u == 0:
                        for p in range(2):
                            pe.wait_ge(*copied(l, ("k", grp, p)))
                        if grp == 3:
                            pe.wait_ge(s_cum, l + 1)
                    w, tb = (P, 0) if u == 0 else (SEQ, 1)
                    for b in range(CW // w):
                        h = b + max(0, 2 * (u - 1))
                        out = bank[:, b * w:(b + 1) * w]
                        m = pe.matmul(out, qT[:, h, tb * P:(tb + 1) * P], kT[:, h, 0:w], start=True, stop=(grp < 3))
                        if grp >= 3:
                            head = HPG * (grp - 3) + h
                            m = pe.matmul(out, ident[0:NH2, head:head + 1].broadcast_to([NH2, P]), ncum[:, 0:w],
                                          start=False, stop=True)
                elif name[0] == "o":
                    _, grp, tb = name
                    if tb == 0:
                        pe.wait_ge(*acc_read(l, group_chunk(grp) + 2))
                    for p in ((0,), (1, 2))[tb]:
                        pe.wait_ge(*copied(l, ("p", grp, p)))
                    for h in range(HPG):
                        for s in range(tb + 1):
                            u, col = (0, h) if tb == 0 else (1 + h // 2, 2 * (h % 2) + s)
                            m = pe.matmul(bank[:, h * HD:(h + 1) * HD], probT[:, u, col * P:(col + 1) * P],
                                          v[:, s, h * HD:(h + 1) * HD], start=(s == 0), stop=(s == tb))
                else:
                    pe.wait_ge(s_fwh, at(l, 2, 2))
                    tok = slice(name[1] * P, (name[1] + 1) * P)
                    for k in range(KT):
                        for q, (a, w) in enumerate(((xhi, wfhi), (xhi, wflo), (xlo, wfhi))):
                            m = pe.matmul(bank[:, 0:NH2], a[:, k, tok], w[:, k, :],
                                          start=(k == 0 and q == 0), stop=(k == KT - 1 and q == 2))
                m.then_inc(s_sfull, 1)

            for c, (kind, j) in enumerate(CHUNKS2):
                ahead, alow = (ahi, alo) if kind == "u" else (xhi, xlo)
                for g in range(granules2(c)):
                    for name in fills2(c, g):
                        fill(name)
                    for name in units2(c, g):
                        unit(name)
                    if c == 0:
                        pe.wait_ge(*copied(l, ("x", g)))
                    if (kind, j) == ("o", 0):
                        pe.wait_ge(*copied(l, ("y", g)))
                    if kind == "u" and j % NCW == 0 and g == 0:
                        for p in range(2):
                            pe.wait_ge(*copied(l, ("a", 2 + 3 * (j // NCW), p)))
                    if g == 0:
                        pe.wait_ge(s_acc[c % 2], at(l, nch // 2, c // 2 + 1))
                    n = FIRST2[c] + g
                    pe.wait_ge(s_lo, at(l, GRAN2, n + 1))
                    for k in range(GK):
                        for tb in range(TB):
                            tile = slice(tb * P, (tb + 1) * P)
                            kk = GK * g + k
                            for q, (a, b) in enumerate(((ahead, whi), (ahead, wlo), (alow, whi))):
                                m = pe.matmul(acc[c % 2][:, tb, :], a[:, kk, tile],
                                              b[:, n % SLOTS, k * CW:(k + 1) * CW],
                                              start=(kk == 0 and q == 0),
                                              stop=(kk == GK * granules2(c) - 1 and q == 2))
                    m.then_inc(s_used, 1)


def rope_tables():
    half = HD // 2
    inv = (np.float32(10000.0) ** (-np.arange(half, dtype=np.float32) / half)).astype(np.float32)
    ang = (np.arange(SEQ, dtype=np.float32)[:, None] * inv[None, :]).astype(np.float32).astype(np.float64)
    t = np.stack([np.cos(ang), np.sin(ang), -np.sin(ang)])
    t = np.stack([t * SCALE2, t]).reshape(2, 3, TB, P, half).transpose(3, 0, 1, 2, 4)
    return np.ascontiguousarray(t.astype(np.float32))


def band(weight):
    t, s = np.arange(P)[:, None], np.arange(SEQ)[None, :]
    return np.concatenate([weight(t - s[:, :P]), weight(t + P - s)], axis=1).astype(np.float32)


def constants():
    count = lambda d: sum(((d >= 0) & (d <= w) & (d % r == 0)).astype(int) for w, r in
                          ((128, 1), (512, 4), (2048, 16)))
    return {
        "ident": np.eye(P, dtype=np.float32),
        "mask_a": band(lambda d: np.where(count(d) > 0, np.log(np.maximum(count(d), 1)), NEG)),
        "mask_b": band(lambda d: np.where(d >= 0, 0.0, NEG)),
        "tables": rope_tables(),
    }


def columns(w, start):
    k = w.shape[0] // P
    return w[:, start:start + CW].reshape(k // GK, GK, P, CW).transpose(0, 2, 1, 3).reshape(k // GK, P, GK * CW)


def second_stream(w_in, w_up_a, w_up_b, w_out):
    starts = {"q": 0, "k": W2, "v": 2 * W2, "z": 3 * W2}
    out = []
    for l in range(DEPTH):
        for kind, j in CHUNKS2:
            if kind in starts:
                out.append(columns(w_in[l], starts[kind] + (4 * W2) * (j // 3) + CW * (j % 3)))
            elif kind == "g":
                out.append(columns(w_in[l], 8 * W2 + NH2 + CW * j))
            elif kind == "u":
                out.append(columns((w_up_a if j < NCW else w_up_b)[l], CW * (j % NCW)))
            else:
                out.append(columns(w_out[l], CW * j))
    return np.concatenate(out)


A_HEADS = 16
A_HD = 64
A_W = A_HEADS * A_HD
A_KV = 4
A_KVW = A_KV * A_HD
A_PER = A_HEADS // A_KV
WINDOW = 128
ROT = A_HD // 4
S_W = D // 4
S_G = 8
S_GD = S_W // S_G
G_HEADS = 4
G_DV = 128
G_DK = 64
G_KW = G_HEADS * G_DK
RANK = 16
TAU = 16.0
EPS = 1e-6
LEVELS = (128, 64, 32, 16, 8, 4, 2, 1)
MOD_W = 1024
MOD_N = KT * D // MOD_W
OFF_GATE = A_W + 2 * A_KVW + 2 * S_W + 2 * G_KW + G_HEADS * G_DV
OFF_Z = OFF_GATE + RANK
CHUNKS1 = [("gqk", A_W + 2 * A_KVW + 2 * S_W), ("gv", A_W + 2 * A_KVW + 2 * S_W + 2 * G_KW), ("kv", A_W),
           ("q0", 0), ("q1", CW), ("su", A_W + 2 * A_KVW), ("sv", A_W + 2 * A_KVW + S_W),
           ("z3", OFF_Z + 3 * CW), ("z2", OFF_Z + 2 * CW), ("z0", OFF_Z), ("z1", OFF_Z + CW)]
C1 = {name: i for i, (name, _) in enumerate(CHUNKS1)}
Z_ORDER = (3, 2, 0, 1)
GPC = KT // GK
NCH1 = len(CHUNKS1) + NCW
GRAN1 = NCH1 * GPC
R_OUT = len(CHUNKS1) * GPC
R_SWA = (52, 59, 66, 73)
R_MOD = {2: 8, 0: 50, 1: 85}
AHEAD = SLOTS - 1
R_MODG, R_MODS, R_MODA = (41, 42, 45, 46), 81, 116
R_LEVEL = 20


def fills1(l, r):
    if r < 0:
        return [("h", 0, 0), ("h", 0, 1)]
    out = []
    if r < GPC - 1:
        out += [("h", l, r + 1)] if r else [("h", l, 0), ("h", l, 1)] if l else []
    if r == 12:
        out += [("gq", l), ("gk", l)]
    if r == 30:
        out += [("ak", l)]
    if r in (38, 46):
        out += [("aq", l, (r - 38) // 8, 0), ("aq", l, (r - 38) // 8, 1)]
    for grp, b in enumerate(R_SWA):
        if 4 <= r - b <= 6:
            out += [("p", l, grp, r - b - 4)]
    if R_OUT <= r < R_OUT + GPC - 1:
        out += [("y", l, 0), ("y", l, 1)] if r == R_OUT else [("y", l, r - R_OUT + 1)]
    return out


def units1(l, r):
    if r < 0:
        return [("ms", 0), ("ma", 0)]
    out = []
    if r == 8:
        out += [("cg", l)]
    if r == 13:
        out += [("gl", l)]
    if r == 17:
        out += [("sc", l, -1, 0), ("sc", l, -1, 1)]
    for i in range(len(LEVELS)):
        if r == R_LEVEL + 4 * i:
            out += [("dz", l, i)]
        if r == R_LEVEL + 3 + 4 * i:
            out += [("sc", l, i, 0), ("sc", l, i, 1)]
    if r in R_MODG:
        out += [("mg", l, R_MODG.index(r))]
    for grp, b in enumerate(R_SWA):
        if 0 <= r - b <= 2:
            out += [("s", l, grp, r - b)]
        if r - b == 8:
            out += [("o", l, grp)]
    if r in (56, 57):
        out += [("go", l, r - 56)]
    if r in (65, 66):
        out += [("sg", l, r - 65)]
    if l + 1 < DEPTH and r == R_MODS:
        out += [("ms", l + 1)]
    if l + 1 < DEPTH and r == R_MODA:
        out += [("ma", l + 1)]
    return out


STEPS1 = [(0, -1)] + [(l, r) for l in range(DEPTH) for r in range(GRAN1)]
FILL1 = {name: i for i, name in enumerate(n for s in STEPS1 for n in fills1(*s))}
UNIT1 = {name: i for i, name in enumerate(n for s in STEPS1 for n in units1(*s))}
THIRDS = [(0, 0), (0, 1)] + [(0, 2), (1, 0), (1, 1), (1, 2)]


def mod_step(l, r):
    if r >= R_MOD[2] and r < R_MOD[2] + MOD_N:
        return THIRDS.index((l, 2)), r - R_MOD[2]
    for third in (0, 1):
        if l + 1 < DEPTH and R_MOD[third] <= r < R_MOD[third] + MOD_N:
            return THIRDS.index((l + 1, third)), r - R_MOD[third]
    return None


def first_block(nc, ctx, x, rings, ps, dram, s_next=None):
    raw, whi, wlo = rings
    acc, psT, psS = ps

    def sb(name, shape, dt=F32):
        return ctx.enter_context(nc.sbuf_tensor(name, shape, dt))

    def sem(name):
        return ctx.enter_context(nc.semaphore(name))

    hhi = sb("hhi", [P, KT, SEQ], F32R)
    hlo = sb("hlo", [P, KT, SEQ], F32R)
    y = sb("b_y", [P, TB, D])
    macc = sb("macc", [P, D])
    mraw = sb("mraw", [P, 2, MOD_W])
    gain = sb("gain", [P, D])
    stage = sb("b_stage", [P, TB, CW])
    zt = sb("zt", [P, TB, CW])
    scr = sb("scr", [P, 6, CW])
    rt = sb("rt", [P, CW])
    av = sb("av", [P, TB, A_KVW])
    kT = sb("b_kT", [P, A_KV // 2, SEQ])
    qT = sb("b_qT", [P, A_HEADS // 2, SEQ])
    la = sb("la", [P, TB, G_KW])
    st = sb("st", [P, 2, 4, P])
    stx = sb("stx", [P, G_HEADS, P])
    sums = sb("sums", [P, len(LEVELS) + 1, P])
    lmask = sb("lmask", [P, len(LEVELS), P], mybir.dt.uint8)
    wmask = sb("wmask", [P, P + SEQ])
    ident = sb("b_ident", [P, P])
    ones = sb("b_ones", [P, P])
    one = sb("b_one", [P, 1])
    sgw = sb("sgw", [P, S_G, P])
    lnr = sb("lnr", [P, 2, S_W])
    sgb = sb("sgb", [P, S_G])
    gnorm = sb("gnorm", [P, G_DV])
    wg = sb("wg", [P, KT, RANK])
    wghi = sb("wghi", [P, KT, RANK], F32R)
    wglo = sb("wglo", [P, KT, RANK], F32R)
    gup = sb("gup", [RANK, G_KW])
    gbias = sb("gbias", [P, G_KW])
    cgT = sb("cgT", [RANK, SEQ])
    sinks = sb("sinks", [P, A_HEADS])
    cvec = sb("cvec", [P, KT])
    csil = sb("csil", [P, KT])
    gpre = sb("gpre", [P, KT])
    shift = sb("shift", [P, DEPTH, KT])
    scale = sb("scale", [P, DEPTH, KT])
    posi = sb("posi", [P, TB], I32)
    posf = sb("posf", [P, TB])
    invf = sb("invf", [P, ROT // 2])
    ang = sb("ang", [P, 4, TB, ROT // 2])
    cs = sb("cs", [P, 2, TB, ROT // 2])
    mx = sb("b_mx", [P, 3, A_PER])
    snk = sb("snk", [P, TB, A_PER])
    den = sb("b_den", [P, TB, A_PER])
    rden = sb("b_rden", [P, 2, TB, A_PER])
    sq = sb("sq", [P, TB, NCW])
    rms = sb("rms", [P, 2, TB])
    gsq = sb("gsq", [P, 2, TB, G_HEADS])
    stats = sb("b_stats", [P, TB, 6])
    mv = sb("b_mv", [P, TB, 2])
    lstd = sb("lstd", [P, 2, TB])
    eps = sb("b_eps", [P, 1])

    s_w = [sem(f"b_w{i}") for i in range(SLOTS)]
    s_hi = sem("b_hi")
    s_lo = sem("b_lo")
    s_used = sem("b_used")
    s_acc = [sem(f"b_acc{i}") for i in range(2)]
    s_tfull = sem("b_tfull")
    s_thi = sem("b_thi")
    s_tfree = [sem(f"b_tfree{i}") for i in range(2)]
    s_sfull = sem("b_sfull")
    s_sfree = [sem(f"b_sfree{i}") for i in range(2)]
    s_x = sem("b_x")
    s_c = sem("b_c")
    s_ident = sem("b_ident")
    s_gpre = sem("b_gpre")
    s_const = sem("b_const")
    s_late = sem("b_late")
    s_mem = sem("b_mem")
    s_par = sem("b_par")
    s_sgw = sem("b_sgw")
    s_m = [sem(f"b_m{i}") for i in range(6)]
    s_macc = sem("b_macc")
    s_mzero = sem("b_mzero")
    s_mbias = [sem(f"b_mbias{i}") for i in range(2)]
    s_gain = sem("b_gain")
    s_mod = sem("b_mod")
    s_silu = sem("b_silu")
    s_ang = sem("b_ang")
    s_trig = sem("b_trig")
    s_sq = sem("b_sq")
    s_osq = sem("b_osq")
    s_ssum = sem("b_ssum")
    s_rms = sem("b_rms")
    s_xn = sem("b_xn")
    s_h = sem("b_h")
    s_wg = sem("b_wg")
    s_neg = sem("b_neg")
    s_ln = sem("b_ln")
    s_la = sem("b_la")
    s_gx = sem("b_gx")
    s_rope = sem("b_rope")
    s_max = sem("b_max")
    s_exp = sem("b_exp")
    s_y = sem("b_ypart")
    s_gsq = sem("b_gsq")
    s_grms = sem("b_grms")
    s_var = sem("b_var")
    s_std = sem("b_std")
    s_vn = sem("b_vn")
    s_ym = sem("b_ym")
    s_xd = sem("b_xd")
    s_self = sem("b_self")

    block = ctx.enter_context(nc.Block())
    gv = y[:, :, 0:CW]
    gqT, gkT = y[:, 0, CW:2 * CW], y[:, 1, CW:2 * CW]
    ks = scr[:, 5, :].rearrange("p (b n) -> p b n", b=TB)
    junk = scr[:].rearrange("p a n -> p (a n)").bitcast(mybir.dt.bfloat16)

    mod_slots = [mraw[:, 0, :], mraw[:, 1, :]] + [raw[:, i, :] for i in range(SLOTS)]
    early = 2 * MOD_N

    def macc_of(q):
        return qT[:].rearrange("p h t -> p (h t)") if q == 0 else macc[:]

    def mod_place(n):
        return n % len(mod_slots) if n < early else n % 2

    def mod_slot(n):
        k = mod_place(n)
        return mod_slots[k], (k, sum(mod_place(m) == k for m in range(n + 1)))

    def mod_before(n):
        return max((m for m in range(n) if mod_place(m) == mod_place(n)), default=None)

    def need(eng, sv):
        if sv[1] > 0:
            eng.wait_ge(*sv)

    def chunk(l, name):
        return l * NCH1 + (len(CHUNKS1) + name if isinstance(name, int) else C1[name])

    def multiplied(c):
        return s_used, GPC * (c + 1)

    def acc_read(c):
        return s_acc[c % 2], c // 2 + 1

    def unit_full(name):
        return s_sfull, UNIT1[name] + 1

    def unit_read(name):
        return s_sfree[UNIT1[name] % 2], UNIT1[name] // 2 + 1

    def bank_s(name):
        return psS[UNIT1[name] % 2]

    def filled(name):
        return s_tfull, FILL1[name] + 1

    def copied(name):
        return s_tfree[FILL1[name] % 2], FILL1[name] // 2 + 1

    def bank_t(name):
        return psT[FILL1[name] % 2]

    def split_index(name):
        return GPC * (2 * name[1] + (name[0] == "y")) + name[2]

    def exp_index(l, grp, u):
        return 3 * (A_KV * l + grp) + u + 1

    n_par = 9

    @block.sync
    def _(sp):
        def mod(q, i):
            n = MOD_N * q + i
            if mod_before(n) is not None:
                sp.wait_ge(s_macc, mod_before(n) + 1)
            l, third = THIRDS[q]
            slot, use = mod_slot(n)
            sp.dma_start(slot, dram["w_mod"][l, third, i]).then_inc(s_m[use[0]], 16)

        def weights(n):
            if n >= SLOTS:
                sp.wait_ge(s_lo, n - SLOTS + 1)
            else:
                sp.wait_ge(s_macc, max(m for m in range(early) if mod_place(m) == n + 2) + 1)
            sp.dma_start(raw[:, n % SLOTS, :], dram["w1"][n]).then_inc(s_w[n % SLOTS], 16)

        for q in range(2):
            for i in range(MOD_N):
                if (q, i) == (0, len(mod_slots)):
                    sp.dma_start(x[:], dram["x"].rearrange("(b p) n -> p b n", p=P)).then_inc(s_x, 16)
                mod(q, i)
        for n in range(DEPTH * GRAN1):
            step = mod_step(*divmod(n, GRAN1))
            weights(n)
            if step:
                mod(*step)
        for n in range(SLOTS if s_next else 0):
            sp.wait_ge(s_lo, DEPTH * GRAN1 - SLOTS + n + 1)
            sp.dma_start(raw[:, n, :], dram["w"][n]).then_inc(s_next[n], 16)

    @block.gpsimd
    def _(pool):
        def mod_bias(q):
            l, third = THIRDS[q]
            pool.wait_ge(s_mzero, q + 1)
            pool.dma_start(macc_of(q)[0:1, :], dram["b_mod"][l, third:third + 1, :]).then_inc(s_mbias[q % 2], 16)

        pool.dma_start(cvec[:], dram["c"]).then_inc(s_c, 16)
        mod_bias(0)
        mod_bias(1)
        pool.dma_start(ident[:], dram["ident"]).then_inc(s_ident, 16)
        for tile, name in ((posi, "positions"), (zt[:].rearrange("p b (i n) -> p (b i) n", n=P), "lmask")):
            pool.dma_start(tile[:], dram[name]).then_inc(s_const, 16)
        pool.dma_start(invf[:], dram["inv_freq"].partition_broadcast(P)).then_inc(s_const, 16)

        def parameters(l):
            if l:
                pool.wait_ge(s_ym, NCW * l)
            pool.dma_start(gpre[:], dram["g_pre"][l]).then_inc(s_gpre, 16)
            if l == 0:
                pool.wait_ge(s_macc, early)
            pool.dma_start(wg[:], dram["wg"][l]).then_inc(s_par, 16)
            pool.dma_start(gup[:], dram["gate_up"][l]).then_inc(s_par, 16)
            pool.dma_start(gbias[:], dram["b_gate"][l].partition_broadcast(P)).then_inc(s_par, 16)
            pool.dma_start(gnorm[:], dram["gnorm"][l].partition_broadcast(P)).then_inc(s_par, 16)
            pool.dma_start(sinks[:], dram["sinks"][l].partition_broadcast(P)).then_inc(s_par, 16)
            pool.dma_start(sgb[:], dram["sg_b"][l]).then_inc(s_par, 16)
            pool.dma_start(lnr[:, 0, :], dram["sg_ln_g"][l].partition_broadcast(P)).then_inc(s_par, 16)
            pool.dma_start(lnr[:, 1, :], dram["sg_ln_b"][l].partition_broadcast(P)).then_inc(s_par, 16)
            pool.dma_start(sgw[:], dram["sg_w"][l]).then_inc(s_par, 16)
            if l == 0:
                pool.dma_start(sums[:], dram["sums"]).then_inc(s_late, 16)
                pool.dma_start(wmask[:], dram["mask_w"]).then_inc(s_late, 16)
            pool.wait_ge(s_par, 16 * n_par * (l + 1))
            pool.affine_select(out=sgw[:], in_=sgw[:], compare_op=ALU.is_ge, fill=0.0, base=0,
                               pattern=[[0, S_G], [1, P]], channel_multiplier=-1).then_inc(s_sgw, 1)

        parameters(0)
        for l in range(DEPTH):
            if l:
                pool.wait_ge(s_xd, NCW * l)
            pool.dma_start(gain[:], dram["g_post"][l].partition_broadcast(P)).then_inc(s_gain, 16)
            mod_bias(THIRDS.index((l, 2)))
            if l + 1 < DEPTH:
                mod_bias(THIRDS.index((l + 1, 0)))
                mod_bias(THIRDS.index((l + 1, 1)))
                parameters(l + 1)

    @block.scalar
    def _(act):
        act.wait_ge(s_c, 16)
        act.activation(csil[:], cvec[:], ACT.Silu).then_inc(s_silu, 1)

        def hi(n):
            act.wait_ge(s_w[n % SLOTS], 16 * (n // SLOTS + 1))
            if n >= SLOTS:
                act.wait_ge(s_used, n - SLOTS + 1)
            act.activation(whi[:, n % SLOTS, :], raw[:, n % SLOTS, :], ACT.Copy).then_inc(s_hi, 1)

        def fill_copy(name, dst, rows=P, n=CW):
            act.wait_ge(*filled(name))
            act.activation(dst, bank_t(name)[0:rows, 0:n], ACT.Copy).then_inc(s_tfree[FILL1[name] % 2], 1)

        def fill_hi(name):
            if name[0] == "h":
                act.wait_ge(*copied(name))
                src = zt[:, name[2] % 2, :]
            else:
                act.wait_ge(*filled(name))
                src = bank_t(name)[:]
            k = 2 * name[2] if name[0] == "h" else y_tile(name[2])
            act.activation(hhi[:, k:k + 2, :], src.rearrange("p (k t) -> p k t", k=2), ACT.Copy).then_inc(s_thi, 1)

        def squares(src, j, last_inc=None):
            for tb in range(TB):
                k = TB * j + tb
                last = act.activation(junk[:, k * CW:(k + 1) * CW], src[:, tb, :], ACT.Square,
                                      accum_out=sq[:, tb, j:j + 1])
            last.then_inc(last_inc, 1)

        def root(n):
            act.wait_ge(s_ssum, n + 1)
            act.activation(rms[:, 0, :], rms[:, 1, :], ACT.Sqrt, scale=1.0 / D, bias=eps[:, 0:1]).then_inc(s_rms, 1)

        def x_squares(l):
            for j in range(NCW):
                if l:
                    act.wait_ge(s_xd, NCW * (l - 1) + j + 1)
                squares(x[:, :, j * CW:(j + 1) * CW], j, s_sq)

        def out_chunk(l, j):
            c = chunk(l, j)
            act.wait_ge(*multiplied(c))
            for tb in range(TB):
                k = TB * j + tb
                act.activation(junk[:, k * CW:(k + 1) * CW], acc[c % 2][:, tb, :], ACT.Square,
                               accum_out=sq[:, tb, j:j + 1]).then_inc(s_osq, 1)

        act.wait_ge(s_mem, 2)
        act.wait_ge(s_ang, 1)
        act.activation(cs[:].rearrange("p a b n -> p (a b n)"), ang[:, 0:2].rearrange("p a b n -> p (a b n)"),
                       ACT.Sin).then_inc(s_trig, 1)
        act.wait_ge(s_x, 16)
        for l in range(DEPTH):
            x_squares(l)
            root(2 * l)
            for r in range(GRAN1):
                if r < GPC:
                    fill_hi(("h", l, r))
                if R_OUT <= r < R_OUT + GPC:
                    fill_hi(("y", l, r - R_OUT))
                if l == 0 or r >= AHEAD:
                    hi(GRAN1 * l + r)
                if r == 7:
                    act.wait_ge(s_par, 16 * n_par * (l + 1))
                    act.activation(wghi[:], wg[:], ACT.Copy).then_inc(s_wg, 1)
                if r == 11:
                    c = chunk(l, "gqk")
                    act.wait_ge(*multiplied(c))
                    act.activation(stage[:, :, 0:G_KW], acc[c % 2][:, :, 0:G_KW], ACT.Copy, scale=G_DK ** -0.5)
                    act.activation(stage[:, :, G_KW:], acc[c % 2][:, :, G_KW:], ACT.Copy).then_inc(s_acc[c % 2], 1)
                if r == 11:
                    act.wait_ge(*unit_full(("cg", l)))
                    act.activation(cgT[:], bank_s(("cg", l))[0:RANK, 0:SEQ], ACT.Copy)\
                        .then_inc(s_sfree[UNIT1["cg", l] % 2], 1)
                if r == 15:
                    fill_copy(("gq", l), gqT)
                if r == 15:
                    fill_copy(("gk", l), gkT)
                if r == 17:
                    act.wait_ge(s_neg, l + 1)
                    act.activation(zt[:, 0, :], zt[:, 0, :], ACT.Exp).then_inc(s_ln, 1)
                    act.wait_ge(s_ln, 2 * l + 1)
                    act.activation(zt[:, 0, :], zt[:, 0, :], ACT.Ln, bias=1.0).then_inc(s_ln, 1)
                if r == 19:
                    c = chunk(l, "gv")
                    act.wait_ge(*multiplied(c))
                    act.activation(gv, acc[c % 2][:], ACT.Copy).then_inc(s_acc[c % 2], 1)
                for i in range(len(LEVELS)):
                    if r == R_LEVEL + 3 + 4 * i:
                        if i >= 2:
                            act.wait_ge(*unit_full(("sc", l, i - 2, 1)))
                        act.wait_ge(*unit_full(("dz", l, i)))
                        act.activation(zt[:, i % 2, :], bank_s(("dz", l, i))[:], ACT.Exp)\
                            .then_inc(s_sfree[UNIT1["dz", l, i] % 2], 1)
                if r == 27:
                    c = chunk(l, "kv")
                    act.wait_ge(*multiplied(c))
                    act.activation(ks, acc[c % 2][:, :, 0:A_KVW], ACT.Copy)
                    act.activation(av[:], acc[c % 2][:, :, A_KVW:], ACT.Copy).then_inc(s_acc[c % 2], 1)
                if r == 33:
                    fill_copy(("ak", l), kT[:].rearrange("p k t -> p (k t)"))
                if r in (35, 43):
                    c = chunk(l, "q0" if r == 35 else "q1")
                    if r == 43:
                        act.wait_ge(*filled(("aq", l, 0, 1)))
                    act.wait_ge(*multiplied(c))
                    dst = stage[:].rearrange("p b (i s e) -> p b i s e", s=2, e=A_HD)
                    for s in range(2):
                        last = act.activation(dst[:, :, :, s, :], acc[c % 2][:, :, s * A_KVW:(s + 1) * A_KVW]
                                              .rearrange("p b (i e) -> p b i e", e=A_HD), ACT.Copy,
                                              scale=A_HD ** -0.5)
                    last.then_inc(s_acc[c % 2], 1)
                if r in (41, 49):
                    i = (r - 41) // 8
                    for k in range(2):
                        a = 4 * i + 2 * k
                        fill_copy(("aq", l, i, k), qT[:, a:a + 2, :].rearrange("p h t -> p (h t)"))
                for grp, b in enumerate(R_SWA):
                    if 4 <= r - b <= 6:
                        u = r - b - 4
                        act.wait_ge(s_max, exp_index(l, grp, u))
                        w = P if u == 0 else SEQ
                        h0, n = max(0, 2 * (u - 1)), CW // w
                        act.activation(snk[:, min(u, 1), h0:h0 + n], snk[:, min(u, 1), h0:h0 + n], ACT.Exp)
                        for i in range(n):
                            p = act.activation(scr[:, u, i * w:(i + 1) * w], scr[:, u, i * w:(i + 1) * w], ACT.Exp,
                                               bias=mx[:, u, i:i + 1], accum_out=den[:, min(u, 1), h0 + i:h0 + i + 1])
                        p.then_inc(s_exp, 1)
                    if 7 <= r - b <= 9:
                        fill_copy(("p", l, grp, r - b - 7), scr[:, 3 + r - b - 7, :])
                if r == 51:
                    c = chunk(l, "su")
                    act.wait_ge(*multiplied(c))
                    act.activation(y[:, :, 2 * CW:3 * CW], acc[c % 2][:], ACT.Gelu_apprx_tanh)\
                        .then_inc(s_acc[c % 2], 1)
                if r == 59:
                    c = chunk(l, "sv")
                    act.wait_ge(*multiplied(c))
                    act.wait_ge(*unit_full(("sc", l, len(LEVELS) - 1, 1)))
                    act.activation(zt[:], acc[c % 2][:], ACT.Gelu_apprx_tanh).then_inc(s_acc[c % 2], 1)
                if r == 61:
                    act.wait_ge(s_var, l + 1)
                    act.activation(lstd[:, 0, :], mv[:, :, 1], ACT.Sqrt, bias=eps[:, 0:1]).then_inc(s_std, 1)
                if r in (59, 60):
                    tb = r - 59
                    act.wait_ge(*unit_full(("go", l, tb)))
                    act.activation(y[:, tb, 3 * CW:], bank_s(("go", l, tb))[:], ACT.Copy)\
                        .then_inc(s_sfree[UNIT1["go", l, tb] % 2], 1)
                if r == 63:
                    act.wait_ge(s_gsq, l + 1)
                    act.activation(gsq[:, 1], gsq[:, 0], ACT.Sqrt, scale=1.0 / G_DV, bias=eps[:, 0:1])\
                        .then_inc(s_grms, 1)
                if r in (69, 75, 83, 91):
                    i = (69, 75, 83, 91).index(r)
                    c = chunk(l, f"z{Z_ORDER[i]}")
                    act.wait_ge(*multiplied(c))
                    if i == 0:
                        act.wait_ge(*unit_full(("sg", l, 1)))
                    else:
                        act.wait_ge(s_ym, NCW * l + i)
                    act.activation(zt[:], acc[c % 2][:], ACT.Silu).then_inc(s_acc[c % 2], 1)
                if r >= R_OUT + GPC and (r - R_OUT) % GPC == 3:
                    out_chunk(l, (r - R_OUT) // GPC - 1)
            for r in range(AHEAD if l + 1 < DEPTH else 0):
                hi(GRAN1 * (l + 1) + r)
            act.activation(one[:], eps[:, 0:1], ACT.Sqrt)
            out_chunk(l, NCW - 1)
            root(2 * l + 1)

    @block.vector
    def _(dve):
        links = [0]

        def link(ins):
            links[0] += 1
            ins.then_inc(s_self, 1)
            dve.wait_ge(s_self, links[0])

        def lo(n):
            dve.wait_ge(s_hi, n + 1)
            dve.tensor_tensor(wlo[:, n % SLOTS, :], raw[:, n % SLOTS, :], whi[:, n % SLOTS, :].bitcast(F32),
                              ALU.subtract).then_inc(s_lo, 1)

        def fill_lo(name):
            dve.wait_ge(s_thi, split_index(name) + 1)
            if name[0] == "h":
                k, src = 2 * name[2], zt[:, name[2] % 2, :]
                signal = s_h
            else:
                k, src = y_tile(name[2]), bank_t(name)[:]
                signal = s_tfree[FILL1[name] % 2]
            dve.tensor_tensor(hlo[:, k:k + 2, :], src.rearrange("p (k t) -> p k t", k=2),
                              hhi[:, k:k + 2, :].bitcast(F32), ALU.subtract).then_inc(signal, 1)

        def fill_mod(l, i):
            name = ("h", l, i)
            dve.wait_ge(*filled(name))
            if i >= 2:
                dve.wait_ge(s_h, GPC * l + i - 1)
            for k in range(2):
                kt = 2 * i + k
                last = dve.tensor_scalar(zt[:, i % 2, k * SEQ:(k + 1) * SEQ], bank_t(name)[:, k * SEQ:(k + 1) * SEQ],
                                         scale[:, l, kt:kt + 1], shift[:, l, kt:kt + 1], ALU.mult, ALU.add)
            last.then_inc(s_tfree[FILL1[name] % 2], 1)

        def mod_zero(q):
            if q >= 2:
                l, third = THIRDS[q - 1]
                dve.wait_ge(*unit_full(("ms", l) if third == 0 else ("ma", l) if third == 1 else ("mg", l, NCW - 1)))
            dve.memset(macc_of(q), 0.0).then_inc(s_mzero, 1)

        def mod(q, i):
            n = MOD_N * q + i
            half, kt = divmod(i, KT)
            cols = slice(half * MOD_W, (half + 1) * MOD_W)
            if i == 0:
                dve.wait_ge(s_mbias[q % 2], 16 * (q // 2 + 1))
            if kt:
                dve.wait_ge(s_macc, n)
            slot, (k, uses) = mod_slot(n)
            dve.wait_ge(s_m[k], 16 * uses)
            dve.scalar_tensor_tensor(out=macc_of(q)[:, cols], in0=slot, scalar=csil[:, kt:kt + 1],
                                     in1=macc_of(q)[:, cols], op0=ALU.mult, op1=ALU.add).then_inc(s_macc, 1)

        def mod_shift(l):
            dve.wait_ge(*unit_full(("ms", l)))
            dve.tensor_copy(shift[:, l, :], bank_s(("ms", l))[:, 0:KT]).then_inc(s_sfree[UNIT1["ms", l] % 2], 1)

        def mod_scale(l):
            dve.wait_ge(*unit_full(("ma", l)))
            dve.wait_ge(s_gpre, 16 * (l + 1))
            dve.scalar_tensor_tensor(out=scale[:, l, :], in0=bank_s(("ma", l))[:, 0:KT], scalar=1.0, in1=gpre[:],
                                     op0=ALU.add, op1=ALU.mult).then_inc(s_sfree[UNIT1["ma", l] % 2], 1)
            dve.wait_ge(*unit_read(("ma", l)))

        def inverse_root(n):
            dve.wait_ge(s_rms, n + 1)
            link(dve.reciprocal(rms[:, 1, :], rms[:, 0, :]))

        def normalised(l):
            dve.wait_ge(s_sq, NCW * (l + 1))
            dve.tensor_reduce(rms[:, 1, :], sq[:], AX.X, ALU.add).then_inc(s_ssum, 1)
            inverse_root(2 * l)
            for j in range(NCW if l == 0 else 2):
                normalise(j)

        def normalise(j):
            cols = slice(j * CW, (j + 1) * CW)
            for tb in range(TB):
                last = dve.tensor_scalar(y[:, tb, cols], x[:, tb, cols], rms[:, 1, tb:tb + 1], None, ALU.mult)
            last.then_inc(s_xn, 1)

        def gained(l, j):
            cols = slice(j * CW, (j + 1) * CW)
            c = chunk(l, j)
            for tb in range(TB):
                dve.wait_ge(s_osq, TB * (NCW * l + j) + tb + 1)
                if (j, tb) == (NCW - 1, TB - 1):
                    dve.tensor_reduce(rms[:, 1, :], sq[:], AX.X, ALU.add).then_inc(s_ssum, 1)
                last = dve.tensor_tensor(y[:, tb, cols], acc[c % 2][:, tb, :], gain[:, cols], ALU.mult)
            last.then_inc(s_acc[c % 2], 1)

        def rope(src, heads):
            half = ROT // 2
            v4 = src.rearrange("p b (h e) -> p b h e", e=A_HD)
            t1, t2 = v4[:, :, :, 0:half], v4[:, :, :, half:ROT]
            n = TB * heads * half
            tmp = [rt[:, i * n:(i + 1) * n].rearrange("p (b h e) -> p b h e", b=TB, e=half) for i in range(4)]
            cos, sin = (cs[:, i].unsqueeze(2).broadcast_to([P, TB, heads, half]) for i in range(2))
            dve.tensor_tensor(tmp[0], t1, cos, ALU.mult)
            dve.tensor_tensor(tmp[1], t2, sin, ALU.mult)
            dve.tensor_tensor(tmp[2], t2, cos, ALU.mult)
            link(dve.tensor_tensor(tmp[3], t1, sin, ALU.mult))
            dve.tensor_tensor(t1, tmp[0], tmp[1], ALU.subtract)
            link(dve.tensor_tensor(t2, tmp[2], tmp[3], ALU.add))
            dve.memset(rt[:, 0:1], 0.0).then_inc(s_rope, 1)

        def scores(l, grp, u):
            name = ("s", l, grp, u)
            n, w, m = (A_PER, P, wmask[:, 0:P]) if u == 0 else (2, SEQ, wmask[:, P:P + SEQ])
            h0 = max(0, 2 * (u - 1))
            sink = sinks[:, A_PER * grp + h0:A_PER * grp + h0 + n]
            if (l, grp, u) == (0, 0, 0):
                dve.wait_ge(s_late, 32)
            dve.wait_ge(*unit_full(name))
            p = scr[:, u, :].rearrange("p (h s) -> p h s", s=w)
            dve.tensor_tensor(p, bank_s(name)[:].rearrange("p (h s) -> p h s", s=w),
                              m.unsqueeze(1).broadcast_to([P, n, w]), ALU.add).then_inc(s_sfree[UNIT1[name] % 2], 1)
            dve.wait_ge(*unit_read(name))
            link(dve.tensor_reduce(mx[:, u, 0:n], p, AX.X, ALU.max))
            link(dve.tensor_tensor(mx[:, u, 0:n], mx[:, u, 0:n], sink, ALU.max))
            link(dve.tensor_scalar(mx[:, u, 0:n], mx[:, u, 0:n], -1.0, None, ALU.mult))
            dve.tensor_tensor(snk[:, min(u, 1), h0:h0 + n], sink, mx[:, u, 0:n], ALU.add).then_inc(s_max, 1)

        def denominators(l, grp):
            dve.wait_ge(s_exp, exp_index(l, grp, 2))
            link(dve.tensor_tensor(den[:], den[:], snk[:], ALU.add))
            link(dve.reciprocal(rden[:, grp % 2], den[:]))

        def attended(l, grp):
            name = ("o", l, grp)
            dve.wait_ge(*unit_full(name))
            if grp == 0:
                dve.wait_ge(*unit_full(("go", l, 1)))
            for tb in range(TB):
                last = dve.tensor_tensor(y[:, tb, grp * A_KVW:(grp + 1) * A_KVW].rearrange("p (h e) -> p h e", e=A_HD),
                                         bank_s(name)[:, tb * A_KVW:(tb + 1) * A_KVW]
                                         .rearrange("p (h e) -> p h e", e=A_HD),
                                         rden[:, grp % 2, tb, :].unsqueeze(2).broadcast_to([P, A_PER, A_HD]), ALU.mult)
            last.then_inc(s_sfree[UNIT1[name] % 2], 1)
            dve.wait_ge(*unit_read(name))

        def angles():
            tau = 2.0 * np.pi
            parts = [6.28125]
            parts.append(float(np.float32(np.round((tau - parts[0]) * 2 ** 21) / 2 ** 21)))
            parts.append(float(np.float32(tau - parts[0] - parts[1])))
            magic = 1.5 * 2.0 ** 23
            link(dve.tensor_copy(posf[:], posi[:]))
            for tb in range(TB):
                last = dve.tensor_scalar(ang[:, 0, tb, :], invf[:], posf[:, tb:tb + 1], None, ALU.mult)
            link(last)
            a, n, r, t = (ang[:, i].rearrange("p b e -> p (b e)") for i in (0, 1, 2, 3))
            link(dve.tensor_scalar(n, a, 1.0 / tau, None, ALU.mult))
            link(dve.tensor_scalar(t, n, magic, None, ALU.add))
            link(dve.tensor_scalar(n, t, magic, None, ALU.subtract))
            link(dve.scalar_tensor_tensor(out=r, in0=n, scalar=-parts[0], in1=a, op0=ALU.mult, op1=ALU.add))
            link(dve.scalar_tensor_tensor(out=t, in0=n, scalar=-parts[1], in1=r, op0=ALU.mult, op1=ALU.add))
            link(dve.scalar_tensor_tensor(out=r, in0=n, scalar=-parts[2], in1=t, op0=ALU.mult, op1=ALU.add))
            link(dve.tensor_scalar(n, r, 3.1415925, -3.1415925, ALU.min, ALU.max))
            link(dve.tensor_scalar(t, n, -1.0, None, ALU.mult))
            link(dve.tensor_tensor(t, t, n, ALU.max))
            dve.tensor_scalar(a, t, -1.0, float(np.pi / 2), ALU.mult, ALU.add).then_inc(s_ang, 1)

        dve.memset(ones[:], 1.0).then_inc(s_mem, 1)
        dve.memset(eps[:], EPS).then_inc(s_mem, 1)
        mod_zero(0)
        mod_zero(1)
        dve.wait_ge(s_silu, 1)
        for i in range(MOD_N):
            mod(0, i)
        dve.wait_ge(s_mem, 2)
        dve.wait_ge(s_const, 48)
        link(dve.tensor_copy(lmask[:].rearrange("p i n -> p (i n)"), zt[:].rearrange("p b n -> p (b n)")))
        angles()
        normalised(0)
        for i in range(MOD_N):
            mod(1, i)
        mod_shift(0)
        mod_scale(0)
        mod_zero(2)

        for l in range(DEPTH):
            if l:
                normalised(l)
            for r in range(GRAN1):
                if r < GPC:
                    if r == 0:
                        fill_mod(l, 0)
                        fill_mod(l, 1)
                    fill_lo(("h", l, r))
                if R_OUT <= r < R_OUT + GPC:
                    fill_lo(("y", l, r - R_OUT))
                if l == 0 or r >= AHEAD:
                    lo(GRAN1 * l + r)
                if 1 <= r and r + 1 < GPC:
                    fill_mod(l, r + 1)
                if l and r < 2:
                    normalise(2 + r)
                if r == 8:
                    dve.wait_ge(s_wg, 2 * l + 1)
                    dve.tensor_tensor(wglo[:], wg[:], wghi[:].bitcast(F32), ALU.subtract).then_inc(s_wg, 1)
                if r == 16:
                    name = ("gl", l)
                    flat = la[:].rearrange("p b n -> p (b n)")
                    dve.wait_ge(*unit_full(name))
                    dve.tensor_tensor(la[:], bank_s(name)[:].rearrange("p (b n) -> p b n", b=TB),
                                      gbias[:].unsqueeze(1).broadcast_to([P, TB, G_KW]), ALU.add)\
                        .then_inc(s_sfree[UNIT1[name] % 2], 1)
                    dve.wait_ge(*unit_read(name))
                    link(dve.tensor_scalar(zt[:, 0, :], flat, -1.0, None, ALU.mult))
                    dve.tensor_tensor(zt[:, 0, :], zt[:, 0, :], flat, ALU.min).then_inc(s_neg, 1)
                    dve.wait_ge(s_neg, l + 1)
                    link(dve.tensor_scalar(flat, flat, 0.0, 1.0 / TAU, ALU.min, ALU.mult))
                if r == 18:
                    flat = la[:].rearrange("p b n -> p (b n)")
                    dve.wait_ge(s_ln, 2 * l + 2)
                    dve.scalar_tensor_tensor(out=flat, in0=zt[:, 0, :], scalar=-1.0 / TAU, in1=flat,
                                             op0=ALU.mult, op1=ALU.add).then_inc(s_la, 1)
                    link(dve.memset(st[:], 0.0))
                for i in range(-1, len(LEVELS)):
                    if i >= 0 and r == R_LEVEL + 4 + 4 * i:
                        m = LEVELS[i]
                        dve.wait_ge(*unit_read(("dz", l, i)))
                        for src, half in ((gqT, 1), (gkT, 0)):
                            a = zt[:, i % 2, :].rearrange("p (n s m) -> p n s m", s=2, m=m)[:, :, half, :]
                            b = src.rearrange("p (n s m) -> p n s m", s=2, m=m)[:, :, half, :]
                            last = dve.tensor_tensor(a, a, b, ALU.mult)
                        last.then_inc(s_gx, 1)
                    if r == (R_LEVEL + 6 + 4 * i if i >= 0 else 20):
                        for odd in range(2):
                            name = ("sc", l, i, odd)
                            bank = bank_s(name)
                            dve.wait_ge(*unit_full(name))
                            if i == 0:
                                dst = stx[:].rearrange("p (k o) t -> p k o t", o=2)[:, :, odd, :]
                                ins = dve.tensor_copy(dst, bank[:, 0:2 * P].rearrange("p (k t) -> p k t", t=P))
                            else:
                                mask = lmask[:, i if i > 0 else 0, :].unsqueeze(1).broadcast_to([P, 4, P])
                                ins = dve.copy_predicated(st[:, odd], mask, bank[:].rearrange("p (k t) -> p k t", t=P))
                            ins.then_inc(s_sfree[UNIT1[name] % 2], 1)
                            dve.wait_ge(*unit_read(name))
                if r == 28:
                    dve.wait_ge(*acc_read(chunk(l, "kv")))
                    rope(ks, A_KV)
                if r in (36, 44):
                    dve.wait_ge(*acc_read(chunk(l, "q0" if r == 36 else "q1")))
                    rope(stage[:], A_HEADS // 2)
                if r - 3 in R_MODG:
                    j = R_MODG.index(r - 3)
                    name = ("mg", l, j)
                    dve.wait_ge(s_gain, 16 * (l + 1))
                    dve.wait_ge(*unit_full(name))
                    dve.tensor_tensor(gain[:, j * CW:(j + 1) * CW], gain[:, j * CW:(j + 1) * CW], bank_s(name)[:],
                                      ALU.mult).then_inc(s_sfree[UNIT1[name] % 2], 1)
                    if j == NCW - 1 and l + 1 < DEPTH:
                        mod_zero(THIRDS.index((l + 1, 0)))
                if l + 1 < DEPTH and r == R_MODS + 3:
                    mod_shift(l + 1)
                    mod_zero(THIRDS.index((l + 1, 1)))
                if l + 1 < DEPTH and r == R_MODA + 3:
                    mod_scale(l + 1)
                    mod_zero(THIRDS.index((l + 1, 2)))
                for grp, b in enumerate(R_SWA):
                    if 3 <= r - b <= 5:
                        scores(l, grp, r - b - 3)
                    if r - b == 7:
                        denominators(l, grp)
                    if r - b == 11:
                        attended(l, grp)
                if r == 60:
                    dve.wait_ge(*acc_read(chunk(l, "sv")))
                    for tb in range(TB):
                        last = dve.bn_stats(stats[:, tb, :], zt[:, tb, :])
                    link(last)
                    for tb in range(TB):
                        last = dve.bn_aggr(mv[:, tb, :], stats[:, tb, :])
                    last.then_inc(s_var, 1)
                if r == 62:
                    dve.wait_ge(s_std, l + 1)
                    link(dve.reciprocal(lstd[:, 1, :], lstd[:, 0, :]))
                    for tb in range(TB):
                        last = dve.tensor_scalar(zt[:, tb, :], zt[:, tb, :], mv[:, tb, 0:1], lstd[:, 1, tb:tb + 1],
                                                 ALU.subtract, ALU.mult)
                    link(last)
                    link(dve.tensor_tensor(zt[:], zt[:], lnr[:, 0, :].unsqueeze(1).broadcast_to([P, TB, S_W]), ALU.mult))
                if r == 63:
                    dve.tensor_tensor(zt[:], zt[:], lnr[:, 1, :].unsqueeze(1).broadcast_to([P, TB, S_W]), ALU.add)\
                        .then_inc(s_vn, 1)
                if r in (61, 62):
                    tb = r - 61
                    dve.wait_ge(*unit_read(("go", l, tb)))
                    link(dve.tensor_tensor(rt[:], y[:, tb, 3 * CW:], y[:, tb, 3 * CW:], ALU.mult))
                    last = dve.tensor_reduce(gsq[:, 0, tb, :], rt[:].rearrange("p (h e) -> p h e", e=G_DV), AX.X, ALU.add)
                    if tb == 0:
                        link(last)
                    else:
                        last.then_inc(s_gsq, 1)
                        dve.wait_ge(s_gsq, l + 1)
                if r == 64:
                    dve.wait_ge(s_grms, l + 1)
                    link(dve.reciprocal(gsq[:, 0], gsq[:, 1]))
                    gy = y[:, :, 3 * CW:].rearrange("p b (h e) -> p b h e", e=G_DV)
                    link(dve.tensor_tensor(gy, gy, gsq[:, 0].unsqueeze(3).broadcast_to([P, TB, G_HEADS, G_DV]), ALU.mult))
                    for tb in range(TB):
                        last = dve.tensor_tensor(gy[:, tb], gy[:, tb],
                                                 gnorm[:].unsqueeze(1).broadcast_to([P, G_HEADS, G_DV]), ALU.mult)
                    link(last)
                if r in (68, 69):
                    tb = r - 68
                    name = ("sg", l, tb)
                    dve.wait_ge(*unit_full(name))
                    dve.tensor_tensor(rt[:].rearrange("p (g e) -> p g e", e=S_GD),
                                      bank_s(name)[:].rearrange("p (g e) -> p g e", e=S_GD),
                                      sgb[:].unsqueeze(2).broadcast_to([P, S_G, S_GD]), ALU.add)\
                        .then_inc(s_sfree[UNIT1[name] % 2], 1)
                    dve.wait_ge(*unit_read(name))
                    link(dve.tensor_tensor(y[:, tb, 2 * CW:3 * CW], y[:, tb, 2 * CW:3 * CW], rt[:], ALU.mult))
                if r in (70, 76, 84, 92):
                    i = (70, 76, 84, 92).index(r)
                    j = Z_ORDER[i]
                    dve.wait_ge(*acc_read(chunk(l, f"z{j}")))
                    dve.tensor_tensor(y[:, :, j * CW:(j + 1) * CW], y[:, :, j * CW:(j + 1) * CW], zt[:], ALU.mult)\
                        .then_inc(s_ym, 1)
                if r >= R_OUT + GPC and (r - R_OUT) % GPC == 3:
                    gained(l, (r - R_OUT) // GPC - 1)
                step = mod_step(l, r)
                if step:
                    mod(*step)
            for r in range(AHEAD if l + 1 < DEPTH else 0):
                lo(GRAN1 * (l + 1) + r)
            gained(l, NCW - 1)
            inverse_root(2 * l + 1)
            dve.wait_ge(*acc_read(chunk(l, NCW - 1)))
            for j in range(NCW):
                cols = slice(j * CW, (j + 1) * CW)
                for tb in range(TB):
                    last = dve.scalar_tensor_tensor(out=x[:, tb, cols], in0=y[:, tb, cols], scalar=rms[:, 1, tb:tb + 1],
                                                    in1=x[:, tb, cols], op0=ALU.mult, op1=ALU.add)
                last.then_inc(s_xd, 1)

    @block.tensor
    def _(pe):
        pe.wait_ge(s_ident, 16)
        pe.wait_ge(s_mem, 2)

        def fill(name):
            i, bank, kind, l = FILL1[name], bank_t(name), name[0], name[1]
            need(pe, (s_tfree[i % 2], i // 2))
            if kind == "h":
                pe.wait_ge(s_xn, NCW * l + name[2] // 2 + 1)
                src, cols = y, [P * (2 * name[2] + k) for k in range(2)]
            elif kind == "y":
                pe.wait_ge(s_ym, NCW * l + name[2] // 2 + 1)
                src, cols = y, [P * (y_tile(name[2]) + k) for k in range(2)]
            elif kind in ("gq", "gk"):
                pe.wait_ge(*acc_read(chunk(l, "gqk")))
                src, cols = stage, [(kind == "gk") * G_KW + k * P for k in range(2)]
            elif kind == "ak":
                pe.wait_ge(s_rope, 3 * l + 1)
                src, cols = ks, [k * P for k in range(2)]
            elif kind == "aq":
                pe.wait_ge(s_rope, 3 * l + 2 + name[2])
                src, cols = stage, [P * (2 * name[3] + k) for k in range(2)]
            if kind == "p":
                pe.wait_ge(s_exp, exp_index(l, name[2], name[3]))
                for k in range(4):
                    t = pe.transpose(bank[:, k * P:(k + 1) * P], scr[:, name[3], k * P:(k + 1) * P], ident[:])
            else:
                for k in range(2):
                    for tb in range(TB):
                        t = pe.transpose(bank[:, k * SEQ + tb * P:k * SEQ + (tb + 1) * P],
                                         src[:, tb, cols[k]:cols[k] + P], ident[:])
            t.then_inc(s_tfull, 1)

        def unit(name):
            i, bank, kind, l = UNIT1[name], bank_s(name), name[0], name[1]
            need(pe, (s_sfree[i % 2], i // 2))
            if kind in ("ms", "ma", "mg"):
                q = THIRDS.index((l, ("ms", "ma", "mg").index(kind)))
                if kind == "mg":
                    pe.wait_ge(s_macc, MOD_N * (q + 1))
                    m = pe.matmul(bank[:], ones[:], macc[:, name[2] * CW:(name[2] + 1) * CW], start=True, stop=True)
                else:
                    for k in range(KT):
                        if k % (MOD_W // P) == 0:
                            pe.wait_ge(s_macc, MOD_N * q + KT * (k // (MOD_W // P) + 1))
                        m = pe.matmul(bank[:, k:k + 1], macc_of(q)[:, k * P:(k + 1) * P], ones[:, 0:1],
                                      start=True, stop=True)
            elif kind == "cg":
                pe.wait_ge(s_wg, 2 * l + 2)
                for k in range(KT):
                    for q, (w, a) in enumerate(((wghi, hhi), (wglo, hhi), (wghi, hlo))):
                        m = pe.matmul(bank[0:RANK, 0:SEQ], w[:, k, :], a[:, k, :],
                                      start=(k == 0 and q == 0), stop=(k == KT - 1 and q == 2))
            elif kind == "gl":
                pe.wait_ge(*unit_read(("cg", l)))
                for tb in range(TB):
                    m = pe.matmul(bank[:, tb * G_KW:(tb + 1) * G_KW], cgT[:, tb * P:(tb + 1) * P], gup[:],
                                  start=True, stop=True)
            elif kind == "dz":
                if name[2] == 0:
                    pe.wait_ge(s_la, l + 1)
                    pe.wait_ge(s_late, 32)
                for pair in range(2):
                    for tb in range(TB):
                        col = pair * SEQ + tb * P
                        t = name[2] + 1 if name[2] else tb
                        m = pe.matmul(bank[:, col:col + P], la[:, tb, pair * P:(pair + 1) * P], sums[:, t, :],
                                      start=True, stop=True)
            elif kind == "sc":
                _, _, i, odd = name
                rows = slice(odd * G_DK, (odd + 1) * G_DK)
                if i < 0:
                    pe.wait_ge(*copied(("gq", l)))
                    pe.wait_ge(*copied(("gk", l)))
                    key, query = gkT, gqT
                else:
                    pe.wait_ge(s_gx, len(LEVELS) * l + i + 1)
                    key = query = zt[:, i % 2, :]
                for pair in range(2):
                    if i == 0:
                        m = pe.matmul(bank[:, pair * P:(pair + 1) * P], key[rows, pair * SEQ:pair * SEQ + P],
                                      query[rows, pair * SEQ + P:(pair + 1) * SEQ], start=True, stop=True)
                    else:
                        for tb in range(TB):
                            tok = slice(pair * SEQ + tb * P, pair * SEQ + (tb + 1) * P)
                            k = TB * pair + tb
                            m = pe.matmul(bank[:, k * P:(k + 1) * P], key[rows, tok], query[rows, tok],
                                          start=True, stop=True)
            elif kind == "go":
                tb = name[2]
                if tb == 0:
                    pe.wait_ge(*unit_read(("sc", l, len(LEVELS) - 1, 0)))
                    pe.wait_ge(*unit_read(("sc", l, len(LEVELS) - 1, 1)))
                for h in range(G_HEADS):
                    out = bank[:, h * G_DV:(h + 1) * G_DV]
                    if tb:
                        pe.matmul(out, stx[:, h, :], gv[:, 0, h * G_DV:(h + 1) * G_DV], start=True, stop=False)
                    m = pe.matmul(out, st[:, h % 2, TB * (h // 2) + tb, :], gv[:, tb, h * G_DV:(h + 1) * G_DV],
                                  start=(tb == 0), stop=True)
            elif kind == "s":
                _, _, grp, u = name
                if u == 0:
                    if grp == 0:
                        pe.wait_ge(*copied(("ak", l)))
                    for k in range(2):
                        pe.wait_ge(*copied(("aq", l, grp // 2, k)))
                rows = slice((grp % 2) * A_HD, (grp % 2 + 1) * A_HD)
                w, tb = (P, 0) if u == 0 else (SEQ, 1)
                for b in range(CW // w):
                    h = 4 * (grp // 2) + b + max(0, 2 * (u - 1))
                    m = pe.matmul(bank[:, b * w:(b + 1) * w], qT[rows, h, tb * P:(tb + 1) * P],
                                  kT[rows, grp // 2, 0:w], start=True, stop=True)
            elif kind == "o":
                grp = name[2]
                for u in (1, 2):
                    pe.wait_ge(*copied(("p", l, grp, u)))
                for tb in range(TB):
                    for h in range(A_PER):
                        for s in range(tb + 1):
                            u, col = (0, h) if tb == 0 else (1 + h // 2, 2 * (h % 2) + s)
                            at_h = tb * A_KVW + h * A_HD
                            m = pe.matmul(bank[:, at_h:at_h + A_HD], scr[:, 3 + u, col * P:(col + 1) * P],
                                          av[:, s, grp * A_HD:(grp + 1) * A_HD], start=(s == 0), stop=(s == tb))
            else:
                tb = name[2]
                pe.wait_ge(s_vn, l + 1)
                pe.wait_ge(s_sgw, l + 1)
                for g in range(S_G):
                    m = pe.matmul(bank[:, g * S_GD:(g + 1) * S_GD], sgw[:, g, :], zt[:, tb, g * S_GD:(g + 1) * S_GD],
                                  start=True, stop=True)
            m.then_inc(s_sfull, 1)

        for l, r in STEPS1:
            for name in fills1(l, r):
                fill(name)
            for name in units1(l, r):
                unit(name)
            if r < 0:
                continue
            c, g = divmod(r, GPC)
            gc = NCH1 * l + c
            if c == 0:
                pe.wait_ge(s_h, GPC * l + g + 1)
            if r >= R_OUT and c == len(CHUNKS1):
                pe.wait_ge(*copied(("y", l, g)))
            if g == 0:
                need(pe, (s_acc[gc % 2], gc // 2))
            n = GRAN1 * l + r
            pe.wait_ge(s_lo, n + 1)
            for k in range(GK):
                kt = (y_tile(g) if c >= len(CHUNKS1) else GK * g) + k
                for tb in range(TB):
                    tile = slice(tb * P, (tb + 1) * P)
                    for q, (a, b) in enumerate(((hhi, whi), (hhi, wlo), (hlo, whi))):
                        m = pe.matmul(acc[gc % 2][:, tb, :], a[:, kt, tile], b[:, n % SLOTS, k * CW:(k + 1) * CW],
                                      start=(g == 0 and k == 0 and q == 0),
                                      stop=(g == GPC - 1 and k == GK - 1 and q == 2))
            m.then_inc(s_used, 1)


def y_tile(i):
    return (CW // P) * Z_ORDER[i // 2] + GK * (i % 2)


def first_constants():
    half = ROT // 2
    inv = np.float32(500000.0) ** (-(np.arange(half, dtype=np.float32) * np.float32(2.0 / ROT)))
    s, t = np.arange(P)[:, None], np.arange(P)[None, :]
    sums = [s > t, s <= t]
    masks = [s == t]
    for m in LEVELS[1:]:
        upper = (t // m) % 2 == 1
        mid = t // m * m
        after = (t // (2 * m)) * 2 * m + m
        sums.append(np.where(upper, (s >= mid) & (s <= t), (s > t) & (s < after)))
        masks.append((s // (2 * m) == t // (2 * m)) & upper & ((s // m) % 2 == 0))
    return {
        "inv_freq": inv.astype(np.float32),
        "sums": np.stack(sums, axis=1).astype(np.float32),
        "lmask": np.stack(masks, axis=1).astype(np.float32),
        "mask_w": band(lambda d: np.where((d >= 0) & (d < WINDOW), 0.0, NEG)),
    }


def first_stream(w_in, w_out):
    out = []
    for l in range(DEPTH):
        for _, start in CHUNKS1:
            out.append(columns(w_in[l], start))
        for j in range(NCW):
            tiles = columns(w_out[l], CW * j)
            out.append(tiles[[y_tile(i) // GK for i in range(GPC)]])
    return np.concatenate(out)


def by_partition(a):
    return np.ascontiguousarray(np.swapaxes(a.reshape(*a.shape[:-1], KT, P), -1, -2))


def first_arrays(x, c, positions, w_mod, b_mod, g_pre, g_post, w_in, w_out, swa_sinks, sg_w, sg_b, sg_ln_g,
                 sg_ln_b, gla_w_gate_up, gla_b_gate, gla_norm_g):
    halves = D // MOD_W
    return {
        "x": np.ascontiguousarray(x[0]),
        "c": by_partition(c[0]),
        "positions": np.ascontiguousarray(positions.reshape(TB, P).T),
        "w_mod": np.ascontiguousarray(w_mod.reshape(DEPTH, KT, P, 3, halves, MOD_W).transpose(0, 3, 4, 1, 2, 5))
        .reshape(DEPTH, 3, MOD_N, P, MOD_W),
        "b_mod": b_mod.reshape(DEPTH, 3, D),
        "g_pre": by_partition(g_pre),
        "g_post": g_post,
        "w1": first_stream(w_in, w_out),
        "wg": np.ascontiguousarray(w_in[:, :, OFF_GATE:OFF_GATE + RANK].reshape(DEPTH, KT, P, RANK)
                                   .transpose(0, 2, 1, 3)),
        "gate_up": gla_w_gate_up,
        "b_gate": gla_b_gate,
        "gnorm": gla_norm_g,
        "sinks": swa_sinks,
        "sg_w": np.ascontiguousarray(sg_w.transpose(0, 3, 1, 2)),
        "sg_b": np.ascontiguousarray(sg_b.transpose(0, 2, 1)),
        "sg_ln_g": sg_ln_g,
        "sg_ln_b": sg_ln_b,
        **first_constants(),
    }


def second_arrays(w_in, b_forget, b_gate, w_up_a, w_up_b, w_out, ln_g, ln_b):
    f = 8 * W2
    return {
        "w": second_stream(w_in, w_up_a, w_up_b, w_out),
        "wf": np.ascontiguousarray(w_in[:, :, f:f + NH2].reshape(DEPTH, KT, P, NH2).transpose(0, 2, 1, 3)),
        "bf": b_forget, "bg": b_gate.reshape(DEPTH * 2 * NCW, CW), "ln_g": ln_g, "ln_b": ln_b,
        **constants(),
    }


def program(nc, dram):
    with ExitStack() as ctx:
        def sb(name, shape, dt=F32):
            return ctx.enter_context(nc.sbuf_tensor(name, shape, dt))

        x = sb("x", [P, TB, D])
        rings = (sb("raw", [P, SLOTS, GK * CW]), sb("whi", [P, SLOTS, GK * CW], F32R),
                 sb("wlo", [P, SLOTS, GK * CW], F32R))
        acc = [ctx.enter_context(nc.psum_tensor(f"acc{i}", [P, TB, CW], F32)) for i in range(2)]
        psT = [ctx.enter_context(nc.psum_tensor(f"psT{i}", [P, CW], F32)) for i in range(2)]
        psS = [ctx.enter_context(nc.psum_tensor(f"psS{i}", [P, CW], F32)) for i in range(2)]
        s_w = [ctx.enter_context(nc.semaphore(f"c_w{i}")) for i in range(SLOTS)]
        with ExitStack() as first:
            first_block(nc, first, x, rings, (acc, psT, psS), dram, s_w)
        with ExitStack() as second:
            second_block(nc, second, x, rings, (acc, psT, psS), dram, s_w)


def kernel(x, c, positions, w_mod, b_mod, g_pre, g_post, w_in, w_out, swa_sinks, sg_w, sg_b, sg_ln_g, sg_ln_b,
           gla_w_gate_up, gla_b_gate, gla_norm_g, w_in_2, b_forget_2, b_gate_2, w_up_a_2, w_up_b_2, w_out_2,
           ln_g_2, ln_b_2):
    import concourse.bacc as bacc
    from concourse.bass_utils import run_bass_kernel_spmd

    nc = bacc.Bacc("TRN2", target_bir_lowering=False, num_devices=1)
    arrays = {
        **first_arrays(x, c, positions, w_mod, b_mod, g_pre, g_post, w_in, w_out, swa_sinks, sg_w, sg_b, sg_ln_g,
                       sg_ln_b, gla_w_gate_up, gla_b_gate, gla_norm_g),
        **second_arrays(w_in_2, b_forget_2, b_gate_2, w_up_a_2, w_up_b_2, w_out_2, ln_g_2, ln_b_2),
    }
    dram = {name: nc.dram_tensor(f"in_{name}", a.shape, mybir.dt.from_np(a.dtype), kind="ExternalInput").ap()
            for name, a in arrays.items()}
    dram["out"] = nc.dram_tensor("out_x", (SEQ, D), F32, kind="ExternalOutput").ap()
    program(nc, dram)
    r = run_bass_kernel_spmd(nc, [{f"in_{name}": a for name, a in arrays.items()}], core_ids=[0])
    return r.results[0]["out_x"].reshape(1, SEQ, D)
```

```python
from contextlib import ExitStack

import numpy as np

import concourse.bass as bass
from concourse import mybir

F32 = mybir.dt.float32
F32R = mybir.dt.float32r
U32 = mybir.dt.uint32
I32 = mybir.dt.int32
ACT = mybir.ActivationFunctionType
ALU = mybir.AluOpType
AX = mybir.AxisListType

P = 128
SEQ = 256
TB = SEQ // P
D = 2048
KT = D // P
CW = 512
NCW = D // CW
GK = 2
SLOTS = 4
NEG = -1.0e30
DEPTH = 2

HD = 128
NH2 = 12
W2 = NH2 * HD
HPG = CW // HD
NGRP = 2 * NH2 // HPG
KT_UP = W2 // P
ALPHA = float((2 * DEPTH) ** 0.25)
SCALE2 = float(HD) ** -0.5
LN_EPS = 1e-5


def at(layer, per_layer, count):
    return layer * per_layer + count


def second_plan():
    chunks = []
    for half in range(2):
        for grp in range(3):
            chunks += [(kind, 3 * half + grp) for kind in "qkvz"]
        chunks += [("g", NCW * half + j) for j in range(NCW)]
        chunks += [("u", NCW * half + j) for j in range(NCW)]
    chunks += [("o", j) for j in range(NCW)]
    first, n = [], 0
    for kind, _ in chunks:
        first.append(n)
        n += (KT_UP if kind == "u" else KT) // GK
    return chunks, first, n


CHUNKS2, FIRST2, GRAN2 = second_plan()


def granules2(c):
    return (FIRST2 + [GRAN2])[c + 1] - FIRST2[c]


def group_step(c, g):
    found = []
    for q in range(len(CHUNKS2)):
        if CHUNKS2[q][0] == "q" and q <= c:
            r = FIRST2[c] + g - FIRST2[q]
            if r < 48:
                found.append((CHUNKS2[q][1], r))
    return found


F_CHUNK = [i for i, k in enumerate(CHUNKS2) if k == ("g", 1)][0]


def fills2(c, g):
    out = []
    if c == 0:
        out += [("x", 0), ("x", 1)] if g == 0 else [("x", g + 1)] if g < KT // 2 - 1 else []
    for grp, r in group_step(c, g):
        out += {12: [("q", grp, 0), ("q", grp, 1)], 20: [("k", grp, 0), ("k", grp, 1)], 28: [("p", grp, 0)],
                29: [("p", grp, 1)], 30: [("p", grp, 2)], 38: [("a", grp, 0)], 39: [("a", grp, 1)]}.get(r, [])
    if c and CHUNKS2[c - 1][0] == "u" and CHUNKS2[c - 1][1] >= NCW and g == 3:
        j = CHUNKS2[c - 1][1] - NCW
        out += [("y", 2 * j), ("y", 2 * j + 1)]
    return out


def units2(c, g):
    out = []
    for grp, r in group_step(c, g):
        out += {23: [("s", grp, 0)], 24: [("s", grp, 1)], 25: [("s", grp, 2)],
                33: [("o", grp, 0)], 34: [("o", grp, 1)]}.get(r, [])
    if (c, g) == (F_CHUNK, 0):
        out += [("f", 0), ("f", 1)]
    return out


def numbered(what):
    names = [n for c in range(len(CHUNKS2)) for g in range(granules2(c)) for n in what(c, g)]
    return {name: i for i, name in enumerate(names)}


FILL2 = numbered(fills2)
UNIT2 = numbered(units2)
NF2, NU2 = len(FILL2), len(UNIT2)
assert NF2 % 2 == 0 and NU2 % 2 == 0
SPLIT2 = {name: i for i, name in enumerate([n for n in FILL2 if n[0] in "xay"])}
NV2 = 2
VLINKS2 = 47


def second_block(nc, ctx, x, rings, ps, dram, s_w, ident):
    raw, whi, wlo = rings
    acc, psT, psS = ps

    def sb(name, shape, dt=F32):
        return ctx.enter_context(nc.sbuf_tensor(name, shape, dt))

    def sem(name):
        return ctx.enter_context(nc.semaphore(name))

    xhi = sb("xhi", [P, KT, SEQ], F32R)
    xlo = sb("xlo", [P, KT, SEQ], F32R)
    ahi = sb("ahi", [P, KT_UP, SEQ], F32R)
    alo = sb("alo", [P, KT_UP, SEQ], F32R)
    y = sb("y", [P, TB, D])
    gb = sb("gb", [P, TB, D])
    stage = sb("stage", [P, TB, CW])
    qT = sb("qT", [P, HPG, SEQ])
    kT = sb("kT", [P, HPG, SEQ])
    v = sb("v", [P, TB, CW])
    z = sb("z", [P, TB, CW])
    prob = sb("prob", [P, 3, CW])
    probT = sb("probT", [P, 3, CW])
    rtmp = sb("rtmp", [P, CW])
    mask_a = sb("mask_a", [P, P + SEQ])
    mask_b = sb("mask_b", [P, P + SEQ])
    tables = sb("tables", [P, 2, 3, TB, HD // 2])
    gate_row = sb("gate_row", [P, 2, CW])
    wf = sb("wf", [P, KT, NH2])
    wfhi = sb("wfhi", [P, KT, NH2], F32R)
    wflo = sb("wflo", [P, KT, NH2], F32R)
    bf = sb("bf", [NH2, 1])
    fb = sb("fb", [NH2, SEQ])
    fl = sb("fl", [NH2, SEQ])
    fe = sb("fe", [NH2, SEQ])
    ncum = sb("ncum", [NH2, SEQ])
    ones = sb("ones", [P, SEQ])
    mx = sb("mx", [P, 3, HPG])
    den = sb("den", [P, TB, HPG])
    rden = sb("rden", [P, TB, HPG])
    stats = sb("stats", [P, TB, NCW, 6])
    mv = sb("mv", [P, TB, 2])
    std = sb("std", [P, TB])
    rstd = sb("rstd", [P, TB])
    nmr = sb("nmr", [P, TB])
    eps = sb("eps", [P, 1])

    s_hi = sem("c_hi")
    s_lo = sem("c_lo")
    s_used = sem("c_used")
    s_acc = [sem(f"c_acc{i}") for i in range(2)]
    s_tfull = sem("c_tfull")
    s_thi = sem("c_thi")
    s_tfree = [sem(f"c_tfree{i}") for i in range(2)]
    s_sfull = sem("c_sfull")
    s_sfree = [sem(f"c_sfree{i}") for i in range(2)]
    s_const = sem("c_const")
    s_mem = sem("c_mem")
    s_rope = sem("c_rope")
    s_max = sem("c_max")
    s_exp = sem("c_exp")
    s_att = sem("c_att")
    s_gate = sem("c_gate")
    s_grow = [sem(f"c_grow{i}") for i in range(2)]
    s_fw = sem("c_fw")
    s_fwh = sem("c_fwh")
    s_f = sem("c_f")
    s_fln = sem("c_fln")
    s_cum = sem("c_cum")
    s_y = sem("c_y")
    s_lnp = sem("c_lnp")
    s_var = sem("c_var")
    s_std = sem("c_std")
    s_xn = sem("c_xn")
    s_xnp = sem("c_xnp")
    s_last = sem("c_last")
    s_half = sem("c_half")
    s_rstd = sem("c_rstd")
    s_xs = sem("c_xs")
    s_pool = sem("c_pool")
    s_self = sem("c_self")
    s_out = sem("c_out")

    block = ctx.enter_context(nc.Block())
    nch = len(CHUNKS2)

    def group_chunk(grp):
        return CHUNKS2.index(("q", grp))

    def dst_of(name):
        if name[0] == "a":
            return ahi, alo, HPG * (name[1] % 3) + 2 * name[2]
        return xhi, xlo, 2 * name[1]

    def multiplied(l, c):
        return s_used, at(l, GRAN2, SLOTS + FIRST2[c] + granules2(c))

    def acc_read(l, c):
        return s_acc[c % 2], at(l, nch // 2, c // 2 + 2)

    def unit_read(l, name):
        return s_sfree[UNIT2[name] % 2], at(l, NU2 // 2, UNIT2[name] // 2 + 2)

    def unit_full(l, name):
        return s_sfull, at(l, NU2, UNIT2[name] + 1)

    def copied(l, name):
        return s_tfree[FILL2[name] % 2], at(l, NF2 // 2, FILL2[name] // 2 + 2)

    def filled(l, name):
        return s_tfull, at(l, NF2, FILL2[name] + 1)

    def bank_t(name):
        return psT[FILL2[name] % 2]

    @block.sync
    def _(sp):
        with sp.Fori(1, DEPTH * GRAN2 // SLOTS) as i:
            for b in range(SLOTS):
                src = dram["w"][sp.snap(i * SLOTS + b)]
                sp.wait_ge(s_lo, i * SLOTS + b - SLOTS + 1)
                sp.dma_start(raw[:, b, :], src).then_inc(s_w[b], 16)
        for j in [*range(NV2), NCW - 1, NV2]:
            if j < NV2:
                sp.wait_ge(s_xn, 2 * (DEPTH * NV2 + j + 1))
            elif j == NV2:
                sp.wait_ge(s_last, 1)
            else:
                sp.wait_ge(s_xnp, DEPTH * (NCW - NV2) + j - NV2)
            sp.dma_start(dram["out"][:, j * CW:(j + 1) * CW].rearrange("(b p) n -> p b n", p=P),
                         x[:, :, j * CW:(j + 1) * CW]).then_inc(s_out, 16)
        sp.wait_ge(s_out, 16 * NCW)

    @block.gpsimd
    def _(pool):
        for tile, name in ((mask_a, "mask_a"), (mask_b, "mask_b"), (tables, "tables")):
            pool.dma_start(tile[:], dram[name]).then_inc(s_const, 16)
        for l in range(DEPTH):
            pool.dma_start(wf[:], dram["wf"][l]).then_inc(s_fw, 16)
            pool.dma_start(bf[:], dram["bf"][l]).then_inc(s_fw, 16)
            for j in range(2 * NCW):
                bias = dram["bg"][l * 2 * NCW + j].partition_broadcast(P)
                if j >= 2:
                    pool.wait_ge(*acc_read(l, CHUNKS2.index(("g", j - 2))))
                pool.dma_start(gate_row[:, j % 2, :], bias).then_inc(s_grow[j % 2], 16)
            pool.wait_ge(s_y, at(l, NCW, NCW))
            pool.dma_start(gb[:, 0, :], dram["ln_g"][l].partition_broadcast(P)).then_inc(s_lnp, 16)
            pool.dma_start(gb[:, 1, :], dram["ln_b"][l].partition_broadcast(P)).then_inc(s_lnp, 16)
            pool.wait_ge(s_lnp, at(l, 32, 32))
            for n, j in enumerate(range(NV2 + (l == DEPTH - 1), NCW)):
                cols = slice(j * CW, (j + 1) * CW)
                pool.wait_ge(s_xs, at(l, NCW - NV2, j - NV2 + 1))
                pool.tensor_tensor(x[:, :, cols], x[:, :, cols], gb[:, 0, cols].unsqueeze(1).broadcast_to([P, TB, CW]),
                                   ALU.mult).then_inc(s_pool, 1)
                pool.wait_ge(s_pool, at(l, NCW - NV2, n + 1))
                pool.tensor_tensor(x[:, :, cols], x[:, :, cols], gb[:, 1, cols].unsqueeze(1).broadcast_to([P, TB, CW]),
                                   ALU.add).then_inc(s_xnp, 1)

    @block.scalar
    def _(act):
        act.wait_ge(s_mem, 2)

        with act.Fori(0, DEPTH) as l:

            def hi(n):
                act.wait_ge(s_w[n % SLOTS], at(l, 16 * GRAN2 // SLOTS, 16 * (n // SLOTS + 1)))
                act.wait_ge(s_used, at(l, GRAN2, n + 1))
                act.activation(whi[:, n % SLOTS, :], raw[:, n % SLOTS, :], ACT.Copy).then_inc(s_hi, 1)

            def fill_hi(name):
                h, _, k = dst_of(name)
                act.wait_ge(*filled(l, name))
                act.activation(h[:, k:k + 2, :], bank_t(name)[:].rearrange("p (k t) -> p k t", k=2),
                               ACT.Copy).then_inc(s_thi, 1)

            def fill_copy(name, dst):
                act.wait_ge(*filled(l, name))
                act.activation(dst, bank_t(name)[:], ACT.Copy).then_inc(s_tfree[FILL2[name] % 2], 1)

            def evacuate(c, dst, func, scale=1.0):
                act.wait_ge(*multiplied(l, c))
                act.activation(dst[:], acc[c % 2][:], func, scale=scale).then_inc(s_acc[c % 2], 1)

            def attention(grp, r):
                c0 = group_chunk(grp)
                if grp >= 3 and r == 12:
                    evacuate(c0, stage, ACT.Copy, SCALE2)
                if grp >= 3 and r == 20:
                    act.wait_ge(*filled(l, ("q", grp, 1)))
                    evacuate(c0 + 1, stage, ACT.Copy)
                if r in (15, 16):
                    i = r - 15
                    fill_copy(("q", grp, i), qT[:, 2 * i:2 * i + 2, :].rearrange("p h t -> p (h t)"))
                if r in (23, 24):
                    i = r - 23
                    fill_copy(("k", grp, i), kT[:, 2 * i:2 * i + 2, :].rearrange("p h t -> p (h t)"))
                if r in (28, 29, 30):
                    u = r - 28
                    act.wait_ge(s_max, at(l, 3 * NGRP, 3 * grp + u + 1))
                    w = P if u == 0 else SEQ
                    for i in range(CW // w):
                        h = i + max(0, 2 * (u - 1))
                        p = act.activation(prob[:, u, i * w:(i + 1) * w], prob[:, u, i * w:(i + 1) * w], ACT.Exp,
                                           bias=mx[:, u, i:i + 1], accum_out=den[:, min(u, 1), h:h + 1])
                    p.then_inc(s_exp, 1)
                if r == 31:
                    evacuate(c0 + 2, v, ACT.Copy)
                if r in (32, 33, 34):
                    fill_copy(("p", grp, r - 32), probT[:, r - 32, :])
                if r == 36:
                    evacuate(c0 + 3, z, ACT.Silu)
                if r in (42, 43):
                    fill_hi(("a", grp, r - 42))

            for c in range(nch):
                prev, j = CHUNKS2[c - 1] if c else (None, None)
                for g in range(granules2(c)):
                    if c == 0:
                        fill_hi(("x", g))
                    hi(FIRST2[c] + g)
                    if (c, g) == (F_CHUNK - 1, 0):
                        act.wait_ge(s_fw, at(l, 32, 32))
                        act.activation(wfhi[:], wf[:], ACT.Copy).then_inc(s_fwh, 1)
                    for grp, r in group_step(c, g):
                        attention(grp, r)
                    if prev == "g" and g == 4:
                        act.wait_ge(*acc_read(l, c - 1))
                        t = (y if j < NCW else gb)[:, :, (j % NCW) * CW:(j % NCW + 1) * CW]
                        act.activation(t, t, ACT.Sigmoid).then_inc(s_gate, 1)
                    if prev == "u" and j >= NCW and g == 5:
                        fill_hi(("y", 2 * (j - NCW)))
                        fill_hi(("y", 2 * (j - NCW) + 1))
                    if (c, g) == (F_CHUNK, 7):
                        act.wait_ge(s_f, l + 1)
                        act.activation(fe[:], fe[:], ACT.Exp).then_inc(s_fln, 1)
                        act.wait_ge(s_fln, at(l, 2, 1))
                        act.activation(fe[:], fe[:], ACT.Ln, bias=1.0).then_inc(s_fln, 1)
            act.wait_ge(s_var, l + 1)
            act.activation(std[:], mv[:, :, 1], ACT.Sqrt, bias=eps[:, 0:1]).then_inc(s_std, 1)
            act.wait_ge(s_rstd, l + 1)
            for j in range(NV2, NCW):
                for tb in range(TB):
                    last = act.activation(x[:, tb, j * CW:(j + 1) * CW], x[:, tb, j * CW:(j + 1) * CW], ACT.Identity,
                                          scale=rstd[:, tb:tb + 1], bias=nmr[:, tb:tb + 1])
                last.then_inc(s_xs, 1)

    @block.vector
    def _(dve):
        dve.memset(ones[:], 1.0).then_inc(s_mem, 1)
        dve.memset(eps[:], LN_EPS).then_inc(s_mem, 1)
        for i, (s, credit) in enumerate(((s_used, SLOTS), (s_acc[0], 1), (s_acc[1], 1), (s_tfree[0], 1), (s_tfree[1], 1),
                          (s_sfree[0], 1), (s_sfree[1], 1), (s_xn, 2 * NV2), (s_xnp, NCW - NV2))):
            dve.memset(rtmp[:, i:i + 1], 0.0).then_inc(s, credit)
        dve.wait_ge(s_mem, 2)
        links = [0]

        with dve.Fori(0, DEPTH) as l:

            def link(ins):
                links[0] += 1
                ins.then_inc(s_self, 1)
                dve.wait_ge(s_self, at(l, VLINKS2, links[0]))

            def lo(n):
                dve.wait_ge(s_hi, at(l, GRAN2, n + 1))
                dve.tensor_tensor(wlo[:, n % SLOTS, :], raw[:, n % SLOTS, :], whi[:, n % SLOTS, :].bitcast(F32),
                                  ALU.subtract).then_inc(s_lo, 1)

            def fill_lo(name):
                h, w, k = dst_of(name)
                dve.wait_ge(s_thi, at(l, len(SPLIT2), SPLIT2[name] + 1))
                dve.tensor_tensor(w[:, k:k + 2, :], bank_t(name)[:].rearrange("p (k t) -> p k t", k=2),
                                  h[:, k:k + 2, :].bitcast(F32), ALU.subtract)\
                    .then_inc(s_tfree[FILL2[name] % 2], 1)

            def rope(c, which, tb):
                if tb == 0:
                    dve.wait_ge(s_const, 48)
                    dve.wait_ge(*multiplied(l, c))
                    if which:
                        dve.wait_ge(*filled(l, ("q", CHUNKS2[c][1], 1)))
                half = HD // 2
                src = acc[c % 2][:, tb, :].rearrange("p (h s e) -> p h s e", s=2, e=half)
                tmp = rtmp[:].rearrange("p (h s e) -> p h s e", s=2, e=half)
                cos, sin, nsin = (tables[:, which, i, tb, :].unsqueeze(1) for i in range(3))
                dve.tensor_tensor(stage[:, tb, :].rearrange("p (h e) -> p h e", e=half),
                                  acc[c % 2][:, tb, :].rearrange("p (h e) -> p h e", e=half),
                                  cos.broadcast_to([P, 2 * HPG, half]), ALU.mult)
                dve.tensor_tensor(tmp[:, :, 0, :], src[:, :, 1, :], nsin.broadcast_to([P, HPG, half]), ALU.mult)
                last = dve.tensor_tensor(tmp[:, :, 1, :], src[:, :, 0, :], sin.broadcast_to([P, HPG, half]),
                                         ALU.mult)
                if tb == 0:
                    link(last)
                else:
                    last.then_inc(s_acc[c % 2], 1)
                    dve.wait_ge(*acc_read(l, c))
                last = dve.tensor_tensor(stage[:, tb, :], stage[:, tb, :], rtmp[:], ALU.add)
                if tb == 0:
                    link(last)
                else:
                    last.then_inc(s_rope, 1)

            def attention(grp, r):
                c0 = group_chunk(grp)
                if grp < 3 and r in (12, 13):
                    rope(c0, 0, r - 12)
                if grp < 3 and r in (20, 21):
                    rope(c0 + 1, 1, r - 20)
                if r in (27, 28, 29):
                    u = r - 27
                    name = ("s", grp, u)
                    bank = UNIT2[name] % 2
                    m = mask_a if grp < 3 else mask_b
                    n, w, m = (HPG, P, m[:, 0:P]) if u == 0 else (2, SEQ, m[:, P:P + SEQ])
                    dve.wait_ge(*unit_full(l, name))
                    p = prob[:, u, :].rearrange("p (h s) -> p h s", s=w)
                    dve.tensor_tensor(p, psS[bank][:].rearrange("p (h s) -> p h s", s=w),
                                      m.unsqueeze(1).broadcast_to([P, n, w]), ALU.add).then_inc(s_sfree[bank], 1)
                    dve.wait_ge(*unit_read(l, name))
                    link(dve.tensor_reduce(mx[:, u, 0:n], p, AX.X, ALU.max))
                    dve.tensor_scalar(mx[:, u, 0:n], mx[:, u, 0:n], -1.0, None, ALU.mult).then_inc(s_max, 1)
                if r == 36:
                    dve.wait_ge(s_exp, at(l, 3 * NGRP, 3 * grp + 3))
                    link(dve.reciprocal(rden[:], den[:]))
                if r in (37, 38):
                    tb = r - 37
                    name = ("o", grp, tb)
                    bank = UNIT2[name] % 2
                    dve.wait_ge(*unit_full(l, name))
                    if tb == 0:
                        dve.wait_ge(*acc_read(l, c0 + 3))
                    else:
                        dve.wait_ge(s_att, at(l, TB * NGRP, TB * grp + 1))
                    t = rtmp[:].rearrange("p (h e) -> p h e", e=HD)
                    dve.tensor_tensor(t, psS[bank][:].rearrange("p (h e) -> p h e", e=HD),
                                      rden[:, tb, :].unsqueeze(2).broadcast_to([P, HPG, HD]), ALU.mult)\
                        .then_inc(s_sfree[bank], 1)
                    dve.wait_ge(*unit_read(l, name))
                    dve.tensor_tensor(z[:, tb, :], z[:, tb, :], rtmp[:], ALU.mult).then_inc(s_att, 1)

            def gate_logits(c):
                j = CHUNKS2[c][1]
                dve.wait_ge(*multiplied(l, c))
                dve.wait_ge(s_grow[j % 2], at(l, 16 * NCW, 16 * (j // 2 + 1)))
                t = (y if j < NCW else gb)[:, :, (j % NCW) * CW:(j % NCW + 1) * CW]
                dve.tensor_tensor(t, acc[c % 2][:], gate_row[:, j % 2, :].unsqueeze(1).broadcast_to([P, TB, CW]),
                                  ALU.add).then_inc(s_acc[c % 2], 1)

            def gated(c):
                j = CHUNKS2[c][1]
                cols = slice((j % NCW) * CW, (j % NCW + 1) * CW)
                dve.wait_ge(*multiplied(l, c))
                dve.wait_ge(s_gate, at(l, 2 * NCW, j + 1))
                t = (y if j < NCW else gb)[:, :, cols]
                dve.tensor_tensor(t, t, acc[c % 2][:], ALU.mult).then_inc(s_acc[c % 2], 1)
                if j >= NCW:
                    dve.wait_ge(*acc_read(l, c))
                    dve.tensor_tensor(y[:, :, cols], y[:, :, cols], t, ALU.add).then_inc(s_y, 1)

            def residual(c):
                j = CHUNKS2[c][1]
                cols = slice(j * CW, (j + 1) * CW)
                dve.wait_ge(*multiplied(l, c))
                dve.scalar_tensor_tensor(out=x[:, :, cols], in0=x[:, :, cols], scalar=ALPHA, in1=acc[c % 2][:],
                                         op0=ALU.mult, op1=ALU.add).then_inc(s_acc[c % 2], 1)
                dve.wait_ge(*acc_read(l, c))
                for tb in range(TB):
                    last = dve.bn_stats(stats[:, tb, j, :], x[:, tb, cols])
                link(last)

            for c in range(nch):
                prev, j = CHUNKS2[c - 1] if c else (None, None)
                for g in range(granules2(c)):
                    if c == 0:
                        fill_lo(("x", g))
                    lo(FIRST2[c] + g)
                    if (c, g) == (F_CHUNK - 1, 1):
                        dve.wait_ge(s_fwh, at(l, 2, 1))
                        dve.tensor_tensor(wflo[:], wf[:], wfhi[:].bitcast(F32), ALU.subtract).then_inc(s_fwh, 1)
                    for grp, r in group_step(c, g):
                        attention(grp, r)
                        if r in (42, 43):
                            fill_lo(("a", grp, r - 42))
                    if prev == "g" and g == 3:
                        gate_logits(c - 1)
                    if prev == "u" and g == 3:
                        gated(c - 1)
                    if prev == "o" and g == 3:
                        residual(c - 1)
                    if prev == "u" and j >= NCW and g == 5:
                        fill_lo(("y", 2 * (j - NCW)))
                        fill_lo(("y", 2 * (j - NCW) + 1))
                    if (c, g) == (F_CHUNK, 4):
                        for i in range(2):
                            bank = UNIT2["f", i] % 2
                            dve.wait_ge(*unit_full(l, ("f", i)))
                            if i == 0:
                                ins = dve.tensor_scalar(fb[:], psS[bank][0:NH2, 0:SEQ], bf[:, 0:1], None, ALU.add)
                            else:
                                ins = dve.tensor_tensor(fb[:], psS[bank][0:NH2, 0:SEQ], fb[:], ALU.add)
                            ins.then_inc(s_sfree[bank], 1)
                            dve.wait_ge(*unit_read(l, ("f", i)))
                        link(dve.tensor_scalar(fe[:], fb[:], -1.0, None, ALU.mult))
                        dve.tensor_tensor(fe[:], fb[:], fe[:], ALU.min)
                        dve.tensor_scalar(fl[:], fb[:], 0.0, None, ALU.min).then_inc(s_f, 1)
                    if (c, g) == (F_CHUNK + 1, 1):
                        dve.wait_ge(s_fln, at(l, 2, 2))
                        link(dve.tensor_tensor(fl[:], fe[:], fl[:], ALU.subtract))
                        dve.tensor_tensor_scan(ncum[:], ones[0:NH2, :], fl[:], 0.0, ALU.mult, ALU.add)\
                            .then_inc(s_cum, 1)
            cols = slice((NCW - 1) * CW, NCW * CW)
            c = nch - 1
            for tb in range(TB):
                dve.wait_ge(*((s_half, l + 1) if tb == 0 else multiplied(l, c)))
                ins = dve.scalar_tensor_tensor(out=x[:, tb, cols], in0=x[:, tb, cols], scalar=ALPHA,
                                               in1=acc[c % 2][:, tb, :], op0=ALU.mult, op1=ALU.add)
                if tb == 0:
                    link(ins)
                else:
                    ins.then_inc(s_acc[c % 2], 1)
                    dve.wait_ge(*acc_read(l, c))
                last = dve.bn_stats(stats[:, tb, NCW - 1, :], x[:, tb, cols])
            link(last)

            dve.wait_ge(s_lnp, at(l, 32, 32))
            dve.memset(rtmp[:, 0:1], 0.0)
            for tb in range(TB):
                last = dve.bn_aggr(mv[:, tb, :], stats[:, tb, :, :])
            last.then_inc(s_var, 1)
            dve.wait_ge(s_std, l + 1)
            link(dve.reciprocal(rstd[:], std[:]))
            dve.scalar_tensor_tensor(out=nmr[:], in0=mv[:, :, 0], scalar=-1.0, in1=rstd[:], op0=ALU.mult, op1=ALU.mult)\
                .then_inc(s_rstd, 1)
            dve.wait_ge(s_rstd, l + 1)
            for start, width in ((0, CW // 2), (CW // 2, CW // 2), *((j * CW, CW) for j in range(1, NV2))):
                cols = slice(start, start + width)
                for tb in range(TB):
                    last = dve.scalar_tensor_tensor(out=x[:, tb, cols], in0=x[:, tb, cols], scalar=mv[:, tb, 0:1],
                                                    in1=gb[:, 0, cols], op0=ALU.subtract, op1=ALU.mult)
                link(last)
                for tb in range(TB):
                    last = dve.scalar_tensor_tensor(out=x[:, tb, cols], in0=x[:, tb, cols], scalar=rstd[:, tb:tb + 1],
                                                    in1=gb[:, 1, cols], op0=ALU.mult, op1=ALU.add)
                last.then_inc(s_xn, width // (CW // 2))
        cols = slice(NV2 * CW, (NV2 + 1) * CW)
        dve.wait_ge(s_xs, (DEPTH - 1) * (NCW - NV2) + 1)
        dve.tensor_tensor(x[:, :, cols], x[:, :, cols], gb[:, 0, cols].unsqueeze(1).broadcast_to([P, TB, CW]),
                          ALU.mult).then_inc(s_self, 1)
        dve.wait_ge(s_self, DEPTH * VLINKS2 + 1)
        dve.tensor_tensor(x[:, :, cols], x[:, :, cols], gb[:, 1, cols].unsqueeze(1).broadcast_to([P, TB, CW]),
                          ALU.add).then_inc(s_last, 1)
        assert links[0] == VLINKS2, links

    @block.tensor
    def _(pe):
        pe.wait_ge(s_mem, 2)

        with pe.Fori(0, DEPTH) as l:

            def fill(name):
                i = FILL2[name]
                pe.wait_ge(s_tfree[i % 2], at(l, NF2 // 2, i // 2 + 1))
                kind, bank = name[0], bank_t(name)
                if kind in "xyaqk":
                    if kind == "x":
                        j = name[1] // 2
                        if j < NV2:
                            pe.wait_ge(s_xn, at(l, 2 * NV2, name[1] + 1))
                        elif name[1] % 2 == 0:
                            pe.wait_ge(s_xnp, at(l, NCW - NV2, j - NV2 + 1))
                        src, col = x, 2 * P * name[1]
                    elif kind == "y":
                        pe.wait_ge(s_y, at(l, NCW, name[1] // 2 + 1))
                        src, col = y, 2 * P * name[1]
                    elif kind == "a":
                        pe.wait_ge(s_att, at(l, TB * NGRP, TB * (name[1] + 1)))
                        src, col = z, 2 * P * name[2]
                    else:
                        if name[1] < 3:
                            pe.wait_ge(s_rope, at(l, NGRP, 2 * name[1] + 1 + (kind == "k")))
                        else:
                            pe.wait_ge(*acc_read(l, group_chunk(name[1]) + (kind == "k")))
                        src, col = stage, 2 * P * name[2]
                    for k in range(2):
                        for tb in range(TB):
                            t = pe.transpose(bank[:, k * SEQ + tb * P:k * SEQ + (tb + 1) * P],
                                             src[:, tb, col + k * P:col + (k + 1) * P], ident[:])
                else:
                    pe.wait_ge(s_exp, at(l, 3 * NGRP, 3 * name[1] + name[2] + 1))
                    for k in range(4):
                        t = pe.transpose(bank[:, k * P:(k + 1) * P], prob[:, name[2], k * P:(k + 1) * P], ident[:])
                t.then_inc(s_tfull, 1)

            def unit(name):
                i = UNIT2[name]
                bank = psS[i % 2]
                pe.wait_ge(s_sfree[i % 2], at(l, NU2 // 2, i // 2 + 1))
                if name[0] == "s":
                    _, grp, u = name
                    if u == 0:
                        for p in range(2):
                            pe.wait_ge(*copied(l, ("k", grp, p)))
                        if grp == 3:
                            pe.wait_ge(s_cum, l + 1)
                    w, tb = (P, 0) if u == 0 else (SEQ, 1)
                    for b in range(CW // w):
                        h = b + max(0, 2 * (u - 1))
                        out = bank[:, b * w:(b + 1) * w]
                        m = pe.matmul(out, qT[:, h, tb * P:(tb + 1) * P], kT[:, h, 0:w], start=True, stop=(grp < 3))
                        if grp >= 3:
                            head = HPG * (grp - 3) + h
                            m = pe.matmul(out, ident[0:NH2, head:head + 1].broadcast_to([NH2, P]), ncum[:, 0:w],
                                          start=False, stop=True)
                elif name[0] == "o":
                    _, grp, tb = name
                    if tb == 0:
                        pe.wait_ge(*acc_read(l, group_chunk(grp) + 2))
                    for p in ((0,), (1, 2))[tb]:
                        pe.wait_ge(*copied(l, ("p", grp, p)))
                    for h in range(HPG):
                        for s in range(tb + 1):
                            u, col = (0, h) if tb == 0 else (1 + h // 2, 2 * (h % 2) + s)
                            m = pe.matmul(bank[:, h * HD:(h + 1) * HD], probT[:, u, col * P:(col + 1) * P],
                                          v[:, s, h * HD:(h + 1) * HD], start=(s == 0), stop=(s == tb))
                else:
                    pe.wait_ge(s_fwh, at(l, 2, 2))
                    half = range(name[1] * KT // 2, (name[1] + 1) * KT // 2)
                    for k in half:
                        for q, (w, a) in enumerate(((wfhi, xhi), (wflo, xhi), (wfhi, xlo))):
                            m = pe.matmul(bank[0:NH2, 0:SEQ], w[:, k, :], a[:, k, :],
                                          start=(k == half[0] and q == 0), stop=(k == half[-1] and q == 2))
                m.then_inc(s_sfull, 1)

            for c, (kind, j) in enumerate(CHUNKS2):
                ahead, alow = (ahi, alo) if kind == "u" else (xhi, xlo)
                for g in range(granules2(c)):
                    for name in fills2(c, g):
                        fill(name)
                    for name in units2(c, g):
                        unit(name)
                    if c == 0:
                        pe.wait_ge(*copied(l, ("x", g)))
                    if (kind, j) == ("o", 0):
                        pe.wait_ge(*copied(l, ("y", g)))
                    if kind == "u" and j % NCW == 0 and g == 0:
                        for p in range(2):
                            pe.wait_ge(*copied(l, ("a", 2 + 3 * (j // NCW), p)))
                    if g == 0:
                        pe.wait_ge(s_acc[c % 2], at(l, nch // 2, c // 2 + 1))
                    n = FIRST2[c] + g
                    pe.wait_ge(s_lo, at(l, GRAN2, n + 1))
                    steps = [(k, tb) for k in range(GK) for tb in range(TB)]
                    if n == GRAN2 - 1:
                        steps = [(k, tb) for tb in range(TB) for k in range(GK)]
                    for k, tb in steps:
                        tile = slice(tb * P, (tb + 1) * P)
                        kk = GK * g + k
                        for q, (a, b) in enumerate(((ahead, whi), (ahead, wlo), (alow, whi))):
                            m = pe.matmul(acc[c % 2][:, tb, :], a[:, kk, tile], b[:, n % SLOTS, k * CW:(k + 1) * CW],
                                          start=(kk == 0 and q == 0),
                                          stop=(kk == GK * granules2(c) - 1 and q == 2))
                        if n == GRAN2 - 1 and (k, tb) == (GK - 1, 0):
                            m.then_inc(s_half, 1)
                    m.then_inc(s_used, 1)


def rope_tables():
    half = HD // 2
    inv = (np.float32(10000.0) ** (-np.arange(half, dtype=np.float32) / half)).astype(np.float32)
    ang = (np.arange(SEQ, dtype=np.float32)[:, None] * inv[None, :]).astype(np.float32).astype(np.float64)
    t = np.stack([np.cos(ang), np.sin(ang), -np.sin(ang)])
    t = np.stack([t * SCALE2, t]).reshape(2, 3, TB, P, half).transpose(3, 0, 1, 2, 4)
    return np.ascontiguousarray(t.astype(np.float32))


def band(weight):
    t, s = np.arange(P)[:, None], np.arange(SEQ)[None, :]
    return np.concatenate([weight(t - s[:, :P]), weight(t + P - s)], axis=1).astype(np.float32)


def constants():
    count = lambda d: sum(((d >= 0) & (d <= w) & (d % r == 0)).astype(int) for w, r in
                          ((128, 1), (512, 4), (2048, 16)))
    return {
        "ident": np.eye(P, dtype=np.float32),
        "mask_a": band(lambda d: np.where(count(d) > 0, np.log(np.maximum(count(d), 1)), NEG)),
        "mask_b": band(lambda d: np.where(d >= 0, 0.0, NEG)),
        "tables": rope_tables(),
    }


def columns(w, start):
    k = w.shape[0] // P
    return w[:, start:start + CW].reshape(k // GK, GK, P, CW).transpose(0, 2, 1, 3).reshape(k // GK, P, GK * CW)


def second_stream(w_in, w_up_a, w_up_b, w_out):
    starts = {"q": 0, "k": W2, "v": 2 * W2, "z": 3 * W2}
    out = []
    for l in range(DEPTH):
        for kind, j in CHUNKS2:
            if kind in starts:
                out.append(columns(w_in[l], starts[kind] + (4 * W2) * (j // 3) + CW * (j % 3)))
            elif kind == "g":
                out.append(columns(w_in[l], 8 * W2 + NH2 + CW * j))
            elif kind == "u":
                out.append(columns((w_up_a if j < NCW else w_up_b)[l], CW * (j % NCW)))
            else:
                out.append(columns(w_out[l], CW * j))
    return np.concatenate(out)


A_HEADS = 16
A_HD = 64
A_W = A_HEADS * A_HD
A_KV = 4
A_KVW = A_KV * A_HD
A_PER = A_HEADS // A_KV
WINDOW = 128
ROT = A_HD // 4
S_W = D // 4
S_G = 8
S_GD = S_W // S_G
G_HEADS = 4
G_DV = 128
G_DK = 64
G_KW = G_HEADS * G_DK
RANK = 16
TAU = 16.0
EPS = 1e-6
LEVELS = (128, 64, 32, 16, 8, 4, 2, 1)
MOD_W = 1024
MOD_N = KT * D // MOD_W
OFF_GATE = A_W + 2 * A_KVW + 2 * S_W + 2 * G_KW + G_HEADS * G_DV
OFF_Z = OFF_GATE + RANK
CHUNKS1 = [("gqk", A_W + 2 * A_KVW + 2 * S_W), ("gv", A_W + 2 * A_KVW + 2 * S_W + 2 * G_KW), ("kv", A_W),
           ("q0", 0), ("q1", CW), ("su", A_W + 2 * A_KVW), ("sv", A_W + 2 * A_KVW + S_W),
           ("z3", OFF_Z + 3 * CW), ("z2", OFF_Z + 2 * CW), ("z0", OFF_Z), ("z1", OFF_Z + CW)]
C1 = {name: i for i, (name, _) in enumerate(CHUNKS1)}
Z_ORDER = (3, 2, 0, 1)
GPC = KT // GK
NCH1 = len(CHUNKS1) + NCW
GRAN1 = NCH1 * GPC
R_OUT = len(CHUNKS1) * GPC
R_SWA = (56, 62, 69, 76)
R_MODG = ((29, 30, 45, 46), (79, 80, 81, 82))
R_MODS = (67, 81)
R_MODA = (99, 116)
HALF_FILL = GPC // 2
R_HALF = 8
AHEAD = SLOTS - 1
R_LEVEL = 24


def place(l, r):
    half = GPC // 2
    if l == 0 and r < 2 * GPC:
        return r // half % 2, half * (r // GPC) + r % half
    return divmod(r, GPC)


def h_fill(l, r):
    c, g = place(l, r)
    return g if c == 0 else None


def h_steps(l, r):
    if l == 0:
        return {0: [2], 1: [3], 2: [4], 3: [5], R_HALF + 1: [6, 7]}.get(r, [])
    return [r + 2] if r + 2 < GPC else []


def fills1(l, r):
    if r < 0:
        return [("h", 0, 0), ("h", 0, 1)]
    out = [("h", l, i) for i in ([0, 1] if l and r == 0 else []) + h_steps(l, r)]
    if r == 16:
        out += [("gq", l), ("gk", l)]
    if r == 30:
        out += [("ak", l)]
    if r in (38, 46):
        out += [("aq", l, (r - 38) // 8, 0), ("aq", l, (r - 38) // 8, 1)]
    for grp, b in enumerate(R_SWA):
        if 4 <= r - b <= 6:
            out += [("p", l, grp, r - b - 4)]
    if r == R_OUT - 2:
        out += [("y", l, 0), ("y", l, 1)]
    if R_OUT <= r < R_OUT + GPC - 2:
        out += [("y", l, r - R_OUT + 2)]
    return out


def units1(l, r):
    if r < 0:
        return [("ms", 0, 0), ("ms", 0, 1), ("ma", 0, 0)]
    out = []
    if (l, r) == (0, R_HALF):
        out += [("ma", 0, 1)]
    if r == 12:
        out += [("cg", l)]
    if r == 16:
        out += [("gl", l)]
    if r == 20:
        out += [("sc", l, -1, 0), ("sc", l, -1, 1)]
    for i in range(len(LEVELS)):
        if r == R_LEVEL + 4 * i:
            out += [("dz", l, i)]
        if r == R_LEVEL + 3 + 4 * i:
            out += [("sc", l, i, 0), ("sc", l, i, 1)]
    if r in R_MODG[l > 0]:
        out += [("mg", l, R_MODG[l > 0].index(r))]
    for grp, b in enumerate(R_SWA):
        if 0 <= r - b <= 2:
            out += [("s", l, grp, r - b)]
        if r - b == 8:
            out += [("o", l, grp)]
    if r in (60, 61):
        out += [("go", l, r - 60)]
    if r in (65, 66):
        out += [("sg", l, r - 65)]
    if l + 1 < DEPTH and r in R_MODS:
        out += [("ms", l + 1, R_MODS.index(r))]
    if l + 1 < DEPTH and r in R_MODA:
        out += [("ma", l + 1, R_MODA.index(r))]
    return out


STEPS1 = [(0, -1)] + [(l, r) for l in range(DEPTH) for r in range(GRAN1)]
FILL1 = {name: i for i, name in enumerate(n for s in STEPS1 for n in fills1(*s))}
UNIT1 = {name: i for i, name in enumerate(n for s in STEPS1 for n in units1(*s))}
THIRDS = [(0, 0), (0, 1)] + [(0, 2), (1, 0), (1, 1), (1, 2)]


def mod_steps():
    steps = {}
    first, last, n = 12, 117, 3 * MOD_N
    for m in range(n):
        steps[0, first + m * (last - first) // n] = (2 + m // MOD_N, m % MOD_N)
    for m in range(MOD_N):
        steps[1, first + 2 * m] = (5, m)
    return steps


MOD_STEPS = mod_steps()
assert DEPTH == 2 and len(MOD_STEPS) == 4 * MOD_N


def mod_step(l, r):
    return MOD_STEPS.get((l, r))


def first_block(nc, ctx, x, rings, ps, dram, ident, s_next=None):
    raw, whi, wlo = rings
    acc, psT, psS = ps

    def sb(name, shape, dt=F32):
        return ctx.enter_context(nc.sbuf_tensor(name, shape, dt))

    def sem(name):
        return ctx.enter_context(nc.semaphore(name))

    hhi = sb("hhi", [P, KT, SEQ], F32R)
    hlo = sb("hlo", [P, KT, SEQ], F32R)
    y = sb("b_y", [P, TB, D])
    macc = sb("macc", [P, D])
    mraw = sb("mraw", [P, 2, MOD_W])
    gain = sb("gain", [P, D])
    stage = sb("b_stage", [P, TB, CW])
    zt = sb("zt", [P, TB, CW])
    scr = sb("scr", [P, 6, CW])
    rt = sb("rt", [P, CW])
    av = sb("av", [P, TB, A_KVW])
    kT = sb("b_kT", [P, A_KV // 2, SEQ])
    qT = sb("b_qT", [P, A_HEADS // 2, SEQ])
    la = sb("la", [P, TB, G_KW])
    st = sb("st", [P, 2, 4, P])
    stx = sb("stx", [P, G_HEADS, P])
    sums = sb("sums", [P, len(LEVELS) + 1, P])
    lmask = sb("lmask", [P, len(LEVELS), P], mybir.dt.uint8)
    wmask = sb("wmask", [P, P + SEQ])
    ones = sb("b_ones", [P, P])
    one = sb("b_one", [P, 1])
    sgw = sb("sgw", [P, S_G, P])
    lnr = sb("lnr", [P, 2, S_W])
    sgb = sb("sgb", [P, S_G])
    gnorm = sb("gnorm", [P, G_DV])
    wg = sb("wg", [P, KT, RANK])
    wghi = sb("wghi", [P, KT, RANK], F32R)
    wglo = sb("wglo", [P, KT, RANK], F32R)
    gup = sb("gup", [RANK, G_KW])
    gbias = sb("gbias", [P, G_KW])
    cgT = sb("cgT", [RANK, SEQ])
    sinks = sb("sinks", [P, A_HEADS])
    cvec = sb("cvec", [P, KT])
    csil = sb("csil", [P, KT])
    gpre = sb("gpre", [P, KT])
    shift = sb("shift", [P, DEPTH, KT])
    scale = sb("scale", [P, DEPTH, KT])
    posi = sb("posi", [P, TB], I32)
    posf = sb("posf", [P, TB])
    invf = sb("invf", [P, ROT // 2])
    ang = sb("ang", [P, 4, TB, ROT // 2])
    cs = sb("cs", [P, 2, TB, ROT // 2])
    mx = sb("b_mx", [P, 3, A_PER])
    snk = sb("snk", [P, TB, A_PER])
    den = sb("b_den", [P, TB, A_PER])
    rden = sb("b_rden", [P, 2, TB, A_PER])
    sq = sb("sq", [P, TB, NCW])
    rms = sb("rms", [P, 2, TB])
    gsq = sb("gsq", [P, 2, TB, G_HEADS])
    stats = sb("b_stats", [P, TB, 6])
    mv = sb("b_mv", [P, TB, 2])
    lstd = sb("lstd", [P, 2, TB])
    eps = sb("b_eps", [P, 1])

    s_w = [sem(f"b_w{i}") for i in range(SLOTS)]
    s_hi = sem("b_hi")
    s_lo = sem("b_lo")
    s_plo = sem("b_plo")
    s_used = sem("b_used")
    s_acc = [sem(f"b_acc{i}") for i in range(2)]
    s_tfull = sem("b_tfull")
    s_thi = sem("b_thi")
    s_tfree = [sem(f"b_tfree{i}") for i in range(2)]
    s_sfull = sem("b_sfull")
    s_sfree = [sem(f"b_sfree{i}") for i in range(2)]
    s_x = sem("b_x")
    s_c = sem("b_c")
    s_ident = sem("b_ident")
    s_gpre = sem("b_gpre")
    s_const = sem("b_const")
    s_late = sem("b_late")
    s_mem = sem("b_mem")
    s_par = sem("b_par")
    s_sgw = sem("b_sgw")
    s_m = [sem(f"b_m{i}") for i in range(6)]
    s_macc = sem("b_macc")
    s_mzero = sem("b_mzero")
    s_mbias = [sem(f"b_mbias{i}") for i in range(4)]
    s_gain = sem("b_gain")
    s_mod = sem("b_mod")
    s_silu = sem("b_silu")
    s_ang = sem("b_ang")
    s_trig = sem("b_trig")
    s_sq = sem("b_sq")
    s_half = sem("b_half")
    s_osq = sem("b_osq")
    s_ssum = sem("b_ssum")
    s_rms = sem("b_rms")
    s_xn = sem("b_xn")
    s_h = sem("b_h")
    s_wg = sem("b_wg")
    s_neg = sem("b_neg")
    s_ln = sem("b_ln")
    s_la = sem("b_la")
    s_gx = sem("b_gx")
    s_rope = sem("b_rope")
    s_max = sem("b_max")
    s_exp = sem("b_exp")
    s_y = sem("b_ypart")
    s_gsq = sem("b_gsq")
    s_grms = sem("b_grms")
    s_var = sem("b_var")
    s_std = sem("b_std")
    s_vn = sem("b_vn")
    s_ym = sem("b_ym")
    s_xd = sem("b_xd")
    s_self = sem("b_self")

    block = ctx.enter_context(nc.Block())
    gv = y[:, :, 0:CW]
    gqT, gkT = y[:, 0, CW:2 * CW], y[:, 1, CW:2 * CW]
    ks = scr[:, 5, :].rearrange("p (b n) -> p b n", b=TB)

    early = 2 * MOD_N
    mod_slots = [mraw[:, 0, :], mraw[:, 1, :], stage[:].rearrange("p b n -> p (b n)")]
    mod_slots += [scr[:, 2 * i:2 * i + 2, :].rearrange("p a n -> p (a n)") for i in range(3)]

    def junk(l):
        tile = scr[:].rearrange("p a n -> p (a n)") if l else gain[:]
        return tile.bitcast(mybir.dt.bfloat16)

    def macc_of(q):
        return qT[:].rearrange("p h t -> p (h t)") if q == 0 else macc[:]

    def mod_place(n):
        return n % len(mod_slots) if n < early else n % 2

    def mod_slot(n):
        k = mod_place(n)
        return mod_slots[k], (k, sum(mod_place(m) == k for m in range(n + 1)))

    def mod_before(n):
        return max((m for m in range(n) if mod_place(m) == mod_place(n)), default=None)

    def need(eng, sv):
        if sv[1] > 0:
            eng.wait_ge(*sv)

    def chunk(l, name):
        return l * NCH1 + (len(CHUNKS1) + name if isinstance(name, int) else C1[name])

    def multiplied(c):
        l, k = divmod(c, NCH1)
        return s_used, GRAN1 * l + max(r for r in range(GRAN1) if place(l, r)[0] == k) + 1

    def split(n):
        return (s_plo, n + 1) if n < R_HALF else (s_lo, n - R_HALF + 1)

    def acc_read(c):
        return s_acc[c % 2], c // 2 + 1

    def unit_full(name):
        return s_sfull, UNIT1[name] + 1

    def unit_read(name):
        return s_sfree[UNIT1[name] % 2], UNIT1[name] // 2 + 1

    def bank_s(name):
        return psS[UNIT1[name] % 2]

    def filled(name):
        return s_tfull, FILL1[name] + 1

    def copied(name):
        return s_tfree[FILL1[name] % 2], FILL1[name] // 2 + 1

    def bank_t(name):
        return psT[FILL1[name] % 2]

    def split_index(name):
        return GPC * (2 * name[1] + (name[0] == "y")) + name[2]

    def exp_index(l, grp, u):
        return 3 * (A_KV * l + grp) + u + 1

    n_par = 9

    @block.sync
    def _(sp):
        def mod(q, i):
            n = MOD_N * q + i
            if mod_before(n) is not None:
                sp.wait_ge(s_macc, mod_before(n) + 1)
            l, third = THIRDS[q]
            slot, use = mod_slot(n)
            sp.dma_start(slot, dram["w_mod"][l, third, i]).then_inc(s_m[use[0]], 16)

        def weights(n):
            if n >= SLOTS:
                sp.wait_ge(*split(n - SLOTS))
            sp.dma_start(raw[:, n % SLOTS, :], dram["w1"][n]).then_inc(s_w[n % SLOTS], 16)

        for i in range(MOD_N):
            if i == MOD_N // 2:
                sp.dma_start(x[:], dram["x"].rearrange("(b p) n -> p b n", p=P)).then_inc(s_x, 16)
            mod(0, i)
        beside = {15: 0, 16: 1, 17: 2, 18: 3, 22: 4, 24: 5, 26: 6, 28: 7, 31: 8}
        for i in range(MOD_N):
            mod(1, i)
            if i in beside:
                weights(beside[i])
        for n in range(len(beside)):
            if mod_step(0, n):
                mod(*mod_step(0, n))
        for n in range(len(beside), DEPTH * GRAN1):
            step = mod_step(*divmod(n, GRAN1))
            weights(n)
            if step:
                mod(*step)
        for n in range(SLOTS if s_next else 0):
            sp.wait_ge(*split(DEPTH * GRAN1 - SLOTS + n))
            sp.dma_start(raw[:, n, :], dram["w"][n]).then_inc(s_next[n], 16)

    @block.gpsimd
    def _(pool):
        def mod_bias(h):
            q, half = divmod(h, 2)
            l, third = THIRDS[q]
            cols = slice(half * MOD_W, (half + 1) * MOD_W)
            pool.wait_ge(s_mzero, h + 1)
            pool.dma_start(macc_of(q)[0:1, cols], dram["b_mod"][l, third:third + 1, cols]).then_inc(s_mbias[h % 4], 16)

        pool.dma_start(cvec[:], dram["c"]).then_inc(s_c, 16)
        for h in range(4):
            mod_bias(h)
        pool.dma_start(ident[:], dram["ident"]).then_inc(s_ident, 16)
        for tile, name in ((posi, "positions"), (zt[:].rearrange("p b (i n) -> p (b i) n", n=P), "lmask")):
            pool.dma_start(tile[:], dram[name]).then_inc(s_const, 16)
        pool.dma_start(invf[:], dram["inv_freq"].partition_broadcast(P)).then_inc(s_const, 16)

        def parameters(l):
            if l:
                pool.wait_ge(s_ym, NCW * l)
            pool.dma_start(gpre[:], dram["g_pre"][l]).then_inc(s_gpre, 16)
            if l == 0:
                for n in range(R_HALF):
                    pool.wait_ge(s_hi, n + 1)
                    if n >= SLOTS:
                        pool.wait_ge(s_used, n - SLOTS + 1)
                    pool.tensor_tensor(wlo[:, n % SLOTS, :], raw[:, n % SLOTS, :], whi[:, n % SLOTS, :].bitcast(F32),
                                       ALU.subtract).then_inc(s_plo, 1)
            pool.wait_ge(s_macc, early if l == 0 else MOD_N * (THIRDS.index((l, 1)) + 1))
            pool.dma_start(wg[:], dram["wg"][l]).then_inc(s_par, 16)
            pool.dma_start(gup[:], dram["gate_up"][l]).then_inc(s_par, 16)
            pool.dma_start(gbias[:], dram["b_gate"][l].partition_broadcast(P)).then_inc(s_par, 16)
            pool.dma_start(gnorm[:], dram["gnorm"][l].partition_broadcast(P)).then_inc(s_par, 16)
            pool.dma_start(sinks[:], dram["sinks"][l].partition_broadcast(P)).then_inc(s_par, 16)
            pool.dma_start(sgb[:], dram["sg_b"][l]).then_inc(s_par, 16)
            pool.dma_start(lnr[:, 0, :], dram["sg_ln_g"][l].partition_broadcast(P)).then_inc(s_par, 16)
            pool.dma_start(lnr[:, 1, :], dram["sg_ln_b"][l].partition_broadcast(P)).then_inc(s_par, 16)
            pool.dma_start(sgw[:], dram["sg_w"][l]).then_inc(s_par, 16)
            if l == 0:
                pool.dma_start(sums[:], dram["sums"]).then_inc(s_late, 16)
                pool.dma_start(wmask[:], dram["mask_w"]).then_inc(s_late, 16)
            pool.wait_ge(s_par, 16 * n_par * (l + 1))
            pool.affine_select(out=sgw[:], in_=sgw[:], compare_op=ALU.is_ge, fill=0.0, base=0,
                               pattern=[[0, S_G], [1, P]], channel_multiplier=-1).then_inc(s_sgw, 1)

        parameters(0)
        for l in range(DEPTH):
            if l:
                pool.wait_ge(s_xd, NCW * l)
            pool.dma_start(gain[:], dram["g_post"][l].partition_broadcast(P)).then_inc(s_gain, 16)
            for third in range(3 if l + 1 < DEPTH else 1):
                q = 2 + 3 * l + third
                mod_bias(2 * q)
                mod_bias(2 * q + 1)
            if l + 1 < DEPTH:
                parameters(l + 1)

    @block.scalar
    def _(act):
        act.wait_ge(s_c, 16)
        act.activation(csil[:], cvec[:], ACT.Silu).then_inc(s_silu, 1)

        def hi(n):
            act.wait_ge(s_w[n % SLOTS], 16 * (n // SLOTS + 1))
            if n >= SLOTS:
                act.wait_ge(s_used, n - SLOTS + 1)
            act.activation(whi[:, n % SLOTS, :], raw[:, n % SLOTS, :], ACT.Copy).then_inc(s_hi, 1)

        def fill_copy(name, dst, rows=P, n=CW):
            act.wait_ge(*filled(name))
            act.activation(dst, bank_t(name)[0:rows, 0:n], ACT.Copy).then_inc(s_tfree[FILL1[name] % 2], 1)

        def fill_hi(name):
            if name[0] == "h":
                act.wait_ge(*copied(name))
                src = zt[:, name[2] % 2, :]
            else:
                act.wait_ge(*filled(name))
                act.wait_ge(s_used, GRAN1 * name[1] + R_OUT - GPC + y_tile(name[2]) // GK + 1)
                src = bank_t(name)[:]
            k = 2 * name[2] if name[0] == "h" else y_tile(name[2])
            act.activation(hhi[:, k:k + 2, :], src.rearrange("p (k t) -> p k t", k=2), ACT.Copy).then_inc(s_thi, 1)

        def root(n):
            act.wait_ge(s_ssum, n + 1)
            act.activation(rms[:, 0, :], rms[:, 1, :], ACT.Sqrt, scale=1.0 / D, bias=eps[:, 0:1]).then_inc(s_rms, 1)

        def x_squares(l):
            for j in range(NCW):
                if l:
                    act.wait_ge(s_xd, NCW * (l - 1) + j + 1)
                for tb in range(TB):
                    last = act.activation(junk(l)[:, (TB * j + tb) * CW:(TB * j + tb + 1) * CW],
                                          x[:, tb, j * CW:(j + 1) * CW], ACT.Square, accum_out=sq[:, tb, j:j + 1])
                last.then_inc(s_sq, 1)

        def out_chunk(l, j):
            c = chunk(l, j)
            for tb in range(TB):
                if tb == 0 and j == NCW - 1:
                    act.wait_ge(s_half, l + 1)
                else:
                    act.wait_ge(*multiplied(c))
                k = TB * j + tb
                act.activation(junk(1)[:, k * CW:(k + 1) * CW], acc[c % 2][:, tb, :], ACT.Square,
                               accum_out=sq[:, tb, j:j + 1]).then_inc(s_osq, 1)

        act.wait_ge(s_mem, 2)
        act.wait_ge(s_x, 16)
        for l in range(DEPTH):
            x_squares(l)
            root(2 * l)
            if l == 0:
                act.wait_ge(s_ang, 1)
                act.activation(cs[:].rearrange("p a b n -> p (a b n)"), ang[:, 0:2].rearrange("p a b n -> p (a b n)"),
                               ACT.Sin).then_inc(s_trig, 1)
            for r in range(GRAN1):
                if h_fill(l, r) is not None:
                    fill_hi(("h", l, h_fill(l, r)))
                if l == 0 or r >= AHEAD:
                    hi(GRAN1 * l + r)
                if R_OUT <= r < R_OUT + GPC:
                    fill_hi(("y", l, r - R_OUT))
                if r == 10:
                    act.wait_ge(s_par, 16 * n_par * (l + 1))
                    act.activation(wghi[:], wg[:], ACT.Copy).then_inc(s_wg, 1)
                if r == 15:
                    c = chunk(l, "gqk")
                    act.wait_ge(*multiplied(c))
                    act.activation(stage[:, :, 0:G_KW], acc[c % 2][:, :, 0:G_KW], ACT.Copy, scale=G_DK ** -0.5)
                    act.activation(stage[:, :, G_KW:], acc[c % 2][:, :, G_KW:], ACT.Copy).then_inc(s_acc[c % 2], 1)
                if r == 15:
                    act.wait_ge(*unit_full(("cg", l)))
                    act.activation(cgT[:], bank_s(("cg", l))[0:RANK, 0:SEQ], ACT.Copy)\
                        .then_inc(s_sfree[UNIT1["cg", l] % 2], 1)
                if r == 19:
                    fill_copy(("gq", l), gqT)
                    fill_copy(("gk", l), gkT)
                if r == 20:
                    act.wait_ge(s_neg, l + 1)
                    act.activation(zt[:, 0, :], zt[:, 0, :], ACT.Exp).then_inc(s_ln, 1)
                    act.wait_ge(s_ln, 2 * l + 1)
                    act.activation(zt[:, 0, :], zt[:, 0, :], ACT.Ln, bias=1.0).then_inc(s_ln, 1)
                if r == 19:
                    c = chunk(l, "gv")
                    act.wait_ge(*multiplied(c))
                    act.activation(gv, acc[c % 2][:], ACT.Copy).then_inc(s_acc[c % 2], 1)
                for i in range(len(LEVELS)):
                    if r == R_LEVEL + 3 + 4 * i:
                        if i >= 2:
                            act.wait_ge(*unit_full(("sc", l, i - 2, 1)))
                        act.wait_ge(*unit_full(("dz", l, i)))
                        act.activation(zt[:, i % 2, :], bank_s(("dz", l, i))[:], ACT.Exp)\
                            .then_inc(s_sfree[UNIT1["dz", l, i] % 2], 1)
                if r == 27:
                    c = chunk(l, "kv")
                    act.wait_ge(*multiplied(c))
                    act.activation(ks, acc[c % 2][:, :, 0:A_KVW], ACT.Copy)
                    act.activation(av[:], acc[c % 2][:, :, A_KVW:], ACT.Copy).then_inc(s_acc[c % 2], 1)
                if r == 33:
                    fill_copy(("ak", l), kT[:].rearrange("p k t -> p (k t)"))
                if r in (35, 43):
                    c = chunk(l, "q0" if r == 35 else "q1")
                    if r == 43:
                        act.wait_ge(*filled(("aq", l, 0, 1)))
                    act.wait_ge(*multiplied(c))
                    dst = stage[:].rearrange("p b (i s e) -> p b i s e", s=2, e=A_HD)
                    for s in range(2):
                        last = act.activation(dst[:, :, :, s, :], acc[c % 2][:, :, s * A_KVW:(s + 1) * A_KVW]
                                              .rearrange("p b (i e) -> p b i e", e=A_HD), ACT.Copy,
                                              scale=A_HD ** -0.5)
                    last.then_inc(s_acc[c % 2], 1)
                if r in (41, 49):
                    i = (r - 41) // 8
                    for k in range(2):
                        a = 4 * i + 2 * k
                        fill_copy(("aq", l, i, k), qT[:, a:a + 2, :].rearrange("p h t -> p (h t)"))
                for grp, b in enumerate(R_SWA):
                    if 4 <= r - b <= 6:
                        u = r - b - 4
                        act.wait_ge(s_max, exp_index(l, grp, u))
                        w = P if u == 0 else SEQ
                        h0, n = max(0, 2 * (u - 1)), CW // w
                        act.activation(snk[:, min(u, 1), h0:h0 + n], snk[:, min(u, 1), h0:h0 + n], ACT.Exp)
                        for i in range(n):
                            p = act.activation(scr[:, u, i * w:(i + 1) * w], scr[:, u, i * w:(i + 1) * w], ACT.Exp,
                                               bias=mx[:, u, i:i + 1], accum_out=den[:, min(u, 1), h0 + i:h0 + i + 1])
                        p.then_inc(s_exp, 1)
                    if 7 <= r - b <= 9:
                        fill_copy(("p", l, grp, r - b - 7), scr[:, 3 + r - b - 7, :])
                if r == 51:
                    c = chunk(l, "su")
                    act.wait_ge(*multiplied(c))
                    act.activation(y[:, :, 2 * CW:3 * CW], acc[c % 2][:], ACT.Gelu_apprx_tanh)\
                        .then_inc(s_acc[c % 2], 1)
                if r == 59:
                    c = chunk(l, "sv")
                    act.wait_ge(*multiplied(c))
                    act.wait_ge(*unit_full(("sc", l, len(LEVELS) - 1, 1)))
                    act.activation(zt[:], acc[c % 2][:], ACT.Gelu_apprx_tanh).then_inc(s_acc[c % 2], 1)
                if r == 61:
                    act.wait_ge(s_var, l + 1)
                    act.activation(lstd[:, 0, :], mv[:, :, 1], ACT.Sqrt, bias=eps[:, 0:1]).then_inc(s_std, 1)
                if r in (63, 64):
                    tb = r - 63
                    act.wait_ge(*unit_full(("go", l, tb)))
                    act.activation(y[:, tb, 3 * CW:], bank_s(("go", l, tb))[:], ACT.Copy)\
                        .then_inc(s_sfree[UNIT1["go", l, tb] % 2], 1)
                if r == 67:
                    act.wait_ge(s_gsq, l + 1)
                    act.activation(gsq[:, 1], gsq[:, 0], ACT.Sqrt, scale=1.0 / G_DV, bias=eps[:, 0:1])\
                        .then_inc(s_grms, 1)
                if r in (69, 75, 83, 91):
                    i = (69, 75, 83, 91).index(r)
                    c = chunk(l, f"z{Z_ORDER[i]}")
                    act.wait_ge(*multiplied(c))
                    if i == 0:
                        act.wait_ge(*unit_full(("sg", l, 1)))
                    else:
                        act.wait_ge(s_ym, NCW * l + i)
                    act.activation(zt[:], acc[c % 2][:], ACT.Silu).then_inc(s_acc[c % 2], 1)
                if r >= R_OUT + GPC and (r - R_OUT) % GPC == 3:
                    out_chunk(l, (r - R_OUT) // GPC - 1)
            for r in range(AHEAD if l + 1 < DEPTH else 0):
                hi(GRAN1 * (l + 1) + r)
            act.activation(one[:], eps[:, 0:1], ACT.Sqrt)
            out_chunk(l, NCW - 1)
            root(2 * l + 1)

    @block.vector
    def _(dve):
        links = [0]

        def link(ins):
            links[0] += 1
            ins.then_inc(s_self, 1)
            dve.wait_ge(s_self, links[0])

        def lo(n):
            dve.wait_ge(s_hi, n + 1)
            dve.tensor_tensor(wlo[:, n % SLOTS, :], raw[:, n % SLOTS, :], whi[:, n % SLOTS, :].bitcast(F32),
                              ALU.subtract).then_inc(s_lo, 1)

        def fill_lo(name):
            dve.wait_ge(s_thi, split_index(name) + 1)
            if name[0] == "h":
                k, src = 2 * name[2], zt[:, name[2] % 2, :]
                signal = s_h
            else:
                k, src = y_tile(name[2]), bank_t(name)[:]
                signal = s_tfree[FILL1[name] % 2]
            dve.tensor_tensor(hlo[:, k:k + 2, :], src.rearrange("p (k t) -> p k t", k=2),
                              hhi[:, k:k + 2, :].bitcast(F32), ALU.subtract).then_inc(signal, 1)

        def fill_mod(l, i):
            name = ("h", l, i)
            dve.wait_ge(*filled(name))
            if i >= 2:
                dve.wait_ge(s_h, GPC * l + i - 1)
            for k in range(2):
                kt = 2 * i + k
                last = dve.tensor_scalar(zt[:, i % 2, k * SEQ:(k + 1) * SEQ], bank_t(name)[:, k * SEQ:(k + 1) * SEQ],
                                         scale[:, l, kt:kt + 1], shift[:, l, kt:kt + 1], ALU.mult, ALU.add)
            last.then_inc(s_tfree[FILL1[name] % 2], 1)

        def mod_zero(h):
            q, half = divmod(h, 2)
            if q >= 2:
                l, third = THIRDS[q - 1]
                dve.wait_ge(*unit_full((("ms", l, half), ("ma", l, half), ("mg", l, 2 * half + 1))[third]))
            dve.memset(macc_of(q)[:, half * MOD_W:(half + 1) * MOD_W], 0.0).then_inc(s_mzero, 1)

        def mod(q, i):
            n = MOD_N * q + i
            half, kt = divmod(i, KT)
            cols = slice(half * MOD_W, (half + 1) * MOD_W)
            h = 2 * q + half
            if kt == 0:
                dve.wait_ge(s_mbias[h % 4], 16 * (h // 4 + 1))
            if kt:
                dve.wait_ge(s_macc, n)
            slot, (k, uses) = mod_slot(n)
            dve.wait_ge(s_m[k], 16 * uses)
            dve.scalar_tensor_tensor(out=macc_of(q)[:, cols], in0=slot, scalar=csil[:, kt:kt + 1],
                                     in1=macc_of(q)[:, cols], op0=ALU.mult, op1=ALU.add).then_inc(s_macc, 1)

        def mod_shift(l, half):
            name = ("ms", l, half)
            kts = slice(half * KT // 2, (half + 1) * KT // 2)
            dve.wait_ge(*unit_full(name))
            dve.tensor_copy(shift[:, l, kts], bank_s(name)[:, kts]).then_inc(s_sfree[UNIT1[name] % 2], 1)

        def mod_scale(l, half):
            name = ("ma", l, half)
            kts = slice(half * KT // 2, (half + 1) * KT // 2)
            dve.wait_ge(*unit_full(name))
            dve.wait_ge(s_gpre, 16 * (l + 1))
            dve.scalar_tensor_tensor(out=scale[:, l, kts], in0=bank_s(name)[:, kts], scalar=1.0, in1=gpre[:, kts],
                                     op0=ALU.add, op1=ALU.mult).then_inc(s_sfree[UNIT1[name] % 2], 1)
            dve.wait_ge(*unit_read(name))

        def inverse_root(n):
            dve.wait_ge(s_rms, n + 1)
            link(dve.reciprocal(rms[:, 1, :], rms[:, 0, :]))

        def row_squares(l):
            dve.wait_ge(s_sq, NCW * (l + 1))
            dve.tensor_reduce(rms[:, 1, :], sq[:], AX.X, ALU.add).then_inc(s_ssum, 1)

        def normalise(j):
            cols = slice(j * CW, (j + 1) * CW)
            for tb in range(TB):
                last = dve.tensor_scalar(y[:, tb, cols], x[:, tb, cols], rms[:, 1, tb:tb + 1], None, ALU.mult)
            last.then_inc(s_xn, 1)

        def gained(l, j):
            cols = slice(j * CW, (j + 1) * CW)
            c = chunk(l, j)
            for tb in range(TB):
                dve.wait_ge(s_osq, TB * (NCW * l + j) + tb + 1)
                if (j, tb) == (NCW - 1, TB - 1):
                    dve.tensor_reduce(rms[:, 1, :], sq[:], AX.X, ALU.add).then_inc(s_ssum, 1)
                last = dve.tensor_tensor(y[:, tb, cols], acc[c % 2][:, tb, :], gain[:, cols], ALU.mult)
            last.then_inc(s_acc[c % 2], 1)

        def rope(src, heads):
            half = ROT // 2
            v4 = src.rearrange("p b (h e) -> p b h e", e=A_HD)
            t1, t2 = v4[:, :, :, 0:half], v4[:, :, :, half:ROT]
            n = TB * heads * half
            tmp = [rt[:, i * n:(i + 1) * n].rearrange("p (b h e) -> p b h e", b=TB, e=half) for i in range(4)]
            cos, sin = (cs[:, i].unsqueeze(2).broadcast_to([P, TB, heads, half]) for i in range(2))
            dve.tensor_tensor(tmp[0], t1, cos, ALU.mult)
            dve.tensor_tensor(tmp[1], t2, sin, ALU.mult)
            dve.tensor_tensor(tmp[2], t2, cos, ALU.mult)
            link(dve.tensor_tensor(tmp[3], t1, sin, ALU.mult))
            dve.tensor_tensor(t1, tmp[0], tmp[1], ALU.subtract)
            link(dve.tensor_tensor(t2, tmp[2], tmp[3], ALU.add))
            dve.memset(rt[:, 0:1], 0.0).then_inc(s_rope, 1)

        def scores(l, grp, u):
            name = ("s", l, grp, u)
            n, w, m = (A_PER, P, wmask[:, 0:P]) if u == 0 else (2, SEQ, wmask[:, P:P + SEQ])
            h0 = max(0, 2 * (u - 1))
            sink = sinks[:, A_PER * grp + h0:A_PER * grp + h0 + n]
            if (l, grp, u) == (0, 0, 0):
                dve.wait_ge(s_late, 32)
            dve.wait_ge(*unit_full(name))
            p = scr[:, u, :].rearrange("p (h s) -> p h s", s=w)
            dve.tensor_tensor(p, bank_s(name)[:].rearrange("p (h s) -> p h s", s=w),
                              m.unsqueeze(1).broadcast_to([P, n, w]), ALU.add).then_inc(s_sfree[UNIT1[name] % 2], 1)
            dve.wait_ge(*unit_read(name))
            link(dve.tensor_reduce(mx[:, u, 0:n], p, AX.X, ALU.max))
            link(dve.tensor_tensor(mx[:, u, 0:n], mx[:, u, 0:n], sink, ALU.max))
            link(dve.tensor_scalar(mx[:, u, 0:n], mx[:, u, 0:n], -1.0, None, ALU.mult))
            dve.tensor_tensor(snk[:, min(u, 1), h0:h0 + n], sink, mx[:, u, 0:n], ALU.add).then_inc(s_max, 1)

        def denominators(l, grp):
            dve.wait_ge(s_exp, exp_index(l, grp, 2))
            link(dve.tensor_tensor(den[:], den[:], snk[:], ALU.add))
            link(dve.reciprocal(rden[:, grp % 2], den[:]))

        def attended(l, grp):
            name = ("o", l, grp)
            dve.wait_ge(*unit_full(name))
            if grp == 0:
                dve.wait_ge(*unit_full(("go", l, 1)))
            for tb in range(TB):
                last = dve.tensor_tensor(y[:, tb, grp * A_KVW:(grp + 1) * A_KVW].rearrange("p (h e) -> p h e", e=A_HD),
                                         bank_s(name)[:, tb * A_KVW:(tb + 1) * A_KVW]
                                         .rearrange("p (h e) -> p h e", e=A_HD),
                                         rden[:, grp % 2, tb, :].unsqueeze(2).broadcast_to([P, A_PER, A_HD]), ALU.mult)
            last.then_inc(s_sfree[UNIT1[name] % 2], 1)
            dve.wait_ge(*unit_read(name))

        def angles():
            tau = 2.0 * np.pi
            parts = [6.28125]
            parts.append(float(np.float32(np.round((tau - parts[0]) * 2 ** 21) / 2 ** 21)))
            parts.append(float(np.float32(tau - parts[0] - parts[1])))
            magic = 1.5 * 2.0 ** 23
            link(dve.tensor_copy(posf[:], posi[:]))
            for tb in range(TB):
                last = dve.tensor_scalar(ang[:, 0, tb, :], invf[:], posf[:, tb:tb + 1], None, ALU.mult)
            link(last)
            a, n, r, t = (ang[:, i].rearrange("p b e -> p (b e)") for i in (0, 1, 2, 3))
            link(dve.tensor_scalar(n, a, 1.0 / tau, None, ALU.mult))
            link(dve.tensor_scalar(t, n, magic, None, ALU.add))
            link(dve.tensor_scalar(n, t, magic, None, ALU.subtract))
            link(dve.scalar_tensor_tensor(out=r, in0=n, scalar=-parts[0], in1=a, op0=ALU.mult, op1=ALU.add))
            link(dve.scalar_tensor_tensor(out=t, in0=n, scalar=-parts[1], in1=r, op0=ALU.mult, op1=ALU.add))
            link(dve.scalar_tensor_tensor(out=r, in0=n, scalar=-parts[2], in1=t, op0=ALU.mult, op1=ALU.add))
            link(dve.tensor_scalar(n, r, 3.1415925, -3.1415925, ALU.min, ALU.max))
            link(dve.tensor_scalar(t, n, -1.0, None, ALU.mult))
            link(dve.tensor_tensor(t, t, n, ALU.max))
            dve.tensor_scalar(a, t, -1.0, float(np.pi / 2), ALU.mult, ALU.add).then_inc(s_ang, 1)

        dve.memset(ones[:], 1.0).then_inc(s_mem, 1)
        dve.memset(eps[:], EPS).then_inc(s_mem, 1)
        for h in range(4):
            mod_zero(h)
        dve.wait_ge(s_silu, 1)
        for i in range(MOD_N):
            mod(0, i)
            if i == 8:
                dve.wait_ge(s_mem, 2)
                dve.wait_ge(s_const, 48)
                link(dve.tensor_copy(lmask[:].rearrange("p i n -> p (i n)"), zt[:].rearrange("p b n -> p (b n)")))
                angles()
        for i in range(MOD_N // 2):
            mod(1, i)
            if i == 1:
                row_squares(0)
            if i == 3:
                inverse_root(0)
            if 4 <= i < 4 + NCW:
                normalise(i - 4)
        mod_shift(0, 0)
        mod_shift(0, 1)
        mod_scale(0, 0)

        for l in range(DEPTH):
            if l:
                row_squares(l)
                inverse_root(2 * l)
                for j in range(2):
                    normalise(j)
            for r in range(GRAN1):
                if r == 0:
                    fill_mod(l, 0)
                    fill_mod(l, 1)
                if h_fill(l, r) is not None:
                    fill_lo(("h", l, h_fill(l, r)))
                if r >= (AHEAD if l else R_HALF):
                    lo(GRAN1 * l + r)
                if R_OUT <= r < R_OUT + GPC:
                    fill_lo(("y", l, r - R_OUT))
                if l == 0 and r < R_HALF:
                    n = MOD_N // 2 // R_HALF
                    for i in range(MOD_N // 2 + r * n, MOD_N // 2 + (r + 1) * n):
                        mod(1, i)
                for i in h_steps(l, r):
                    if l or i not in (HALF_FILL, HALF_FILL + 1):
                        fill_mod(l, i)
                if (l, r + 1) == (0, R_HALF):
                    mod_scale(0, 1)
                    fill_mod(l, HALF_FILL)
                    fill_mod(l, HALF_FILL + 1)
                if (l, r) == (0, R_HALF):
                    mod_zero(4)
                    mod_zero(5)
                if l and r < 2:
                    normalise(2 + r)
                if r == 11:
                    dve.wait_ge(s_wg, 2 * l + 1)
                    dve.tensor_tensor(wglo[:], wg[:], wghi[:].bitcast(F32), ALU.subtract).then_inc(s_wg, 1)
                if r == 19:
                    name = ("gl", l)
                    flat = la[:].rearrange("p b n -> p (b n)")
                    dve.wait_ge(*unit_full(name))
                    dve.tensor_tensor(la[:], bank_s(name)[:].rearrange("p (b n) -> p b n", b=TB),
                                      gbias[:].unsqueeze(1).broadcast_to([P, TB, G_KW]), ALU.add)\
                        .then_inc(s_sfree[UNIT1[name] % 2], 1)
                    dve.wait_ge(*unit_read(name))
                    link(dve.tensor_scalar(zt[:, 0, :], flat, -1.0, None, ALU.mult))
                    dve.tensor_tensor(zt[:, 0, :], zt[:, 0, :], flat, ALU.min).then_inc(s_neg, 1)
                    dve.wait_ge(s_neg, l + 1)
                    link(dve.tensor_scalar(flat, flat, 0.0, 1.0 / TAU, ALU.min, ALU.mult))
                if r == 21:
                    flat = la[:].rearrange("p b n -> p (b n)")
                    dve.wait_ge(s_ln, 2 * l + 2)
                    dve.scalar_tensor_tensor(out=flat, in0=zt[:, 0, :], scalar=-1.0 / TAU, in1=flat,
                                             op0=ALU.mult, op1=ALU.add).then_inc(s_la, 1)
                    link(dve.memset(st[:], 0.0))
                for i in range(-1, len(LEVELS)):
                    if i >= 0 and r == R_LEVEL + 4 + 4 * i:
                        m = LEVELS[i]
                        dve.wait_ge(*unit_read(("dz", l, i)))
                        for src, half in ((gqT, 1), (gkT, 0)):
                            a = zt[:, i % 2, :].rearrange("p (n s m) -> p n s m", s=2, m=m)[:, :, half, :]
                            b = src.rearrange("p (n s m) -> p n s m", s=2, m=m)[:, :, half, :]
                            last = dve.tensor_tensor(a, a, b, ALU.mult)
                        last.then_inc(s_gx, 1)
                    if r == (R_LEVEL + 6 + 4 * i if i >= 0 else 23):
                        for odd in range(2):
                            name = ("sc", l, i, odd)
                            bank = bank_s(name)
                            dve.wait_ge(*unit_full(name))
                            if i == 0:
                                dst = stx[:].rearrange("p (k o) t -> p k o t", o=2)[:, :, odd, :]
                                ins = dve.tensor_copy(dst, bank[:, 0:2 * P].rearrange("p (k t) -> p k t", t=P))
                            else:
                                mask = lmask[:, i if i > 0 else 0, :].unsqueeze(1).broadcast_to([P, 4, P])
                                ins = dve.copy_predicated(st[:, odd], mask, bank[:].rearrange("p (k t) -> p k t", t=P))
                            ins.then_inc(s_sfree[UNIT1[name] % 2], 1)
                            dve.wait_ge(*unit_read(name))
                if r == 28:
                    dve.wait_ge(*acc_read(chunk(l, "kv")))
                    rope(ks, A_KV)
                if r in (36, 44):
                    dve.wait_ge(*acc_read(chunk(l, "q0" if r == 36 else "q1")))
                    rope(stage[:], A_HEADS // 2)
                if r - 3 in R_MODG[l > 0]:
                    j = R_MODG[l > 0].index(r - 3)
                    name = ("mg", l, j)
                    dve.wait_ge(s_gain, 16 * (l + 1))
                    dve.wait_ge(*unit_full(name))
                    dve.tensor_tensor(gain[:, j * CW:(j + 1) * CW], gain[:, j * CW:(j + 1) * CW], bank_s(name)[:],
                                      ALU.mult).then_inc(s_sfree[UNIT1[name] % 2], 1)
                    if j % 2 and l + 1 < DEPTH:
                        mod_zero(2 * THIRDS.index((l + 1, 0)) + j // 2)
                if l + 1 < DEPTH and r - 3 in R_MODS:
                    half = R_MODS.index(r - 3)
                    mod_shift(l + 1, half)
                    mod_zero(2 * THIRDS.index((l + 1, 1)) + half)
                if l + 1 < DEPTH and r - 3 in R_MODA:
                    half = R_MODA.index(r - 3)
                    mod_scale(l + 1, half)
                    mod_zero(2 * THIRDS.index((l + 1, 2)) + half)
                for grp, b in enumerate(R_SWA):
                    if 3 <= r - b <= 5:
                        scores(l, grp, r - b - 3)
                    if r - b == 7:
                        denominators(l, grp)
                    if r - b == 11:
                        attended(l, grp)
                if r == 60:
                    dve.wait_ge(*acc_read(chunk(l, "sv")))
                    for tb in range(TB):
                        last = dve.bn_stats(stats[:, tb, :], zt[:, tb, :])
                    link(last)
                    for tb in range(TB):
                        last = dve.bn_aggr(mv[:, tb, :], stats[:, tb, :])
                    last.then_inc(s_var, 1)
                if r == 62:
                    dve.wait_ge(s_std, l + 1)
                    link(dve.reciprocal(lstd[:, 1, :], lstd[:, 0, :]))
                    for tb in range(TB):
                        last = dve.tensor_scalar(zt[:, tb, :], zt[:, tb, :], mv[:, tb, 0:1], lstd[:, 1, tb:tb + 1],
                                                 ALU.subtract, ALU.mult)
                    link(last)
                    link(dve.tensor_tensor(zt[:], zt[:], lnr[:, 0, :].unsqueeze(1).broadcast_to([P, TB, S_W]), ALU.mult))
                if r == 63:
                    dve.tensor_tensor(zt[:], zt[:], lnr[:, 1, :].unsqueeze(1).broadcast_to([P, TB, S_W]), ALU.add)\
                        .then_inc(s_vn, 1)
                if r in (65, 66):
                    tb = r - 65
                    dve.wait_ge(*unit_read(("go", l, tb)))
                    link(dve.tensor_tensor(rt[:], y[:, tb, 3 * CW:], y[:, tb, 3 * CW:], ALU.mult))
                    last = dve.tensor_reduce(gsq[:, 0, tb, :], rt[:].rearrange("p (h e) -> p h e", e=G_DV), AX.X, ALU.add)
                    if tb == 0:
                        link(last)
                    else:
                        last.then_inc(s_gsq, 1)
                        dve.wait_ge(s_gsq, l + 1)
                if r == 68:
                    dve.wait_ge(s_grms, l + 1)
                    link(dve.reciprocal(gsq[:, 0], gsq[:, 1]))
                    gy = y[:, :, 3 * CW:].rearrange("p b (h e) -> p b h e", e=G_DV)
                    link(dve.tensor_tensor(gy, gy, gsq[:, 0].unsqueeze(3).broadcast_to([P, TB, G_HEADS, G_DV]), ALU.mult))
                    for tb in range(TB):
                        last = dve.tensor_tensor(gy[:, tb], gy[:, tb],
                                                 gnorm[:].unsqueeze(1).broadcast_to([P, G_HEADS, G_DV]), ALU.mult)
                    link(last)
                if r in (68, 69):
                    tb = r - 68
                    name = ("sg", l, tb)
                    dve.wait_ge(*unit_full(name))
                    dve.tensor_tensor(rt[:].rearrange("p (g e) -> p g e", e=S_GD),
                                      bank_s(name)[:].rearrange("p (g e) -> p g e", e=S_GD),
                                      sgb[:].unsqueeze(2).broadcast_to([P, S_G, S_GD]), ALU.add)\
                        .then_inc(s_sfree[UNIT1[name] % 2], 1)
                    dve.wait_ge(*unit_read(name))
                    link(dve.tensor_tensor(y[:, tb, 2 * CW:3 * CW], y[:, tb, 2 * CW:3 * CW], rt[:], ALU.mult))
                if r in (70, 76, 84, 92):
                    i = (70, 76, 84, 92).index(r)
                    j = Z_ORDER[i]
                    dve.wait_ge(*acc_read(chunk(l, f"z{j}")))
                    dve.tensor_tensor(y[:, :, j * CW:(j + 1) * CW], y[:, :, j * CW:(j + 1) * CW], zt[:], ALU.mult)\
                        .then_inc(s_ym, 1)
                if r >= R_OUT + GPC and (r - R_OUT) % GPC == 3:
                    gained(l, (r - R_OUT) // GPC - 1)
                step = mod_step(l, r)
                if step:
                    mod(*step)
            for r in range(AHEAD if l + 1 < DEPTH else 0):
                lo(GRAN1 * (l + 1) + r)
            gained(l, NCW - 1)
            inverse_root(2 * l + 1)
            dve.wait_ge(*acc_read(chunk(l, NCW - 1)))
            for j in range(NCW):
                cols = slice(j * CW, (j + 1) * CW)
                for tb in range(TB):
                    last = dve.scalar_tensor_tensor(out=x[:, tb, cols], in0=y[:, tb, cols], scalar=rms[:, 1, tb:tb + 1],
                                                    in1=x[:, tb, cols], op0=ALU.mult, op1=ALU.add)
                last.then_inc(s_xd, 1)

    @block.tensor
    def _(pe):
        pe.wait_ge(s_ident, 16)
        pe.wait_ge(s_mem, 2)

        def fill(name):
            i, bank, kind, l = FILL1[name], bank_t(name), name[0], name[1]
            need(pe, (s_tfree[i % 2], i // 2))
            if kind == "h":
                pe.wait_ge(s_xn, NCW * l + name[2] // 2 + 1)
                src, cols = y, [P * (2 * name[2] + k) for k in range(2)]
            elif kind == "y":
                pe.wait_ge(s_ym, NCW * l + name[2] // 2 + 1)
                src, cols = y, [P * (y_tile(name[2]) + k) for k in range(2)]
            elif kind in ("gq", "gk"):
                pe.wait_ge(*acc_read(chunk(l, "gqk")))
                src, cols = stage, [(kind == "gk") * G_KW + k * P for k in range(2)]
            elif kind == "ak":
                pe.wait_ge(s_rope, 3 * l + 1)
                src, cols = ks, [k * P for k in range(2)]
            elif kind == "aq":
                pe.wait_ge(s_rope, 3 * l + 2 + name[2])
                src, cols = stage, [P * (2 * name[3] + k) for k in range(2)]
            if kind == "p":
                pe.wait_ge(s_exp, exp_index(l, name[2], name[3]))
                for k in range(4):
                    t = pe.transpose(bank[:, k * P:(k + 1) * P], scr[:, name[3], k * P:(k + 1) * P], ident[:])
            else:
                for k in range(2):
                    for tb in range(TB):
                        t = pe.transpose(bank[:, k * SEQ + tb * P:k * SEQ + (tb + 1) * P],
                                         src[:, tb, cols[k]:cols[k] + P], ident[:])
            t.then_inc(s_tfull, 1)

        def unit(name):
            i, bank, kind, l = UNIT1[name], bank_s(name), name[0], name[1]
            need(pe, (s_sfree[i % 2], i // 2))
            if kind in ("ms", "ma", "mg"):
                q = THIRDS.index((l, ("ms", "ma", "mg").index(kind)))
                half = name[2] // 2 if kind == "mg" else name[2]
                pe.wait_ge(s_macc, MOD_N * q + KT * (half + 1))
                if kind == "mg":
                    m = pe.matmul(bank[:], ones[:], macc[:, name[2] * CW:(name[2] + 1) * CW], start=True, stop=True)
                else:
                    for k in range(half * KT // 2, (half + 1) * KT // 2):
                        m = pe.matmul(bank[:, k:k + 1], macc_of(q)[:, k * P:(k + 1) * P], ones[:, 0:1],
                                      start=True, stop=True)
            elif kind == "cg":
                pe.wait_ge(s_wg, 2 * l + 2)
                for k in range(KT):
                    for q, (w, a) in enumerate(((wghi, hhi), (wglo, hhi), (wghi, hlo))):
                        m = pe.matmul(bank[0:RANK, 0:SEQ], w[:, k, :], a[:, k, :],
                                      start=(k == 0 and q == 0), stop=(k == KT - 1 and q == 2))
            elif kind == "gl":
                pe.wait_ge(*unit_read(("cg", l)))
                for tb in range(TB):
                    m = pe.matmul(bank[:, tb * G_KW:(tb + 1) * G_KW], cgT[:, tb * P:(tb + 1) * P], gup[:],
                                  start=True, stop=True)
            elif kind == "dz":
                if name[2] == 0:
                    pe.wait_ge(s_la, l + 1)
                    pe.wait_ge(s_late, 32)
                for pair in range(2):
                    for tb in range(TB):
                        col = pair * SEQ + tb * P
                        t = name[2] + 1 if name[2] else tb
                        m = pe.matmul(bank[:, col:col + P], la[:, tb, pair * P:(pair + 1) * P], sums[:, t, :],
                                      start=True, stop=True)
            elif kind == "sc":
                _, _, i, odd = name
                rows = slice(odd * G_DK, (odd + 1) * G_DK)
                if i < 0:
                    pe.wait_ge(*copied(("gq", l)))
                    pe.wait_ge(*copied(("gk", l)))
                    key, query = gkT, gqT
                else:
                    pe.wait_ge(s_gx, len(LEVELS) * l + i + 1)
                    key = query = zt[:, i % 2, :]
                for pair in range(2):
                    if i == 0:
                        m = pe.matmul(bank[:, pair * P:(pair + 1) * P], key[rows, pair * SEQ:pair * SEQ + P],
                                      query[rows, pair * SEQ + P:(pair + 1) * SEQ], start=True, stop=True)
                    else:
                        for tb in range(TB):
                            tok = slice(pair * SEQ + tb * P, pair * SEQ + (tb + 1) * P)
                            k = TB * pair + tb
                            m = pe.matmul(bank[:, k * P:(k + 1) * P], key[rows, tok], query[rows, tok],
                                          start=True, stop=True)
            elif kind == "go":
                tb = name[2]
                if tb == 0:
                    pe.wait_ge(*unit_read(("sc", l, len(LEVELS) - 1, 0)))
                    pe.wait_ge(*unit_read(("sc", l, len(LEVELS) - 1, 1)))
                for h in range(G_HEADS):
                    out = bank[:, h * G_DV:(h + 1) * G_DV]
                    if tb:
                        pe.matmul(out, stx[:, h, :], gv[:, 0, h * G_DV:(h + 1) * G_DV], start=True, stop=False)
                    m = pe.matmul(out, st[:, h % 2, TB * (h // 2) + tb, :], gv[:, tb, h * G_DV:(h + 1) * G_DV],
                                  start=(tb == 0), stop=True)
            elif kind == "s":
                _, _, grp, u = name
                if u == 0:
                    if grp == 0:
                        pe.wait_ge(*copied(("ak", l)))
                    for k in range(2):
                        pe.wait_ge(*copied(("aq", l, grp // 2, k)))
                rows = slice((grp % 2) * A_HD, (grp % 2 + 1) * A_HD)
                w, tb = (P, 0) if u == 0 else (SEQ, 1)
                for b in range(CW // w):
                    h = 4 * (grp // 2) + b + max(0, 2 * (u - 1))
                    m = pe.matmul(bank[:, b * w:(b + 1) * w], qT[rows, h, tb * P:(tb + 1) * P],
                                  kT[rows, grp // 2, 0:w], start=True, stop=True)
            elif kind == "o":
                grp = name[2]
                for u in (1, 2):
                    pe.wait_ge(*copied(("p", l, grp, u)))
                for tb in range(TB):
                    for h in range(A_PER):
                        for s in range(tb + 1):
                            u, col = (0, h) if tb == 0 else (1 + h // 2, 2 * (h % 2) + s)
                            at_h = tb * A_KVW + h * A_HD
                            m = pe.matmul(bank[:, at_h:at_h + A_HD], scr[:, 3 + u, col * P:(col + 1) * P],
                                          av[:, s, grp * A_HD:(grp + 1) * A_HD], start=(s == 0), stop=(s == tb))
            else:
                tb = name[2]
                pe.wait_ge(s_vn, l + 1)
                pe.wait_ge(s_sgw, l + 1)
                for g in range(S_G):
                    m = pe.matmul(bank[:, g * S_GD:(g + 1) * S_GD], sgw[:, g, :], zt[:, tb, g * S_GD:(g + 1) * S_GD],
                                  start=True, stop=True)
            m.then_inc(s_sfull, 1)

        for l, r in STEPS1:
            for name in fills1(l, r):
                fill(name)
            for name in units1(l, r):
                unit(name)
            if r < 0:
                continue
            c, g = place(l, r)
            gc = NCH1 * l + c
            if c == 0:
                pe.wait_ge(s_h, GPC * l + g + 1)
            if r >= R_OUT and c == len(CHUNKS1):
                pe.wait_ge(*copied(("y", l, g)))
            if g == 0:
                need(pe, (s_acc[gc % 2], gc // 2))
            n = GRAN1 * l + r
            pe.wait_ge(*split(n))
            steps = [(k, tb) for k in range(GK) for tb in range(TB)]
            if r == GRAN1 - 1:
                steps = [(k, tb) for tb in range(TB) for k in range(GK)]
            for k, tb in steps:
                kt = (y_tile(g) if c >= len(CHUNKS1) else GK * g) + k
                tile = slice(tb * P, (tb + 1) * P)
                for q, (a, b) in enumerate(((hhi, whi), (hhi, wlo), (hlo, whi))):
                    m = pe.matmul(acc[gc % 2][:, tb, :], a[:, kt, tile], b[:, n % SLOTS, k * CW:(k + 1) * CW],
                                  start=(g == 0 and k == 0 and q == 0),
                                  stop=(g == GPC - 1 and k == GK - 1 and q == 2))
                if r == GRAN1 - 1 and (k, tb) == (GK - 1, 0):
                    m.then_inc(s_half, 1)
            m.then_inc(s_used, 1)


def y_tile(i):
    return (CW // P) * Z_ORDER[i // 2] + GK * (i % 2)


def first_constants():
    half = ROT // 2
    inv = np.float32(500000.0) ** (-(np.arange(half, dtype=np.float32) * np.float32(2.0 / ROT)))
    s, t = np.arange(P)[:, None], np.arange(P)[None, :]
    sums = [s > t, s <= t]
    masks = [s == t]
    for m in LEVELS[1:]:
        upper = (t // m) % 2 == 1
        mid = t // m * m
        after = (t // (2 * m)) * 2 * m + m
        sums.append(np.where(upper, (s >= mid) & (s <= t), (s > t) & (s < after)))
        masks.append((s // (2 * m) == t // (2 * m)) & upper & ((s // m) % 2 == 0))
    return {
        "inv_freq": inv.astype(np.float32),
        "sums": np.stack(sums, axis=1).astype(np.float32),
        "lmask": np.stack(masks, axis=1).astype(np.float32),
        "mask_w": band(lambda d: np.where((d >= 0) & (d < WINDOW), 0.0, NEG)),
    }


def first_stream(w_in, w_out):
    out = []
    for l in range(DEPTH):
        chunks = [columns(w_in[l], start) for _, start in CHUNKS1]
        for c, g in (place(l, r) for r in range(R_OUT)):
            out.append(chunks[c][g:g + 1])
        for j in range(NCW):
            tiles = columns(w_out[l], CW * j)
            out.append(tiles[[y_tile(i) // GK for i in range(GPC)]])
    return np.concatenate(out)


def by_partition(a):
    return np.ascontiguousarray(np.swapaxes(a.reshape(*a.shape[:-1], KT, P), -1, -2))


def first_arrays(x, c, positions, w_mod, b_mod, g_pre, g_post, w_in, w_out, swa_sinks, sg_w, sg_b, sg_ln_g,
                 sg_ln_b, gla_w_gate_up, gla_b_gate, gla_norm_g):
    halves = D // MOD_W
    return {
        "x": np.ascontiguousarray(x[0]),
        "c": by_partition(c[0]),
        "positions": np.ascontiguousarray(positions.reshape(TB, P).T),
        "w_mod": np.ascontiguousarray(w_mod.reshape(DEPTH, KT, P, 3, halves, MOD_W).transpose(0, 3, 4, 1, 2, 5))
        .reshape(DEPTH, 3, MOD_N, P, MOD_W),
        "b_mod": b_mod.reshape(DEPTH, 3, D),
        "g_pre": by_partition(g_pre),
        "g_post": g_post,
        "w1": first_stream(w_in, w_out),
        "wg": np.ascontiguousarray(w_in[:, :, OFF_GATE:OFF_GATE + RANK].reshape(DEPTH, KT, P, RANK)
                                   .transpose(0, 2, 1, 3)),
        "gate_up": gla_w_gate_up,
        "b_gate": gla_b_gate,
        "gnorm": gla_norm_g,
        "sinks": swa_sinks,
        "sg_w": np.ascontiguousarray(sg_w.transpose(0, 3, 1, 2)),
        "sg_b": np.ascontiguousarray(sg_b.transpose(0, 2, 1)),
        "sg_ln_g": sg_ln_g,
        "sg_ln_b": sg_ln_b,
        **first_constants(),
    }


def second_arrays(w_in, b_forget, b_gate, w_up_a, w_up_b, w_out, ln_g, ln_b):
    f = 8 * W2
    return {
        "w": second_stream(w_in, w_up_a, w_up_b, w_out),
        "wf": np.ascontiguousarray(w_in[:, :, f:f + NH2].reshape(DEPTH, KT, P, NH2).transpose(0, 2, 1, 3)),
        "bf": b_forget.reshape(DEPTH, NH2, 1), "bg": b_gate.reshape(DEPTH * 2 * NCW, CW), "ln_g": ln_g, "ln_b": ln_b,
        **constants(),
    }


def program(nc, dram):
    with ExitStack() as ctx:
        def sb(name, shape, dt=F32):
            return ctx.enter_context(nc.sbuf_tensor(name, shape, dt))

        x = sb("x", [P, TB, D])
        ident = sb("ident", [P, P])
        rings = (sb("raw", [P, SLOTS, GK * CW]), sb("whi", [P, SLOTS, GK * CW], F32R),
                 sb("wlo", [P, SLOTS, GK * CW], F32R))
        acc = [ctx.enter_context(nc.psum_tensor(f"acc{i}", [P, TB, CW], F32)) for i in range(2)]
        psT = [ctx.enter_context(nc.psum_tensor(f"psT{i}", [P, CW], F32)) for i in range(2)]
        psS = [ctx.enter_context(nc.psum_tensor(f"psS{i}", [P, CW], F32)) for i in range(2)]
        s_w = [ctx.enter_context(nc.semaphore(f"c_w{i}")) for i in range(SLOTS)]
        with ExitStack() as first:
            first_block(nc, first, x, rings, (acc, psT, psS), dram, ident, s_w)
        with ExitStack() as second:
            second_block(nc, second, x, rings, (acc, psT, psS), dram, s_w, ident)


def kernel(x, c, positions, w_mod, b_mod, g_pre, g_post, w_in, w_out, swa_sinks, sg_w, sg_b, sg_ln_g, sg_ln_b,
           gla_w_gate_up, gla_b_gate, gla_norm_g, w_in_2, b_forget_2, b_gate_2, w_up_a_2, w_up_b_2, w_out_2,
           ln_g_2, ln_b_2):
    import concourse.bacc as bacc
    from concourse.bass_utils import run_bass_kernel_spmd

    nc = bacc.Bacc("TRN2", target_bir_lowering=False, num_devices=1)
    arrays = {
        **first_arrays(x, c, positions, w_mod, b_mod, g_pre, g_post, w_in, w_out, swa_sinks, sg_w, sg_b, sg_ln_g,
                       sg_ln_b, gla_w_gate_up, gla_b_gate, gla_norm_g),
        **second_arrays(w_in_2, b_forget_2, b_gate_2, w_up_a_2, w_up_b_2, w_out_2, ln_g_2, ln_b_2),
    }
    dram = {name: nc.dram_tensor(f"in_{name}", a.shape, mybir.dt.from_np(a.dtype), kind="ExternalInput").ap()
            for name, a in arrays.items()}
    dram["out"] = nc.dram_tensor("out_x", (SEQ, D), F32, kind="ExternalOutput").ap()
    program(nc, dram)
    r = run_bass_kernel_spmd(nc, [{f"in_{name}": a for name, a in arrays.items()}], core_ids=[0])
    return r.results[0]["out_x"].reshape(1, SEQ, D)
```
